# Optimizing a Trainium2 kernel written in Bass

```python
import jax, jax.numpy as jnp
from jax import lax
import numpy as np

D_MODEL = 2048
BATCH = 1
SEQ = 256
DEPTH = 2

N_A_LAYERS = DEPTH // 2
N_B_LAYERS = DEPTH - N_A_LAYERS
EPS = 1e-6
MOD_INIT = 0.1
N_MOD = 6

CHUNK = 128
SGU_WIDTH = 2 * D_MODEL
SGU_GROUPS = 16
SGU_GROUP_DIM = SGU_WIDTH // SGU_GROUPS

D_FF = 11 * D_MODEL // 4
CONV_W = 3

N_HEADS = 16
HEAD_DIM = D_MODEL // N_HEADS
N_KV = 4
GROUP = N_HEADS // N_KV
N_BRANCH = 3
N_KV_TENSORS = 2 * N_BRANCH
CMP_LEN = 32
CMP_STRIDE = 16
SLC_LEN = 64
SLC_TOPK = 16
N_FORCED_LOCAL = 2
WINDOW = 512
Q_BLOCK = 128
NEG_INF = -1e30
FORCE_BONUS = 1e4

kernel_name = 'yoco_sgu_nsa_hybrid'

def alibi_slopes():
    h = jnp.arange(1, N_HEADS + 1, dtype=jnp.float32)
    return (2.0 ** (-8.0 * h / N_HEADS)).reshape(N_KV, GROUP)

def rms_norm(x, gain):
    xf = x.astype(jnp.float32)
    y = xf * lax.rsqrt(jnp.mean(xf * xf, axis=-1, keepdims=True) + EPS)
    return (y * gain.astype(jnp.float32)).astype(x.dtype)

def adaln(c, w, b, n):
    m = jax.nn.silu(c) @ w + b
    return jnp.split(m[:, None, :], n, axis=-1)

def modulate(x, gain, shift, scale):
    return rms_norm(x, gain) * (1 + scale) + shift

def masked_softmax(s, valid):
    s = jnp.where(valid, s, NEG_INF)
    m = jnp.max(s, axis=-1, keepdims=True)
    e = jnp.where(valid, jnp.exp(s - m), 0.0)
    return e / jnp.maximum(jnp.sum(e, axis=-1, keepdims=True), 1e-30)

def conv_ffn(h, w_up, conv_w, conv_b, w_down):
    T = h.shape[1]
    z = h @ w_up
    zp = jnp.pad(z, ((0, 0), (CONV_W - 1, 0), (0, 0)))
    z = conv_b + sum(conv_w[k] * zp[:, k:k + T] for k in range(CONV_W))
    a, v = jnp.split(z, 2, axis=-1)
    return (jax.nn.silu(a) * v) @ w_down

def chunked_sgu(h, w_in, v_gain, w_s, b_s, w_out):
    B, T, _ = h.shape
    u, v = jnp.split(jax.nn.gelu(h @ w_in), 2, axis=-1)
    v = rms_norm(v, v_gain).reshape(B, T // CHUNK, CHUNK, SGU_GROUPS, SGU_GROUP_DIM)
    w_causal = jnp.where(jnp.tril(jnp.ones((CHUNK, CHUNK), dtype=bool)), w_s, 0.0)
    sv = jnp.einsum('gts,bnsgc->bntgc', w_causal, v) + b_s.T[:, :, None]
    return (u * sv.reshape(B, T, SGU_WIDTH)) @ w_out

def nsa_shared_kv(x, c, gain, mod_w, mod_b, w_kv, cmp_pos, cmp_w1, cmp_w2, k_gain):
    B, T, _ = x.shape
    shift, scale = adaln(c, mod_w, mod_b, 2)
    h = modulate(x, gain, shift, scale)
    kv = (h @ w_kv).reshape(B, T, N_KV_TENSORS, N_KV, HEAD_DIM)
    n_cmp = T // CMP_STRIDE - 1

    def compress(t, i):
        s = t.reshape(B, T // CMP_STRIDE, CMP_STRIDE, N_KV, HEAD_DIM)
        blocks = jnp.concatenate([s[:, :-1], s[:, 1:]], axis=2) + cmp_pos[i][:, None, :]
        flat = blocks.transpose(0, 1, 3, 2, 4).reshape(B, n_cmp, N_KV, CMP_LEN * HEAD_DIM)
        return jax.nn.gelu(flat @ cmp_w1[i]) @ cmp_w2[i]

    k_cmp = rms_norm(compress(kv[:, :, 0], 0), k_gain[0])
    v_cmp = compress(kv[:, :, 1], 1)
    k_slc = rms_norm(kv[:, :, 2], k_gain[1])
    v_slc = kv[:, :, 3]
    k_win = rms_norm(kv[:, :, 4], k_gain[2])
    v_win = kv[:, :, 5]
    return (k_cmp, v_cmp, k_slc, v_slc, k_win, v_win)

def nsa_attention(h, kv, w_in, q_gain, w_o):
    k_cmp, v_cmp, k_slc, v_slc, k_win, v_win = kv
    B, T, _ = h.shape
    f32 = jnp.float32
    proj = h @ w_in
    q = rms_norm(proj[..., :N_HEADS * HEAD_DIM].reshape(B, T, N_KV, GROUP, HEAD_DIM), q_gain)
    gates = jax.nn.sigmoid(proj[..., N_HEADS * HEAD_DIM:].astype(f32)).reshape(B, T, N_BRANCH, N_KV, GROUP)
    sl = alibi_slopes()[None, :, :, None, None]
    scale = HEAD_DIM ** -0.5
    n_cmp = k_cmp.shape[1]
    n_slc = T // SLC_LEN
    top_k = min(SLC_TOPK, n_slc)
    cmp_start = jnp.arange(n_cmp) * CMP_STRIDE
    cmp_end = cmp_start + CMP_LEN - 1
    blk = jnp.arange(n_slc)
    slc_start = blk * SLC_LEN
    overlap = ((cmp_start[:, None] < slc_start[None, :] + SLC_LEN)
               & (cmp_start[:, None] + CMP_LEN > slc_start[None, :])).astype(f32)
    k_blocks = k_slc.reshape(B, n_slc, SLC_LEN, N_KV, HEAD_DIM).transpose(0, 3, 1, 2, 4)
    v_blocks = v_slc.reshape(B, n_slc, SLC_LEN, N_KV, HEAD_DIM).transpose(0, 3, 1, 2, 4)
    k_win_p = jnp.pad(k_win, ((0, 0), (WINDOW, 0), (0, 0), (0, 0)))
    v_win_p = jnp.pad(v_win, ((0, 0), (WINDOW, 0), (0, 0), (0, 0)))
    b_ix = jnp.arange(B)[:, None, None, None]
    g_ix = jnp.arange(N_KV)[None, :, None, None]
    tok = jnp.arange(SLC_LEN)
    n_sel = top_k * SLC_LEN

    def query_block(qb):
        t0 = qb * Q_BLOCK
        qi = lax.dynamic_slice_in_dim(q, t0, Q_BLOCK, axis=1)
        gi = lax.dynamic_slice_in_dim(gates, t0, Q_BLOCK, axis=1)
        t = t0 + jnp.arange(Q_BLOCK)
        d_cmp = t[:, None] - cmp_end[None, :]
        s = jnp.einsum('bqgrd,bngd->bgrqn', qi, k_cmp, preferred_element_type=f32) * scale - sl * d_cmp
        p_cmp = masked_softmax(s, d_cmp >= 0)
        o_cmp = jnp.einsum('bgrqn,bngd->bqgrd', p_cmp, v_cmp.astype(f32))
        imp = jnp.einsum('bgrqn,ns->bgqs', p_cmp, overlap)
        cur = (t // SLC_LEN)[:, None]
        forced = (blk[None, :] == 0) | ((blk[None, :] <= cur) & (blk[None, :] > cur - N_FORCED_LOCAL))
        imp = jnp.where(forced, imp + FORCE_BONUS, imp)
        imp = jnp.where(blk[None, :] <= cur, imp, NEG_INF)
        _, idx = lax.top_k(imp, top_k)
        ks = k_blocks[b_ix, g_ix, idx].reshape(B, N_KV, Q_BLOCK, n_sel, HEAD_DIM)
        vs = v_blocks[b_ix, g_ix, idx].reshape(B, N_KV, Q_BLOCK, n_sel, HEAD_DIM)
        d_slc = (t[None, None, :, None, None] - (idx[..., None] * SLC_LEN + tok)).reshape(B, N_KV, 1, Q_BLOCK, n_sel)
        s = jnp.einsum('bqgrd,bgqkd->bgrqk', qi, ks, preferred_element_type=f32) * scale - sl * d_slc
        p = masked_softmax(s, d_slc >= 0)
        o_slc = jnp.einsum('bgrqk,bgqkd->bqgrd', p, vs.astype(f32))
        kw = lax.dynamic_slice_in_dim(k_win_p, t0, Q_BLOCK + WINDOW, axis=1)
        vw = lax.dynamic_slice_in_dim(v_win_p, t0, Q_BLOCK + WINDOW, axis=1)
        sp = t0 - WINDOW + jnp.arange(Q_BLOCK + WINDOW)
        d_win = t[:, None] - sp[None, :]
        valid = (d_win >= 0) & (d_win < WINDOW) & (sp[None, :] >= 0)
        s = jnp.einsum('bqgrd,bkgd->bgrqk', qi, kw, preferred_element_type=f32) * scale - sl * d_win
        p = masked_softmax(s, valid)
        o_win = jnp.einsum('bgrqk,bkgd->bqgrd', p, vw.astype(f32))
        g = gi[..., None]
        return g[:, :, 0] * o_cmp + g[:, :, 1] * o_slc + g[:, :, 2] * o_win

    out = lax.map(query_block, jnp.arange(T // Q_BLOCK))
    out = out.transpose(1, 0, 2, 3, 4, 5).reshape(B, T, N_HEADS * HEAD_DIM).astype(h.dtype)
    return out @ w_o

def setup_inputs(seed: int = 0) -> dict:
    key = jax.random.key(seed)
    ks = jax.random.split(key, 32)
    f32 = jnp.float32

    def dense(k, shape, fan_in, mult=1.0):
        return jax.random.normal(k, shape, f32) * (mult * fan_in ** -0.5)

    def near_one(k, shape):
        return 1.0 + 0.02 * jax.random.normal(k, shape, f32)

    def small(k, shape):
        return 0.02 * jax.random.normal(k, shape, f32)

    gate_offset = jnp.zeros((N_MOD, D_MODEL), f32).at[jnp.array([2, 5])].set(1.0).reshape(N_MOD * D_MODEL)
    return {
        'x': jax.random.normal(ks[0], (BATCH, SEQ, D_MODEL), f32),
        'c': jax.random.normal(ks[1], (BATCH, D_MODEL), f32),
        'mod_w': dense(ks[2], (DEPTH, D_MODEL, N_MOD * D_MODEL), D_MODEL, MOD_INIT),
        'mod_b': small(ks[3], (DEPTH, N_MOD * D_MODEL)) + gate_offset,
        'norm_gain': near_one(ks[4], (DEPTH, 2, D_MODEL)),
        'ffn_w_up': dense(ks[5], (DEPTH, D_MODEL, 2 * D_FF), D_MODEL),
        'ffn_conv_w': dense(ks[6], (DEPTH, CONV_W, 2 * D_FF), CONV_W),
        'ffn_conv_b': small(ks[7], (DEPTH, 2 * D_FF)),
        'ffn_w_down': dense(ks[8], (DEPTH, D_FF, D_MODEL), D_FF),
        'sgu_w_in': dense(ks[9], (N_A_LAYERS, D_MODEL, 2 * SGU_WIDTH), D_MODEL),
        'sgu_v_gain': near_one(ks[10], (N_A_LAYERS, SGU_WIDTH)),
        'sgu_w_s': dense(ks[11], (N_A_LAYERS, SGU_GROUPS, CHUNK, CHUNK), CHUNK),
        'sgu_b_s': near_one(ks[12], (N_A_LAYERS, SGU_GROUPS, CHUNK)),
        'sgu_w_out': dense(ks[13], (N_A_LAYERS, SGU_WIDTH, D_MODEL), SGU_WIDTH),
        'kv_gain': near_one(ks[14], (D_MODEL,)),
        'kv_mod_w': dense(ks[15], (D_MODEL, 2 * D_MODEL), D_MODEL, MOD_INIT),
        'kv_mod_b': small(ks[16], (2 * D_MODEL,)),
        'w_kv': dense(ks[17], (D_MODEL, N_KV_TENSORS * N_KV * HEAD_DIM), D_MODEL),
        'cmp_pos': 0.5 * jax.random.normal(ks[18], (2, CMP_LEN, HEAD_DIM), f32),
        'cmp_w1': dense(ks[19], (2, CMP_LEN * HEAD_DIM, HEAD_DIM), CMP_LEN * HEAD_DIM),
        'cmp_w2': dense(ks[20], (2, HEAD_DIM, HEAD_DIM), HEAD_DIM),
        'k_gain': near_one(ks[21], (N_BRANCH, HEAD_DIM)),
        'nsa_w_in': dense(ks[22], (N_B_LAYERS, D_MODEL, N_HEADS * HEAD_DIM + N_BRANCH * N_HEADS), D_MODEL),
        'nsa_q_gain': near_one(ks[23], (N_B_LAYERS, HEAD_DIM)),
        'nsa_w_o': dense(ks[24], (N_B_LAYERS, N_HEADS * HEAD_DIM, D_MODEL), N_HEADS * HEAD_DIM),
    }

def reference(x, c, mod_w, mod_b, norm_gain, ffn_w_up, ffn_conv_w, ffn_conv_b, ffn_w_down,
              sgu_w_in, sgu_v_gain, sgu_w_s, sgu_b_s, sgu_w_out,
              kv_gain, kv_mod_w, kv_mod_b, w_kv, cmp_pos, cmp_w1, cmp_w2, k_gain,
              nsa_w_in, nsa_q_gain, nsa_w_o):
    shared_kv = None
    for layer in range(DEPTH):
        if layer == N_A_LAYERS:
            shared_kv = nsa_shared_kv(x, c, kv_gain, kv_mod_w, kv_mod_b, w_kv, cmp_pos, cmp_w1, cmp_w2, k_gain)
        sh1, sc1, g1, sh2, sc2, g2 = adaln(c, mod_w[layer], mod_b[layer], N_MOD)
        h = modulate(x, norm_gain[layer, 0], sh1, sc1)
        if layer < N_A_LAYERS:
            a = layer
            y = chunked_sgu(h, sgu_w_in[a], sgu_v_gain[a], sgu_w_s[a], sgu_b_s[a], sgu_w_out[a])
        else:
            bl = layer - N_A_LAYERS
            y = nsa_attention(h, shared_kv, nsa_w_in[bl], nsa_q_gain[bl], nsa_w_o[bl])
        x = x + g1 * y
        h = modulate(x, norm_gain[layer, 1], sh2, sc2)
        x = x + g2 * conv_ffn(h, ffn_w_up[layer], ffn_conv_w[layer], ffn_conv_b[layer], ffn_w_down[layer])
    return x


_drawn_inputs = setup_inputs


def setup_inputs(seed=0):
    import zlib

    import numpy as np

    out = dict(_drawn_inputs(seed))
    spreads = {}
    factors = {'ffn_conv_b': 3.353,
     'sgu_v_gain': 6.708,
     'sgu_b_s': 4.754,
     'kv_gain': 8.0,
     'kv_mod_b': 4.207,
     'k_gain': 8.0,
     'nsa_q_gain': 8.0}
    for name, (base, spread) in spreads.items():
        noise = np.random.default_rng([zlib.crc32(name.encode()), seed]).standard_normal(out[name].shape)
        drawn = base * np.exp(spread * noise) if base else spread * noise
        out[name] = __import__('jax').numpy.asarray(drawn.astype(out[name].dtype))
    for name, factor in factors.items():
        out[name] = (out[name] * factor).astype(out[name].dtype)
    return out
```

```python
from contextlib import ExitStack

import numpy as np

import concourse.bass as bass
from concourse import mybir

P = 128
D = 2048
T = 256
KT = D // P
EPS = 1e-6
SGU_W = 2 * D
SGU_G = 16
D_FF = 11 * D // 4
FT = D_FF // P
NH, NKV, HD = 16, 4, 128
GRP = NH // NKV
CMP_LEN, CMP_STRIDE = 32, 16
NCMP = T // CMP_STRIDE - 1
NB = NKV * NCMP
NGATE = 3 * NH
BIG = 1e30

COLS = 512
TPC = COLS // P
KPP = 4
PIECE = KPP * COLS
SUB = PIECE // 2
RAW_SLOTS = 4
SPLIT_SLOTS = 4
HILO = 2 * T

F32, F32R = mybir.dt.float32, mybir.dt.float32r
ALU, ACT, AX = mybir.AluOpType, mybir.ActivationFunctionType, mybir.AxisListType

MODS = [("mod0", 0), ("mod0", 1), ("mod0", 2), ("mod0", 3), ("mod0", 4), ("mod0", 5), ("kv", 0), ("kv", 1),
        ("mod1", 0), ("mod1", 1), ("mod1", 2), ("mod1", 3), ("mod1", 4), ("mod1", 5)]
SH1_0, SC1_0, G1_0, SH2_0, SC2_0, G2_0, SH_KV, SC_KV, SH1_1, SC1_1, G1_1, SH2_1, SC2_1, G2_1 = range(14)
GAIN_OF = {SC1_0: 0, SC2_0: 1, SC_KV: 4, SC1_1: 2, SC2_1: 3}

C_C = 0
C_MODB = C_C + KT
C_GAIN = C_MODB + len(MODS) * KT
C_VGAIN = C_GAIN + 5 * KT
C_CONVW = C_VGAIN + SGU_W // P
C_CONVB = C_CONVW + 2 * 3 * 2 * FT
C_KG = C_CONVB + 2 * 2 * FT
C_QG = C_KG + 3
C_POS = C_QG + 1
C_W2 = C_POS + 2 * CMP_LEN
N_SMALL = C_W2 + 2 * HD

DW = 16 + T
N_POS = 2 * DW + 2

PAT = {
    "P0": "ssssEsEsEsEs",
    "P2": "ssssEsEsmEsEsm",
    "P4": "ssssEmsEsmmEsEsm",
    "Q0": "ssssEEsEsE",
    "Q1": "ssssEEsEsEm",
    "M16": "m" * 16,
    "G1": "sE",
}


def ready_after(k):
    return sum(2 if j in GAIN_OF else 1 for j in range(k + 1))


class Chunk:

    def __init__(self, kind, loc, pattern, source):
        self.kind, self.loc, self.pattern, self.source = kind, loc, pattern, source
        self.tokens = PAT[pattern]
        self.nsub = self.tokens.count("s")
        self.n = {}


def plan():
    phases = []

    def add(name, kinds, count, pattern, source):
        phases.append((name, [Chunk(kinds[i % len(kinds)], i // len(kinds), pattern, source)
                              for i in range(count)]))

    add("mod_a", ["mod"], 1, "M16", None)
    add("mod_b", ["mod"], 1, "M16", None)
    add("sgu_v", ["v"], 8, "P2", ("sgu_v", 0))
    for half in range(2):
        add(f"sgu_u{half}", ["u"], 4, "P2", ("sgu_u", half))
        add(f"sgu_o{half}", ["dn"], 4, "P2", ("sgu_out", half))
    for layer in range(2):
        if layer == 1:
            phases.append(("kv", [Chunk(k, j, p, ("kv", j)) for k, j, p in (
                ("kvf", 0, "P2"), ("kvf", 1, "P2"), ("kvf", 2, "P4"), ("kvt", 3, "P2"), ("kvf", 4, "P4"),
                ("kvt", 5, "P2"))]))
            phases.append(("cmp", [Chunk("cmp", 0, "P0", ("cmp", 0))]))
            add("q", ["q"], 4, "P4", ("q", 0))
            phases.append(("gate", [Chunk("gate", 0, "G1", ("gate", 0))]))
            add("wo", ["dn"], 4, "P4", ("wo", 0))
        for part, (ups, up_pat, dn_pat) in enumerate(
                ((4, "P2", "P4"), (4, "P2", "P4"), (3, "P2", "Q1")) if layer == 0 else
                ((4, "P2", "P0"), (4, "P0", "P0"), (3, "P0", "Q0"))):
            add(f"up{layer}{part}", ["ua", "uv"], 2 * ups, up_pat, ("up", layer, part))
            add(f"dn{layer}{part}", ["dn"], 4, dn_pat, ("down", layer, part))
    count = dict(c=0, G=0, S=0, M=0, zlo=0, zsum=0, tap2=0, tap1=0, conv=0, gated=0, prod=0, ahi=0, alo=0, xup=0,
                 vread=0)
    last_m = 0
    every = []
    for name, chunks in phases:
        for ch in chunks:
            ch.n = dict(count)
            ch.piece_of, ch.kinds_of = [], []
            halves = 0
            for tok in ch.tokens:
                if tok == "m" or (tok == "s" and halves % 2 == 0):
                    ch.kinds_of.append("m" if tok == "m" else "w")
                halves += tok == "s"
                if tok != "E":
                    ch.piece_of.append(len(ch.kinds_of) - 1)
                else:
                    ch.piece_of.append(None)
            ch.last_m = last_m
            if "m" in ch.kinds_of:
                last_m = count["G"] + max(i for i, k in enumerate(ch.kinds_of) if k == "m") + 1
            count["G"] += len(ch.kinds_of)
            count["M"] += ch.kinds_of.count("m")
            count["S"] += ch.nsub
            k = ch.kind
            if k != "mod":
                count["c"] += 1
            if k in ("ua", "uv", "u", "kvf", "q", "cmp"):
                count["zlo"] += 1
                count["zsum"] += 1
            if k in ("ua", "uv"):
                count["tap2"] += 1
                count["tap1"] += 1
                count["conv"] += 1
            if k in ("ua", "u"):
                count["gated"] += 1
            if k in ("uv", "u"):
                count["prod"] += 1
                count["ahi"] += 1
                count["alo"] += 1
            if k == "dn":
                count["xup"] += 1
            if k in ("v", "kvt", "gate"):
                count["vread"] += 1
            if k != "mod":
                every.append(ch)
    return phases, every, count


def free_rule(ch):
    if ch.kind in ("v", "kvt", "gate"):
        return "vread", ch.n["vread"] + 1
    if ch.kind == "dn":
        return "xlow", ch.n["xup"] + 1
    return "zsum", ch.n["zsum"] + 1


class At:

    def __init__(self, first, second=None, it=None, back=0):
        self.first, self.second, self.it, self.back = first, second, it, back

    def val(self, f):
        a = f(self.first)
        if self.second is None:
            return a
        step = f(self.second) - a
        return a - step * self.back + self.it * step if step else a

    def static(self, f):
        assert self.second is None or f(self.first) == f(self.second)
        return f(self.first)


def walk(eng, phases, step):
    prev = None
    for name, chunks in phases:
        body = 2 if len(chunks) > 1 else 1
        looped = len(chunks) >= 3 * body and name != "kv"
        straight = chunks[:body] if looped else chunks
        for i, ch in enumerate(straight):
            step(name, At(ch), At(prev) if prev else None, i == 0)
            prev = ch
        if looped:
            with eng.Fori(1, len(chunks) // body) as it:
                for b in range(body):
                    cur = At(chunks[b], chunks[b + body], it)
                    before = At(chunks[b - 1], chunks[b - 1 + body], it, 0) if b else \
                        At(chunks[body - 1], chunks[2 * body - 1], it, 1)
                    step(name, cur, before, False)
            prev = chunks[-1]


PHASES, EVERY, TOTAL = plan()
BY_NAME = dict(PHASES)
ORDER = {ch.n["c"]: ch for ch in EVERY}


def build(nc, io, stop=None):
    phases = PHASES
    if stop is not None:
        names = [n for n, _ in PHASES]
        phases = PHASES[:names.index(stop)]
    n_pieces = TOTAL["G"] if stop is None else BY_NAME[stop][0].n["G"]
    slopes = [2.0 ** (-8.0 * (h + 1) / NH) for h in range(NH)]
    ctx = ExitStack()
    with ctx:
        def sb(name, shape, dt=F32):
            return ctx.enter_context(nc.sbuf_tensor(name, shape, dt))

        with nc.sbuf_tensor("attn_area", [P, KT * HILO], F32) as attn_area:
            pass
        h_op = sb("h_op", [P, KT, HILO], F32R)
        with nc.sbuf_tensor("mix_area", [P, KT * HILO], F32) as mix_area:
            pass
        act_op = sb("act_op", [P, KT, HILO], F32R)
        x = sb("x_res", [P, KT, T])
        raw = sb("raw", [P, RAW_SLOTS, PIECE])
        w_hi = sb("w_hi", [P, SPLIT_SLOTS, SUB], F32R)
        w_lo = sb("w_lo", [P, SPLIT_SLOTS, SUB], F32R)
        scratch = sb("scratch", [P, 32 * T])
        mod_acc = sb("mod_acc", [P, D])
        modv = sb("modv", [P, len(MODS), KT])
        small = sb("small", [P, N_SMALL])
        zpad = sb("zpad", [P, TPC, T + 2])
        temp = sb("temp", [P, 2, TPC * T])
        rstd = sb("rstd", [P, T])
        kcmp = sb("kcmp", [P, NB])
        vcmp = sb("vcmp", [16, NKV * HD])
        gates = sb("gates", [P, 2, NGATE])
        cmp_g = sb("cmp_g", [P, 2 * NB])
        silu_c = sb("silu_c", [P, KT])
        ones = sb("ones", [P, P])
        ident = sb("ident", [P, P])
        vstat = sb("vstat", [P, 24])
        banks = ctx.enter_context(nc.psum_tensor("banks", [P, 8, 512], F32))

        y, gt = temp[:, 0, :], temp[:, 1, :]
        y4 = y.rearrange("p (j t) -> p j t", j=TPC)
        gt4 = gt.rearrange("p (j t) -> p j t", j=TPC)
        sv = scratch[:, :].rearrange("p (c t) -> p c t", t=T)
        w_sT = mix_area[:, 0:2048].rearrange("p (g t) -> p g t", g=SGU_G)
        w_sn = mix_area[:, 2048:6144].rearrange("p (n g t) -> p n g t", n=2, g=SGU_G)
        b_sb = mix_area[:, 6144:8192].rearrange("p (g t) -> p g t", g=SGU_G)
        kc0, vc0 = scratch[:, 0:1024], scratch[:, 1024:2048]
        q_raw = scratch[:, 0:4096]
        k_slc, k_win = scratch[:, 4096:5120], scratch[:, 5120:6144]
        v_slc, v_win = scratch[:, 6144:7168], scratch[:, 7168:8192]
        blocks = temp[:, :, :].rearrange("p a b -> p (a b)")[:, 0:CMP_LEN * NB]
        blk_op = act_op[:, :, :].rearrange("p k t -> p (k t)")

        sems = {}

        def sem(name):
            if name not in sems:
                sems[name] = ctx.enter_context(nc.semaphore(name))
            return sems[name]

        raw_loaded = [sem(f"raw_loaded{s}") for s in range(RAW_SLOTS)]
        hi_ready = sem("hi_ready")
        stream = sem("stream")
        sub_done = sem("sub_done")
        small_loaded, x_loaded, mix_loaded, pos_loaded = (
            sem("small_loaded"), sem("x_loaded"), sem("mix_loaded"), sem("pos_loaded"))
        zeroed, consts_set, c_ready = sem("zeroed"), sem("consts_set"), sem("c_ready")
        zlo, zsum, tap2, tap1, conv = sem("zlo"), sem("zsum"), sem("tap2"), sem("tap1"), sem("conv")
        gated, prod, ahi, alo, xup, xlow, vread = (
            sem("gated"), sem("prod"), sem("ahi"), sem("alo"), sem("xup"), sem("xlow"), sem("vread"))
        read_sems = {"vread": vread, "zsum": zsum, "xlow": xlow}
        mod_red, mod_ready = sem("mod_red"), sem("mod_ready")
        squared, summed, mean_ok, recip_ok, rstd_ok = (
            sem("squared"), sem("summed"), sem("mean_ok"), sem("recip_ok"), sem("rstd_ok"))
        normed, affine, h_hi, h_ready = sem("normed"), sem("affine"), sem("h_hi"), sem("h_ready")
        vsq, vred, vmean, vrec, vrstd = sem("vsq"), sem("vred"), sem("vmean"), sem("vrec"), sem("vrstd")
        masked, wsn, mixed, sv_ready = sem("masked"), sem("wsn"), sem("mixed"), sem("sv_ready")
        blk, blk_hi, blk_lo, cmp_gelu = sem("blk"), sem("blk_hi"), sem("blk_lo"), sem("cmp_gelu")
        stored = sem("stored")

        def vec(slice_, kt):
            return modv[:, slice_, kt:kt + 1] if isinstance(kt, int) else modv[:, slice_, bass.ds(kt, 1)]

        def col(c0, i):
            return small[:, c0 + i:c0 + i + 1] if isinstance(i, int) else small[:, bass.ds(i + c0, 1)]

        H_OF = {"sgu_v": (SH1_0, SC1_0, True), "up00": (SH2_0, SC2_0, True), "kv": (SH_KV, SC_KV, True),
                "q": (SH1_1, SC1_1, False), "up10": (SH2_1, SC2_1, True)}
        H_ORDER = [n for n, _ in PHASES if n in H_OF]
        STAT_ORDER = [n for n in H_ORDER if H_OF[n][2]]
        REDUCED = {"mod_b": [SH1_0], "sgu_v": [SC1_0], "sgu_u0": [G1_0], "sgu_u1": [SH2_0], "up00": [SC2_0],
                   "dn00": [G2_0], "up01": [SH_KV], "dn01": [SC_KV], "up02": [SH1_1], "kv": [SC1_1],
                   "cmp": [G1_1], "wo": [SH2_1], "up10": [SC2_1], "dn10": [G2_1]}
        GATE_OF = {"sgu_o0": G1_0, "sgu_o1": G1_0, "dn00": G2_0, "dn01": G2_0, "dn02": G2_0, "wo": G1_1,
                   "dn10": G2_1, "dn11": G2_1, "dn12": G2_1}
        PHASE_OF = {}
        for pname, chunks in PHASES:
            for ch in chunks:
                PHASE_OF[id(ch)] = pname

        def h_index(name):
            return H_ORDER.index(name)

        def free_wait(eng, cur):
            if cur.first.n["c"] < 2 and cur.second is None:
                return
            if cur.second is None:
                which, value = free_rule(ORDER[cur.first.n["c"] - 2])
            else:
                which, value = free_rule(cur.first)
                step = free_rule(cur.second)[1] - value
                value = value - step + cur.it * step
            eng.wait_ge(read_sems[which], value)

        def done_wait(eng, prev):
            eng.wait_ge(sub_done, prev.val(lambda c: c.n["S"] + c.nsub))

        def group(prev):
            return 4 * (prev.static(lambda c: c.n["c"] % 2))

        UNITS = [(h, qb) for h in range(NH) for qb in range(2)]
        area = attn_area
        pos = area[:, 7168:7168 + N_POS]
        stat_small = area[:, 6208:6208 + 32 + NB]
        neg_max = area[:, 6400:6400 + 96]
        denom = area[:, 6500:6500 + 96]
        coef = area[:, 6600:6600 + 96]
        k_gains = vstat[:, 0:3]
        rt_k = temp[:, :, :].rearrange("p a b -> p (a b)")

        def scores(i):
            return area[:, 528 * (i % 4):528 * (i % 4) + 528]

        def both(ap, n):
            return ap.rearrange("p (b k) -> p b k", b=2)[:, :, 0:n]

        def probs_t(i):
            o = 2112 + 640 * (i % 2)
            return area[:, o:o + 640]

        def attention_act(act):
            act.dma_start(pos, io["pos"]).then_inc(pos_loaded, 16)
            act.wait_ge(zsum, BY_NAME["q"][-1].n["zsum"] + 1)
            act.activation(area[:, 0:4096], q_raw, ACT.Square).then_inc(sem("at_sq"), 1)
            act.activation(area[:, 4096:6144], scratch[:, 4096:6144], ACT.Square).then_inc(sem("at_sq"), 1)
            act.wait_ge(sem("at_kc"), 1)
            act.activation(area[:, 6144:6144 + NB], kcmp[:, :], ACT.Square).then_inc(sem("at_sq"), 1)
            act.wait_ge(sem("at_rec"), 1)
            act.activation(rt_k, rt_k, ACT.Sqrt).then_inc(sem("at_rt"), 1)
            act.wait_ge(sem("at_rec"), 2)
            act.activation(stat_small, stat_small, ACT.Sqrt).then_inc(sem("at_rt"), 1)
            for i in range(len(UNITS) + 3):
                if i < len(UNITS):
                    h, qb = UNITS[i]
                    keys = P * (qb + 1)
                    act.wait_ge(sem("at_qk"), i + 1)
                    act.wait_ge(sem("at_kn"), 2)
                    if i >= 4:
                        act.wait_ge(sem("at_tr"), i - 3)
                    r = stat_small[:, 16 * qb + h:16 * qb + h + 1]
                    act.activation(both(scores(i)[:, 16:528], keys), both(banks[:, i % 2, :], keys), ACT.Copy,
                                   scale=r)
                    act.activation(scores(i)[:, 0:NCMP], banks[:, 6 + i % 2, 0:NCMP], ACT.Copy, scale=r) \
                        .then_inc(sem("at_sc"), 1)
                if 1 <= i <= len(UNITS):
                    j = i - 1
                    keys = P * (UNITS[j][1] + 1)
                    act.wait_ge(sem("at_mx"), j + 1)
                    for b, (o, n) in enumerate(((0, NCMP), (16, keys), (16 + T, keys))):
                        part = scores(j)[:, o:o + n]
                        last = act.activation(part, part, ACT.Exp, bias=neg_max[:, 3 * j + b:3 * j + b + 1],
                                              accum_out=denom[:, 3 * j + b:3 * j + b + 1])
                    last.then_inc(sem("at_ex"), 1)
                if i >= 3:
                    j = i - 3
                    h, qb = UNITS[j]
                    act.wait_ge(sem("at_pv"), j + 1)
                    act.activation(act_op[:, h, P * qb:P * (qb + 1)], banks[:, 6 + j % 2, 0:P], ACT.Copy) \
                        .then_inc(sem("at_ohi"), 1)

        def attention_dve(dve):
            dve.wait_ge(vread, BY_NAME["gate"][0].n["vread"] + 1)
            dve.wait_ge(pos_loaded, 16)
            for qb in range(2):
                dve.tensor_scalar(gates[:, qb, 0:NH], gates[:, qb, 0:NH],
                                  pos[:, 2 * DW + qb:2 * DW + qb + 1], None, ALU.mult)
            dve.tensor_scalar(k_gains, small[:, C_KG:C_KG + 3], small[:, C_QG:C_QG + 1], None, ALU.mult) \
                .then_inc(sem("at_gains"), 1)
            dve.wait_ge(sem("at_cmp"), 1)
            dve.tensor_copy(kcmp[:, :], banks[:, 5, 0:NB])
            dve.tensor_copy(vcmp[0:NCMP, :], banks[0:NCMP, 6, :]).then_inc(sem("at_kc"), 1)
            dve.wait_ge(sem("at_stat"), 2)
            dve.tensor_scalar(stat_small[:, 0:32], banks[:, 4, 0:32], 1.0 / HD, EPS, ALU.mult, ALU.add)
            dve.tensor_scalar(rt_k[:, 0:1536].rearrange("p (a b) -> p a b", a=3), banks[:, 0:3, :], 1.0 / HD, EPS,
                              ALU.mult, ALU.add)
            dve.tensor_scalar(rt_k[:, 1536:2048], banks[:, 7, :], 1.0 / HD, EPS, ALU.mult, ALU.add) \
                .then_inc(sem("at_ms"), 1)
            dve.wait_ge(sem("at_ms"), 1)
            dve.reciprocal(rt_k, rt_k).then_inc(sem("at_rec"), 1)
            dve.wait_ge(sem("at_stat"), 3)
            dve.tensor_scalar(stat_small[:, 32:32 + NB], banks[:, 3, 0:NB], 1.0 / HD, EPS, ALU.mult,
                              ALU.add).then_inc(sem("at_ms"), 1)
            dve.wait_ge(sem("at_ms"), 2)
            dve.reciprocal(stat_small, stat_small).then_inc(sem("at_rec"), 1)
            dve.wait_ge(sem("at_gains"), 1)
            dve.wait_ge(sem("at_rt"), 1)
            for b, k in ((1, k_slc), (2, k_win)):
                dve.scalar_tensor_tensor(out=k, in0=k, scalar=k_gains[:, b:b + 1],
                                         in1=rt_k[:, 1024 * (b - 1):1024 * b], op0=ALU.mult, op1=ALU.mult)
            dve.wait_ge(sem("at_rt"), 2)
            dve.scalar_tensor_tensor(out=kcmp[:, :], in0=kcmp[:, :], scalar=k_gains[:, 0:1],
                                     in1=stat_small[:, 32:32 + NB], op0=ALU.mult, op1=ALU.mult) \
                .then_inc(sem("at_kn"), 1)
            dve.tensor_scalar(stat_small[:, 0:32], stat_small[:, 0:32], float(HD) ** -0.5, None, ALU.mult) \
                .then_inc(sem("at_kn"), 1)
            for i in range(len(UNITS) + 3):
                if i < len(UNITS):
                    h, qb = UNITS[i]
                    keys = P * (qb + 1)
                    dist = pos[:, DW * qb:DW * (qb + 1)]
                    main, short = both(scores(i)[:, 16:528], keys), scores(i)[:, 0:NCMP]
                    dve.wait_ge(sem("at_sc"), i + 1)
                    dve.scalar_tensor_tensor(
                        out=main, in0=dist[:, 16:16 + keys].rearrange("p (o k) -> p o k", o=1)
                        .to_broadcast([P, 2, keys]), scalar=-slopes[h], in1=main, op0=ALU.mult, op1=ALU.add)
                    dve.scalar_tensor_tensor(out=short, in0=dist[:, 0:NCMP], scalar=-slopes[h], in1=short,
                                             op0=ALU.mult, op1=ALU.add).then_inc(sem("at_bias"), 1)
                    dve.wait_ge(sem("at_bias"), i + 1)
                    dve.tensor_reduce(neg_max[:, 3 * i + 1:3 * i + 3], main, AX.X, ALU.max, negate=True)
                    dve.tensor_reduce(neg_max[:, 3 * i:3 * i + 1], short, AX.X, ALU.max, negate=True) \
                        .then_inc(sem("at_mx"), 1)
                if 1 <= i <= len(UNITS):
                    j = i - 1
                    h, qb = UNITS[j]
                    d, f = denom[:, 3 * j:3 * j + 3], coef[:, 3 * j:3 * j + 3]
                    dve.wait_ge(sem("at_ex"), j + 1)
                    dve.tensor_scalar(d, d, 1e-30, None, ALU.max).then_inc(sem("at_den"), 1)
                    dve.wait_ge(sem("at_den"), j + 1)
                    dve.reciprocal(f, d).then_inc(sem("at_inv"), 1)
                    dve.wait_ge(sem("at_inv"), j + 1)
                    dve.tensor_tensor(f, f, gates[:, qb, :].rearrange("p (b h) -> p h b", h=NH)[:, h, :],
                                      ALU.mult).then_inc(sem("at_coef"), 1)
                if 2 <= i <= len(UNITS) + 1:
                    j = i - 2
                    keys = P * (UNITS[j][1] + 1)
                    dve.wait_ge(sem("at_tr"), j + 1)
                    if j >= 2:
                        dve.wait_ge(sem("at_pv"), j - 1)
                    dve.tensor_copy(both(probs_t(j)[:, 0:512], keys), both(banks[:, 4 + j % 2, :], keys))
                    dve.tensor_copy(probs_t(j)[0:NCMP, 512:640], banks[0:NCMP, 2 + j % 2, P:2 * P]) \
                        .then_inc(sem("at_pt"), 1)
                if i >= 3:
                    j = i - 3
                    h, qb = UNITS[j]
                    dve.wait_ge(sem("at_ohi"), j + 1)
                    dve.tensor_tensor(act_op[:, h, T + P * qb:T + P * (qb + 1)], banks[:, 6 + j % 2, 0:P],
                                      act_op[:, h, P * qb:P * (qb + 1)].bitcast(F32), ALU.subtract) \
                        .then_inc(sem("at_olo"), 1)

        def attention_pool(pool):
            for j in range(len(UNITS)):
                keys = P * (UNITS[j][1] + 1)
                pool.wait_ge(sem("at_coef"), j + 1)
                for b, (o, n) in enumerate(((0, NCMP), (16, keys), (16 + T, keys))):
                    part = scores(j)[:, o:o + n]
                    last = pool.tensor_scalar(part, part, coef[:, 3 * j + b:3 * j + b + 1], None, ALU.mult)
                last.then_inc(sem("at_scaled"), 1)

        def attention_pe(pe):
            gate = BY_NAME["gate"][0]
            pe.wait_ge(vread, gate.n["vread"] + 1)
            pe.wait_ge(mod_ready, ready_after(SH2_1))
            pe.wait_ge(sem("ident_set"), 1)
            pe.wait_ge(cmp_gelu, 1)
            pe.matmul(banks[:, 5, 0:NB], small[:, C_W2:C_W2 + HD], cmp_g[:, 0:NB], start=True, stop=True,
                      skip_group_check=True)
            for g in range(NKV):
                last = pe.matmul(banks[0:NCMP, 6, HD * g:HD * (g + 1)],
                                 cmp_g[:, NB + NCMP * g:NB + NCMP * (g + 1)], small[:, C_W2 + HD:C_W2 + 2 * HD],
                                 start=True, stop=True, skip_group_check=True)
            last.then_inc(sem("at_cmp"), 1)
            pe.wait_ge(sem("at_sq"), 1)
            for qb in range(2):
                for h in range(NH):
                    last = pe.matmul(banks[:, 4, 16 * qb + h:16 * qb + h + 1],
                                     area[:, T * h + P * qb:T * h + P * (qb + 1)], ones[:, 0:1],
                                     start=True, stop=True, skip_group_check=True)
            last.then_inc(sem("at_stat"), 1)
            pe.wait_ge(sem("at_sq"), 2)
            for i, b in enumerate((0, 1, 2, 7)):
                last = pe.matmul(banks[:, b, :], ones[:, :], area[:, 4096 + 512 * i:4096 + 512 * (i + 1)],
                                 start=True, stop=True)
            last.then_inc(sem("at_stat"), 1)
            pe.wait_ge(sem("at_sq"), 3)
            pe.matmul(banks[:, 3, 0:NB], ones[:, :], area[:, 6144:6144 + NB], start=True, stop=True,
                      skip_group_check=True).then_inc(sem("at_stat"), 1)
            pe.wait_ge(sem("at_kn"), 2)
            for i in range(len(UNITS) + 3):
                if i < len(UNITS):
                    h, qb = UNITS[i]
                    g, keys = h // GRP, P * (qb + 1)
                    if i >= 2:
                        pe.wait_ge(sem("at_sc"), i - 1)
                    if i >= 4:
                        pe.wait_ge(sem("at_olo"), i - 3)
                    query = q_raw[:, T * h + P * qb:T * h + P * (qb + 1)]
                    pe.matmul(banks[:, i % 2, 0:keys], query, k_slc[:, T * g:T * g + keys], start=True, stop=True,
                              skip_group_check=True)
                    pe.matmul(banks[:, i % 2, T:T + keys], query, k_win[:, T * g:T * g + keys], start=True,
                              stop=True, skip_group_check=True)
                    pe.matmul(banks[:, 6 + i % 2, 0:NCMP], query, kcmp[:, NCMP * g:NCMP * (g + 1)], start=True,
                              stop=True, skip_group_check=True).then_inc(sem("at_qk"), 1)
                if 2 <= i <= len(UNITS) + 1:
                    j = i - 2
                    qb = UNITS[j][1]
                    pe.wait_ge(sem("at_scaled"), j + 1)
                    if j >= 2:
                        pe.wait_ge(sem("at_pt"), j - 1)
                    for b in range(2):
                        for n in range(qb + 1):
                            o = T * b + P * n
                            pe.transpose(banks[:, 4 + j % 2, o:o + P], scores(j)[:, 16 + o:16 + o + P],
                                         ident[:, :])
                    pe.transpose(banks[0:NCMP, 2 + j % 2, P:2 * P], scores(j)[:, 0:NCMP], ident[:, :]) \
                        .then_inc(sem("at_tr"), 1)
                if i >= 3:
                    j = i - 3
                    h, qb = UNITS[j]
                    g = h // GRP
                    pe.wait_ge(sem("at_pt"), j + 1)
                    pe.wait_ge(sem("at_sc"), min(j + 3, len(UNITS)))
                    if j >= 2:
                        pe.wait_ge(sem("at_olo"), j - 1)
                    out = banks[:, 6 + j % 2, 0:P]
                    pt = probs_t(j)
                    for b, v in ((0, v_slc), (1, v_win)):
                        for n in range(qb + 1):
                            pe.matmul(out, v[:, 512 * n + HD * g:512 * n + HD * (g + 1)],
                                      pt[:, T * b + P * n:T * b + P * (n + 1)], start=(b == 0 and n == 0),
                                      stop=False, skip_group_check=True)
                    pe.matmul(out, vcmp[0:NCMP, HD * g:HD * (g + 1)], pt[0:NCMP, 512:640], start=False, stop=True,
                              skip_group_check=True).then_inc(sem("at_pv"), 1)

        def z_view(prev):
            kind = prev.first.kind
            if kind in ("ua", "uv"):
                return zpad[:, :, 2:T + 2]
            if kind == "u":
                return y4
            if kind == "q":
                o = TPC * T * BY_NAME["q"].index(prev.first)
                return q_raw[:, o:o + TPC * T].rearrange("p (j t) -> p j t", j=TPC)
            dst = {0: kc0, 1: vc0, 2: k_slc, 4: k_win}[prev.first.loc]
            return dst.rearrange("p (j t) -> p j t", j=4)

        def local(prev):
            phase = BY_NAME[PHASE_OF[id(prev.first)]]
            c0 = phase[0].n["c"]
            per = 2 if prev.first.kind in ("ua", "uv") else 1
            return prev.val(lambda c: (c.n["c"] - c0) // per)

        def act_tiles(prev):
            k = local(prev)
            return act_op[:, TPC * k:TPC * k + TPC, :] if isinstance(k, int) else \
                act_op[:, bass.ds(k * TPC, TPC), :]

        def v_tiles(prev, n):
            k = local(prev)
            rows = sv[:, 4 * k:4 * k + 4, :] if isinstance(k, int) else sv[:, bass.ds(k * 4, 4), :]
            return rows[:, :, P * n:P * (n + 1)]

        def x_tile(prev, j):
            k = local(prev)
            return x[:, TPC * k + j, :]

        def conv_col(prev, tap, j):
            name = PHASE_OF[id(prev.first)]
            layer, part = int(name[2]), int(name[3])
            k = local(prev)
            base = (C_CONVB + layer * 2 * FT) if tap is None else C_CONVW + (layer * 3 + tap) * 2 * FT
            base += (FT if prev.first.kind == "uv" else 0) + 16 * part + j
            return small[:, base + 4 * k:base + 4 * k + 1] if isinstance(k, int) else \
                small[:, bass.ds(k * 4 + base, 1)]

        def blk_view(i):
            return blk_op[:, i * CMP_LEN * 2 * NB:(i + 1) * CMP_LEN * 2 * NB].rearrange(
                "p (l n) -> p l n", l=CMP_LEN)

        def mix_dve(dve):
            dve.wait_ge(vsq, 16)
            dve.tensor_reduce(vstat[:, 16:18], vstat[:, 0:16].rearrange("p (n c) -> p n c", n=2), AX.X, ALU.add) \
                .then_inc(vred, 1)
            dve.wait_ge(vred, 1)
            dve.tensor_scalar(vstat[:, 20:22], vstat[:, 16:18], 1.0 / SGU_W, EPS, ALU.mult, ALU.add) \
                .then_inc(vmean, 1)
            dve.wait_ge(vmean, 1)
            dve.reciprocal(vstat[:, 18:20], vstat[:, 20:22]).then_inc(vrec, 1)
            dve.wait_ge(vrstd, 1)
            dve.wait_ge(masked, 1)
            for n in range(2):
                dve.tensor_scalar(w_sn[:, n, :, :], w_sT, vstat[:, 18 + n:19 + n], None, ALU.mult).then_inc(wsn, 1)
            dve.wait_ge(mix_loaded, 32)
            for ct in range(SGU_W // P):
                dve.wait_ge(mixed, ct + 1)
                dve.scalar_tensor_tensor(
                    out=sv[:, ct, :].rearrange("p (n t) -> p n t", n=2),
                    in0=banks[:, ct % 4, 0:T].rearrange("p (n t) -> p n t", n=2), scalar=col(C_VGAIN, ct),
                    in1=b_sb[:, ct // 2, :].rearrange("p (o t) -> p o t", o=1).to_broadcast([P, 2, P]),
                    op0=ALU.mult, op1=ALU.add).then_inc(sv_ready, 1)

        block = ctx.enter_context(nc.Block())

        @block.sync
        def _(sp):
            sp.dma_start(small[:, :], io["small"]).then_inc(small_loaded, 16)
            sp.dma_start(x[:, :, :], io["x"].rearrange("p (k t) -> p k t", t=T)).then_inc(x_loaded, 16)
            for s in range(RAW_SLOTS):
                sp.dma_start(raw[:, s, :], io["stream"][s * P:(s + 1) * P, :]).then_inc(raw_loaded[s], 16)
            sp.dma_start(w_sT, io["w_s"].rearrange("p (g t) -> p g t", g=SGU_G)).then_inc(mix_loaded, 16)
            sp.dma_start(b_sb, io["b_s"].rearrange("p (g t) -> p g t", g=SGU_G)).then_inc(mix_loaded, 16)
            full = n_pieces // RAW_SLOTS
            with sp.Fori(1, full) as i:
                for s in range(RAW_SLOTS):
                    sp.wait_ge(stream, i * (2 * RAW_SLOTS) + (2 * (s + 1) - 2 * RAW_SLOTS))
                    sp.dma_start(raw[:, s, :], io["stream"][bass.ds(i * (RAW_SLOTS * P) + s * P, P), :]) \
                        .then_inc(raw_loaded[s], 16)
            for g in range(full * RAW_SLOTS, n_pieces):
                sp.wait_ge(stream, 2 * (g - RAW_SLOTS + 1))
                sp.dma_start(raw[:, g % RAW_SLOTS, :], io["stream"][g * P:(g + 1) * P, :]) \
                    .then_inc(raw_loaded[g % RAW_SLOTS], 16)
            last = phases[-1][1]
            if last[0].kind == "dn" and len(last) == 4:
                for i, ch in enumerate(last):
                    sp.wait_ge(xlow, ch.n["xup"] + 1)
                    sp.dma_start(io["out"].rearrange("p (k t) -> p k t", t=T)[:, TPC * i:TPC * (i + 1), :],
                                 x[:, TPC * i:TPC * (i + 1), :]).then_inc(stored, 16)
                sp.wait_ge(stored, 64)

        @block.scalar
        def _(act):
            act.wait_ge(small_loaded, 16)
            act.activation(silu_c[:, :], small[:, C_C:C_C + KT], ACT.Silu).then_inc(c_ready, 1)

            def split_hi(cur, u, tok):
                off, chunk = cur.first.piece_of[tok], cur.first
                slot = cur.static(lambda c: (c.n["G"] + off) % RAW_SLOTS)
                out = cur.static(lambda c: (c.n["S"] + u) % SPLIT_SLOTS)
                act.wait_ge(raw_loaded[slot], cur.val(lambda c: 16 * ((c.n["G"] + off) // RAW_SLOTS + 1)))
                if cur.second is not None or chunk.n["S"] + u >= SPLIT_SLOTS:
                    act.wait_ge(sub_done, cur.val(lambda c: c.n["S"] + u - SPLIT_SLOTS + 1))
                n = KT * NGATE if chunk.kind == "gate" else SUB
                half = (u % 2) * SUB
                act.activation(w_hi[:, out, 0:n], raw[:, slot, half:half + n], ACT.Copy).then_inc(hi_ready, 1)

            def make_h(name):
                i = h_index(name)
                if H_OF[name][2]:
                    k = STAT_ORDER.index(name)
                    if k == 0:
                        act.wait_ge(x_loaded, 16)
                    for q in range(4):
                        if k > 0:
                            before = BY_NAME[{"up00": "sgu_o1", "kv": "dn02", "up10": "wo"}[name]][q]
                            act.wait_ge(xlow, before.n["xup"] + 1)
                        if q >= 2:
                            act.wait_ge(summed, 4 * k + q - 1)
                        act.activation(temp[:, q % 2, :], x[:, TPC * q:TPC * (q + 1), :]
                                       .rearrange("p k t -> p (k t)"), ACT.Square).then_inc(squared, 1)
                    act.wait_ge(recip_ok, k + 1)
                    act.activation(rstd[:, :], rstd[:, :], ACT.Sqrt).then_inc(rstd_ok, 1)
                for q in range(4):
                    act.wait_ge(affine, 4 * i + q + 1)
                    act.activation(h_op[:, TPC * q:TPC * (q + 1), 0:T],
                                   temp[:, q % 2, :].rearrange("p (k t) -> p k t", t=T), ACT.Copy).then_inc(h_hi, 1)

            def stages(name, cur, prev, first):
                todo = [[], [], [], []]
                kind = prev.first.kind if prev else "mod"
                if kind == "mod":
                    pass
                elif kind in ("ua", "uv", "u", "kvf", "q", "cmp"):
                    g = group(prev)

                    def copy_lo():
                        done_wait(act, prev)
                        if kind == "cmp":
                            out, src = cmp_g[:, :].rearrange("p (i n) -> p i n", i=2), banks[:, g:g + 2, NB:2 * NB]
                        else:
                            out, src = z_view(prev), banks[:, g:g + 4, T:HILO]
                        if kind in ("ua", "uv"):
                            act.wait_ge(zeroed, 1)
                            act.wait_ge(conv, prev.val(lambda c: c.n["conv"]))
                        if kind == "u":
                            act.wait_ge(alo, prev.val(lambda c: c.n["alo"]))
                        if kind == "q":
                            act.wait_ge(blk, 2)
                        act.activation(out, src, ACT.Copy).then_inc(zlo, 1)
                    todo[0].append(copy_lo)
                    if kind in ("ua", "uv"):
                        def last_tap():
                            act.wait_ge(zsum, prev.val(lambda c: c.n["zsum"] + 1))
                            act.wait_ge(alo, prev.val(lambda c: c.n["alo"]))
                            act.wait_ge(gated, prev.val(lambda c: c.n["gated"]))
                            for j in range(TPC):
                                act.activation(y4[:, j, :], zpad[:, j, 2:T + 2], ACT.Identity,
                                               bias=conv_col(prev, None, j),
                                               scale=conv_col(prev, 2, j)).then_inc(tap2, 1)
                        todo[1].append(last_tap)
                    if kind == "ua":
                        def silu():
                            act.wait_ge(conv, prev.val(lambda c: c.n["conv"] + 1))
                            act.wait_ge(prod, prev.val(lambda c: c.n["prod"]))
                            act.activation(gt, y, ACT.Silu).then_inc(gated, 1)
                        todo[2].append(silu)
                    if kind == "u":
                        def gelu():
                            act.wait_ge(zsum, prev.val(lambda c: c.n["zsum"] + 1))
                            act.activation(gt, y, ACT.Gelu_apprx_tanh).then_inc(gated, 1)
                        todo[1].append(gelu)
                    if kind in ("uv", "u"):
                        def act_hi():
                            act.wait_ge(prod, prev.val(lambda c: c.n["prod"] + 1))
                            act.activation(act_tiles(prev)[:, :, 0:T], y4, ACT.Copy).then_inc(ahi, 1)
                        todo[3].append(act_hi)
                    if kind == "cmp":
                        def gelu_cmp():
                            act.wait_ge(zsum, prev.val(lambda c: c.n["zsum"] + 1))
                            act.activation(cmp_g[:, :], cmp_g[:, :], ACT.Gelu_apprx_tanh).then_inc(cmp_gelu, 1)
                        todo[1].append(gelu_cmp)
                elif kind == "v":
                    g = group(prev)

                    def gelu_v():
                        done_wait(act, prev)
                        for n in range(2):
                            last = act.activation(v_tiles(prev, n),
                                                  banks[:, g + n, :].rearrange("p (c t) -> p c t", t=P),
                                                  ACT.Gelu_apprx_tanh)
                        last.then_inc(vread, 1)
                    todo[0].append(gelu_v)

                    def square_v():
                        act.wait_ge(vread, prev.val(lambda c: c.n["vread"] + 1))
                        if prev.first.n["vread"] > 0 or prev.second is not None:
                            act.wait_ge(vsq, prev.val(lambda c: 2 * c.n["vread"]))
                        for n in range(2):
                            loc = prev.val(lambda c: c.n["c"] + 8 * n)
                            out = vstat[:, loc:loc + 1] if isinstance(loc, int) else vstat[:, bass.ds(loc, 1)]
                            act.activation(temp[:, n, 0:COLS].rearrange("p (c t) -> p c t", t=P),
                                           v_tiles(prev, n), ACT.Square, accum_out=out).then_inc(vsq, 1)
                    todo[2].append(square_v)
                elif kind == "kvt":
                    g = group(prev)

                    def copy_v():
                        done_wait(act, prev)
                        dst = v_slc if prev.first.loc == 3 else v_win
                        act.activation(dst.rearrange("p (n c) -> p n c", n=2), banks[:, g:g + 2, :],
                                       ACT.Copy).then_inc(vread, 1)
                    todo[0].append(copy_v)
                elif kind == "gate":
                    g = group(prev)

                    def sigmoid():
                        done_wait(act, prev)
                        act.activation(gates[:, :, :], banks[:, g:g + 2, 0:NGATE], ACT.Sigmoid).then_inc(vread, 1)
                    todo[0].append(sigmoid)
                if name == "kv" and not first and cur.first.loc in (3, 4):
                    i = cur.first.loc - 3

                    def blocks_hi():
                        act.wait_ge(blk, i + 1)
                        act.activation(blk_view(i)[:, :, 0:NB], blocks.rearrange("p (l n) -> p l n", l=CMP_LEN),
                                       ACT.Copy).then_inc(blk_hi, 1)
                    todo[3].append(blocks_hi)
                if first and name == "sgu_u0":
                    def v_rstd():
                        act.wait_ge(vrec, 1)
                        act.activation(vstat[:, 18:20], vstat[:, 18:20], ACT.Sqrt).then_inc(vrstd, 1)
                    todo[3].append(v_rstd)
                if first and name == "wo":
                    todo[3].append(lambda: attention_act(act))
                if first and name in H_OF:
                    todo[3].append(lambda: make_h(name))
                return todo

            def step(name, cur, prev, first):
                if cur.first.kind == "mod":
                    return
                todo, u, e = stages(name, cur, prev, first), 0, 0
                if first and (name in H_OF or name in ("wo", "sgu_u0")):
                    todo = [[f for part in todo for f in part], [], [], []]
                for tok, t in enumerate(cur.first.tokens):
                    if t == "s":
                        split_hi(cur, u, tok)
                        u += 1
                    elif t == "E":
                        for f in (todo[e] if cur.first.kind != "gate" else [f for part in todo for f in part]):
                            f()
                        e += 1

            walk(act, phases, step)
            if phases[-1][1][-1].kind != "dn":
                for part in stages("end", At(phases[-1][1][-1]), At(phases[-1][1][-1]), False):
                    for f in part:
                        f()

        @block.vector
        def _(dve):
            dve.memset(zpad[:, :, :], 0.0).then_inc(zeroed, 1)
            dve.memset(ones[:, :], 1.0).then_inc(consts_set, 1)

            def split_lo(cur, u, tok):
                off, chunk = cur.first.piece_of[tok], cur.first
                slot = cur.static(lambda c: (c.n["G"] + off) % RAW_SLOTS)
                out = cur.static(lambda c: (c.n["S"] + u) % SPLIT_SLOTS)
                dve.wait_ge(hi_ready, cur.val(lambda c: c.n["S"] + u + 1))
                n = KT * NGATE if chunk.kind == "gate" else SUB
                half = (u % 2) * SUB
                dve.tensor_tensor(w_lo[:, out, 0:n], raw[:, slot, half:half + n], w_hi[:, out, 0:n].bitcast(F32),
                                  ALU.subtract).then_inc(stream, 2 if chunk.kind == "gate" else 1)

            def mod_piece(cur, m, tok):
                off = cur.first.piece_of[tok]
                slot = cur.static(lambda c: (c.n["G"] + off) % RAW_SLOTS)
                row = cur.val(lambda c: (c.n["M"] + m) % KT)
                dve.wait_ge(raw_loaded[slot], cur.val(lambda c: 16 * ((c.n["G"] + off) // RAW_SLOTS + 1)))
                if cur.second is None and (cur.first.n["M"] + m) % KT == 0:
                    k = (cur.first.n["M"] + m) // KT
                    if k:
                        dve.wait_ge(mod_red, k)
                    dve.wait_ge(c_ready, 1)
                    dve.tensor_scalar(mod_acc[:, :], raw[:, slot, :], silu_c[:, 0:1], None, ALU.mult) \
                        .then_inc(stream, 2)
                    return
                before = [i for i in range(off) if cur.first.kinds_of[i] == "m"]
                if before:
                    dve.wait_ge(stream, cur.val(lambda c: 2 * (c.n["G"] + before[-1] + 1)))
                elif cur.second is None:
                    dve.wait_ge(stream, 2 * cur.first.last_m)
                else:
                    back = cur.second.n["G"] - cur.second.last_m
                    dve.wait_ge(stream, cur.val(lambda c: 2 * (c.n["G"] - back)))
                s = silu_c[:, row:row + 1] if isinstance(row, int) else silu_c[:, bass.ds(row, 1)]
                dve.scalar_tensor_tensor(out=mod_acc[:, :], in0=raw[:, slot, :], scalar=s, in1=mod_acc[:, :],
                                         op0=ALU.mult, op1=ALU.add).then_inc(stream, 2)

            def mod_vector(k):
                dve.wait_ge(mod_red, k + 1)
                dve.tensor_tensor(modv[:, k, :], banks[:, 3, 16 * (k % 2):16 * (k % 2) + KT],
                                  small[:, C_MODB + KT * k:C_MODB + KT * (k + 1)], ALU.add).then_inc(mod_ready, 1)
                if k in GAIN_OF:
                    g = C_GAIN + KT * GAIN_OF[k]
                    dve.wait_ge(mod_ready, ready_after(k) - 1)
                    dve.scalar_tensor_tensor(out=modv[:, k, :], in0=modv[:, k, :], scalar=1.0,
                                             in1=small[:, g:g + KT], op0=ALU.add, op1=ALU.mult) \
                        .then_inc(mod_ready, 1)

            def make_h(name):
                i = h_index(name)
                shift, scale, fresh = H_OF[name]
                if fresh:
                    k = STAT_ORDER.index(name)
                    dve.wait_ge(summed, 4 * k + 4)
                    dve.tensor_scalar(rstd[:, :], banks[:, 0, 0:T], 1.0 / D, EPS, ALU.mult, ALU.add) \
                        .then_inc(mean_ok, 1)
                    dve.wait_ge(mean_ok, k + 1)
                    dve.reciprocal(rstd[:, :], rstd[:, :]).then_inc(recip_ok, 1)
                    dve.wait_ge(rstd_ok, k + 1)
                dve.wait_ge(mod_ready, ready_after(scale))
                if name == "q":
                    dve.wait_ge(blk_lo, 2)

                def norm(q):
                    if q >= 2:
                        dve.wait_ge(h_ready, 4 * i + q - 1)
                    elif not fresh:
                        dve.wait_ge(h_ready, 4 * i)
                    dve.tensor_tensor(temp[:, q % 2, :].rearrange("p (k t) -> p k t", t=T),
                                      x[:, TPC * q:TPC * (q + 1), :],
                                      rstd[:, :].rearrange("p (o t) -> p o t", o=1).to_broadcast([P, TPC, T]),
                                      ALU.mult).then_inc(normed, 1)

                def scale_shift(q):
                    dve.wait_ge(normed, 4 * i + q + 1)
                    for j in range(TPC):
                        part = temp[:, q % 2, T * j:T * (j + 1)]
                        kt = TPC * q + j
                        last = dve.tensor_scalar(part, part, vec(scale, kt), vec(shift, kt), ALU.mult, ALU.add)
                    last.then_inc(affine, 1)

                def low(q):
                    dve.wait_ge(h_hi, 4 * i + q + 1)
                    rows = h_op[:, TPC * q:TPC * (q + 1), :]
                    dve.tensor_tensor(rows[:, :, T:HILO], temp[:, q % 2, :].rearrange("p (k t) -> p k t", t=T),
                                      rows[:, :, 0:T].bitcast(F32), ALU.subtract).then_inc(h_ready, 1)

                for q in range(5):
                    if q < 4:
                        norm(q) if q < 2 else None
                    if q >= 1:
                        low(q - 1)
                        if q + 1 < 4:
                            norm(q + 1)
                    if q < 4:
                        scale_shift(q)

            def stages(name, cur, prev, first):
                todo = [[], [], [], []]
                kind = prev.first.kind if prev else "mod"
                if kind in ("ua", "uv", "u", "kvf", "q", "cmp"):
                    g = group(prev)

                    def add_hi():
                        dve.wait_ge(zlo, prev.val(lambda c: c.n["zlo"] + 1))
                        if kind == "cmp":
                            out, src = cmp_g[:, :].rearrange("p (i n) -> p i n", i=2), banks[:, g:g + 2, 0:NB]
                        else:
                            out, src = z_view(prev), banks[:, g:g + 4, 0:T]
                        dve.tensor_tensor(out, src, out, ALU.add).then_inc(zsum, 1)
                    todo[0].append(add_hi)
                if kind in ("ua", "uv"):
                    def taps():
                        dve.wait_ge(zeroed, 1)
                        for j in range(TPC):
                            dve.wait_ge(tap2, prev.val(lambda c: TPC * c.n["tap2"]) + j + 1)
                            dve.scalar_tensor_tensor(
                                out=y4[:, j, :], in0=zpad[:, j, 1:1 + T], scalar=conv_col(prev, 1, j),
                                in1=y4[:, j, :], op0=ALU.mult, op1=ALU.add).then_inc(tap1, 1)
                        for j in range(TPC):
                            dve.wait_ge(tap1, prev.val(lambda c: TPC * c.n["tap1"]) + j + 1)
                            last = dve.scalar_tensor_tensor(
                                out=y4[:, j, :], in0=zpad[:, j, 0:T], scalar=conv_col(prev, 0, j),
                                in1=y4[:, j, :], op0=ALU.mult, op1=ALU.add)
                        last.then_inc(conv, 1)
                    todo[1].append(taps)
                if kind == "dn":
                    g = group(prev)
                    gate = GATE_OF[PHASE_OF[id(prev.first)]]
                    kt = prev.first.loc

                    def add_x(part):
                        def go():
                            if part == 0:
                                done_wait(dve, prev)
                                dve.wait_ge(mod_ready, ready_after(gate))
                                if prev.first.n["xup"] > 0:
                                    dve.wait_ge(xlow, prev.first.n["xup"])
                            else:
                                dve.wait_ge(xup, prev.first.n["xup"] + 1)
                            for j in range(TPC):
                                tile = x[:, TPC * kt + j, :]
                                last = dve.scalar_tensor_tensor(
                                    out=tile, in0=banks[:, g + j, T * part:T * (part + 1)],
                                    scalar=vec(gate, TPC * kt + j), in1=tile, op0=ALU.mult, op1=ALU.add)
                            last.then_inc(xlow if part else xup, 1)
                        return go
                    todo[0].append(add_x(0))
                    todo[1].append(add_x(1))
                if first and name == "sgu_u0":
                    todo[3].append(lambda: mix_dve(dve))
                if first and name == "wo":
                    todo[3].append(lambda: attention_dve(dve))
                if first and name in H_OF:
                    todo[3].append(lambda: make_h(name))
                return todo

            def step(name, cur, prev, first):
                if first:
                    for k in REDUCED.get(name, []):
                        if cur.first.kind == "mod":
                            mod_vector(k)
                if cur.first.kind == "mod":
                    todo = [[], [], [], []]
                else:
                    todo = stages(name, cur, prev, first)
                if first and (name in H_OF or name in ("wo", "sgu_u0")):
                    todo = [[f for part in todo for f in part], [], [], []]
                if first and cur.first.kind != "mod":
                    todo[0] = [lambda k=k: mod_vector(k) for k in REDUCED.get(name, [])] + todo[0]
                u = m = e = 0
                for tok, t in enumerate(cur.first.tokens):
                    if t == "s":
                        split_lo(cur, u, tok)
                        u += 1
                    elif t == "m":
                        mod_piece(cur, m, tok)
                        m += 1
                    elif t == "E":
                        for f in (todo[e] if cur.first.kind != "gate" else [f for part in todo for f in part]):
                            f()
                        e += 1

            walk(dve, phases, step)
            for part in stages("end", At(phases[-1][1][-1]), At(phases[-1][1][-1]), False):
                for f in part:
                    f()

        @block.gpsimd
        def _(pool):
            pool.memset(ident[:, :], 0.0).then_inc(sem("ident_zero"), 1)
            pool.wait_ge(sem("ident_zero"), 1)
            pool.affine_select(out=ident[:, :], in_=ident[:, :], compare_op=ALU.not_equal, fill=1.0, base=0,
                               pattern=[[-1, P]], channel_multiplier=1).then_inc(sem("ident_set"), 1)
            pool.wait_ge(mix_loaded, 32)
            pool.affine_select(out=w_sT, in_=w_sT, compare_op=ALU.is_ge, fill=0.0, base=0,
                               pattern=[[0, SGU_G], [1, P]], channel_multiplier=-1).then_inc(masked, 1)

            def stages(name, cur, prev, first):
                todo = [[], [], [], []]
                kind = prev.first.kind if prev else "mod"
                if kind in ("uv", "u"):
                    def product():
                        if kind == "uv":
                            pool.wait_ge(conv, prev.val(lambda c: c.n["conv"] + 1))
                            pool.wait_ge(gated, prev.val(lambda c: c.n["gated"]))
                            pool.tensor_tensor(y, y, gt, ALU.mult).then_inc(prod, 1)
                        else:
                            half = int(PHASE_OF[id(prev.first)][-1])
                            ct = 16 * half + TPC * prev.first.loc
                            pool.wait_ge(gated, prev.val(lambda c: c.n["gated"] + 1))
                            pool.wait_ge(sv_ready, ct + 4)
                            pool.tensor_tensor(y4, gt4, sv[:, ct:ct + 4, :], ALU.mult).then_inc(prod, 1)

                    def low():
                        pool.wait_ge(ahi, prev.val(lambda c: c.n["ahi"] + 1))
                        rows = act_tiles(prev)
                        pool.tensor_tensor(rows[:, :, T:HILO], y4, rows[:, :, 0:T].bitcast(F32), ALU.subtract) \
                            .then_inc(alo, 1)
                    todo[2].append(product)
                    todo[3].append(low)
                if name == "kv" and not first and cur.first.loc in (3, 4):
                    i = cur.first.loc - 3

                    def make_blocks():
                        src = (kc0, vc0)[i]
                        pool.wait_ge(zsum, BY_NAME["kv"][i].n["zsum"] + 1)
                        if i:
                            pool.wait_ge(blk_lo, 1)
                        else:
                            pool.wait_ge(h_ready, 4 * (h_index("kv") + 1))
                        for g in range(NKV):
                            tok = src[:, g * T:(g + 1) * T].rearrange("p (n l) -> p l n", l=CMP_STRIDE)
                            for part in range(2):
                                ins = pool.tensor_tensor(
                                    blocks.rearrange("p (l g n) -> p l g n", l=CMP_LEN, g=NKV)
                                    [:, 16 * part:16 * (part + 1), g, :],
                                    tok[:, :, part:part + NCMP],
                                    small[:, C_POS + CMP_LEN * i + 16 * part:C_POS + CMP_LEN * i + 16 * (part + 1)]
                                    .rearrange("p (l o) -> p l o", o=1).to_broadcast([P, CMP_STRIDE, NCMP]),
                                    ALU.add)
                        ins.then_inc(blk, 1)
                        pool.wait_ge(blk_hi, i + 1)
                        pool.tensor_tensor(blk_view(i)[:, :, NB:2 * NB],
                                           blocks.rearrange("p (l n) -> p l n", l=CMP_LEN),
                                           blk_view(i)[:, :, 0:NB].bitcast(F32), ALU.subtract).then_inc(blk_lo, 1)
                    todo[3].append(make_blocks)
                if first and name == "wo":
                    todo[3].append(lambda: attention_pool(pool))
                return todo

            def step(name, cur, prev, first):
                for part in stages(name, cur, prev, first):
                    for f in part:
                        f()

            walk(pool, phases, step)
            for part in stages("end", At(phases[-1][1][-1]), At(phases[-1][1][-1]), False):
                for f in part:
                    f()

        @block.tensor
        def _(pe):
            def reduce_mod(k):
                g_end = None
                for name, chunks in PHASES:
                    for ch in chunks:
                        if ch.n["M"] < KT * (k + 1) <= ch.n["M"] + ch.kinds_of.count("m"):
                            pos = [i for i, kk in enumerate(ch.kinds_of) if kk == "m"]
                            g_end = ch.n["G"] + pos[KT * (k + 1) - ch.n["M"] - 1]
                pe.wait_ge(stream, 2 * (g_end + 1))
                pe.wait_ge(consts_set, 1)
                if k:
                    pe.wait_ge(mod_ready, ready_after(k - 1))
                for kt in range(KT):
                    last = pe.matmul(banks[:, 3, 16 * (k % 2) + kt:16 * (k % 2) + kt + 1],
                                     mod_acc[:, P * kt:P * (kt + 1)], ones[:, 0:1], start=True, stop=True,
                                     skip_group_check=True)
                last.then_inc(mod_red, 1)

            def operand_wait(name, first, u):
                if not first:
                    return
                if name == "wo":
                    pe.wait_ge(sem("at_olo"), 4 * (u + 1))
                need = u // 2 + 1
                if u % 2:
                    return
                if name in H_OF:
                    pe.wait_ge(h_ready, 4 * h_index(name) + need)
                elif name.startswith("dn"):
                    src = BY_NAME["up" + name[2:]]
                    v = [c for c in src if c.kind == "uv"]
                    pe.wait_ge(alo, v[min(need, len(v)) - 1].n["alo"] + 1)
                elif name.startswith("sgu_o"):
                    pe.wait_ge(alo, BY_NAME["sgu_u" + name[-1]][need - 1].n["alo"] + 1)
                elif name == "cmp" and u == 0:
                    pe.wait_ge(blk_lo, 2)

            def step(name, cur, prev, first):
                kind = cur.first.kind
                if first and kind == "mod":
                    for k in REDUCED.get(name, []):
                        reduce_mod(k)
                if kind == "mod":
                    return
                g = group(cur)
                reduces = REDUCED.get(name, []) if first else []
                free_wait(pe, cur)
                if reduces:
                    c = cur.first.n["c"]
                    if c >= 2:
                        which, value = free_rule(ORDER[c - 2 if c % 2 == 0 else c - 1])
                        pe.wait_ge(read_sems[which], value)
                    for k in reduces:
                        reduce_mod(k)
                if first and name == "sgu_u0":
                    mix_pe()
                if first and name == "wo":
                    attention_pe(pe)
                if first and name in H_OF and H_OF[name][2]:
                    k = STAT_ORDER.index(name)
                    for q in range(4):
                        pe.wait_ge(squared, 4 * k + q + 1)
                        for j in range(TPC):
                            last = pe.matmul(banks[:, 0, 0:T], ones[:, :], temp[:, q % 2, T * j:T * (j + 1)],
                                             start=(q == 0 and j == 0), stop=(q == 3 and j == 3))
                        last.then_inc(summed, 1)
                operand = h_op if name in ("sgu_v", "sgu_u0", "sgu_u1", "kv", "q", "gate") or \
                    name.startswith("up") else act_op
                tokens = cur.first.tokens
                u = 0
                for tok, t in enumerate(tokens):
                    if t != "s":
                        continue
                    off = cur.first.piece_of[tok]
                    slot = cur.static(lambda c: (c.n["S"] + u) % SPLIT_SLOTS)
                    pe.wait_ge(stream, cur.val(lambda c: 2 * (c.n["G"] + off) + u % 2 + 1))
                    operand_wait(name, first, u)
                    if kind in ("v", "kvt"):
                        hi = w_hi[:, slot, :].rearrange("p (k c) -> p k c", k=2)
                        lo = w_lo[:, slot, :].rearrange("p (k c) -> p k c", k=2)
                        for n in range(2):
                            for k in range(2):
                                kt = 2 * u + k
                                a_hi, a_lo = (operand[:, kt, o + P * n:o + P * (n + 1)] for o in (0, T))
                                out = banks[:, g + n, :]
                                pe.matmul(out, a_hi, hi[:, k, :], start=(kt == 0), stop=False,
                                          skip_group_check=True)
                                pe.matmul(out, a_hi, lo[:, k, :], start=False, stop=False, skip_group_check=True)
                                last = pe.matmul(out, a_lo, hi[:, k, :], start=False, stop=(kt == KT - 1),
                                                 skip_group_check=True)
                    elif kind == "gate":
                        hi = w_hi[:, slot, 0:KT * NGATE].rearrange("p (k c) -> p k c", k=KT)
                        lo = w_lo[:, slot, 0:KT * NGATE].rearrange("p (k c) -> p k c", k=KT)
                        for n in range(2):
                            for kt in range(KT):
                                a_hi, a_lo = (operand[:, kt, o + P * n:o + P * (n + 1)] for o in (0, T))
                                out = banks[:, g + n, 0:NGATE]
                                pe.matmul(out, a_hi, hi[:, kt, :], start=(kt == 0), stop=False,
                                          skip_group_check=True)
                                pe.matmul(out, a_hi, lo[:, kt, :], start=False, stop=False, skip_group_check=True)
                                last = pe.matmul(out, a_lo, hi[:, kt, :], start=False, stop=(kt == KT - 1),
                                                 skip_group_check=True)
                    elif kind == "cmp":
                        hi = w_hi[:, slot, :].rearrange("p (l c) -> p l c", l=8)
                        lo = w_lo[:, slot, :].rearrange("p (l c) -> p l c", l=8)
                        i = u // 4
                        for k in range(8):
                            row = 8 * (u % 4) + k
                            rows = blk_view(i)[:, row, :]
                            pe.matmul(banks[:, g + i, 0:2 * NB], hi[:, k, :], rows, start=(row == 0), stop=False,
                                      skip_group_check=True)
                            last = pe.matmul(banks[:, g + i, 0:NB], lo[:, k, :], rows[:, 0:NB], start=False,
                                             stop=(row == CMP_LEN - 1), skip_group_check=True)
                    else:
                        hi = w_hi[:, slot, :].rearrange("p (k c) -> p k c", k=2)
                        lo = w_lo[:, slot, :].rearrange("p (k c) -> p k c", k=2)
                        last_kt = 2 * cur.first.nsub - 1
                        for j in range(TPC):
                            if j == 3 and u == 0 and reduces:
                                pe.wait_ge(mod_ready, ready_after(reduces[-1]))
                            for k in range(2):
                                kt = 2 * u + k
                                pe.matmul(banks[:, g + j, :], hi[:, k, P * j:P * (j + 1)], operand[:, kt, :],
                                          start=(kt == 0), stop=False, skip_group_check=True)
                                last = pe.matmul(banks[:, g + j, 0:T], lo[:, k, P * j:P * (j + 1)],
                                                 operand[:, kt, 0:T], start=False, stop=(kt == last_kt),
                                                 skip_group_check=True)
                    last.then_inc(sub_done, 1)
                    u += 1

            def mix_pe():
                pe.wait_ge(mod_ready, ready_after(G1_0))
                pe.wait_ge(vread, 8)
                for ct in range(SGU_W // P):
                    if ct >= 4:
                        pe.wait_ge(sv_ready, ct - 3)
                    for n in range(2):
                        if ct == 0:
                            pe.wait_ge(wsn, n + 1)
                        last = pe.matmul(banks[:, ct % 4, P * n:P * (n + 1)], sv[:, ct, P * n:P * (n + 1)],
                                         w_sn[:, n, ct // 2, :], start=True, stop=True, skip_group_check=True)
                    last.then_inc(mixed, 1)
                pe.wait_ge(sv_ready, SGU_W // P)

            walk(pe, phases, step)


def stream_pieces(a):
    def cut(w):
        n = w.shape[1] // COLS
        k = w.shape[0] // (KPP * P)
        return w.reshape(k, KPP, P, n, COLS).transpose(3, 0, 2, 1, 4).reshape(n, k, P, PIECE)

    mod = {"mod0": a["mod_w"][0], "mod1": a["mod_w"][1], "kv": a["kv_mod_w"]}
    out = np.zeros((TOTAL["G"], P, PIECE), np.float32)
    cache = {}

    def weights(ch):
        s, i = ch.source, ch.loc
        if s not in cache:
            cache.clear()
            if s[0] == "sgu_v":
                cache[s] = cut(a["sgu_w_in"][0][:, SGU_W:])
            elif s[0] == "sgu_u":
                cache[s] = cut(a["sgu_w_in"][0][:, D * s[1]:D * (s[1] + 1)])
            elif s[0] == "sgu_out":
                cache[s] = cut(a["sgu_w_out"][0][D * s[1]:D * (s[1] + 1)])
            elif s[0] == "up":
                w = a["ffn_w_up"][s[1]]
                c0 = D * s[2]
                c1 = min(c0 + D, D_FF)
                both = [cut(w[:, c0:c1]), cut(w[:, D_FF + c0:D_FF + c1])]
                cache[s] = np.stack(both, 1)
            elif s[0] == "down":
                cache[s] = cut(a["ffn_w_down"][s[1]][D * s[2]:min(D * (s[2] + 1), D_FF)])
            elif s[0] == "kv":
                cache[s] = cut(a["w_kv"])
            elif s[0] == "q":
                cache[s] = cut(a["nsa_w_in"][0][:, :D])
            elif s[0] == "wo":
                cache[s] = cut(a["nsa_w_o"][0])
            elif s[0] == "cmp":
                cache[s] = a["cmp_w1"].reshape(2, 2, 16, P, HD).transpose(0, 1, 3, 2, 4).reshape(1, 4, P, PIECE)
            elif s[0] == "gate":
                g = a["nsa_w_in"][0][:, D:].reshape(KT, P, NGATE).transpose(1, 0, 2).reshape(P, KT * NGATE)
                cache[s] = np.zeros((1, 1, P, PIECE), np.float32)
                cache[s][0, 0, :, :KT * NGATE] = g
        w = cache[s]
        if ch.kind in ("ua", "uv"):
            return w[i, 0 if ch.kind == "ua" else 1]
        if ch.kind in ("kvf", "kvt"):
            return w[ch.loc]
        return w[i]

    for _, chunks in PHASES:
        for ch in chunks:
            g, m, q = ch.n["G"], ch.n["M"], 0
            w = weights(ch) if ch.source else None
            for kind in ch.kinds_of:
                if kind == "m":
                    name, block = MODS[m // KT]
                    out[g] = mod[name][P * (m % KT):P * (m % KT + 1), D * block:D * (block + 1)]
                    m += 1
                else:
                    out[g] = w[q]
                    q += 1
                g += 1
    return out.reshape(TOTAL["G"] * P, PIECE)


def small_table(a):
    def tall(v):
        return np.ascontiguousarray(v.reshape(-1, P).T)

    modb = {"mod0": a["mod_b"][0], "mod1": a["mod_b"][1], "kv": a["kv_mod_b"]}
    parts = [tall(a["c"][0])]
    parts += [tall(modb[n][D * b:D * (b + 1)]) for n, b in MODS]
    parts += [tall(a["norm_gain"].reshape(4 * D)), tall(a["kv_gain"]), tall(a["sgu_v_gain"][0])]
    parts += [tall(a["ffn_conv_w"].reshape(-1)), tall(a["ffn_conv_b"].reshape(-1))]
    parts += [a["k_gain"].T, a["nsa_q_gain"].T]
    parts += [a["cmp_pos"].reshape(2 * CMP_LEN, HD).T]
    parts += [a["cmp_w2"][0], a["cmp_w2"][1]]
    out = np.ascontiguousarray(np.concatenate(parts, 1))
    assert out.shape == (P, N_SMALL), out.shape
    return out


def position_table():
    out = np.zeros((P, N_POS), np.float32)
    for qb in range(2):
        t = qb * P + np.arange(P)[:, None]
        d = t - (np.arange(NCMP) * CMP_STRIDE + CMP_LEN - 1)[None, :]
        out[:, DW * qb:DW * qb + NCMP] = np.where(d >= 0, d, BIG)
        d = t - np.arange(T)[None, :]
        out[:, DW * qb + 16:DW * (qb + 1)] = np.where(d >= 0, d, BIG)
        out[:, 2 * DW + qb] = t[:, 0] >= CMP_LEN - 1
    return out


def kernel(**inputs):
    import concourse.bacc as bacc
    from concourse.bass_utils import run_bass_kernel_spmd

    a = {k: np.asarray(v) for k, v in inputs.items()}
    arrays = {
        "in_stream": stream_pieces(a),
        "in_small": small_table(a),
        "in_x": np.ascontiguousarray(a["x"][0].T.reshape(KT, P, T).transpose(1, 0, 2).reshape(P, KT * T)),
        "in_w_s": np.ascontiguousarray(a["sgu_w_s"][0].transpose(2, 0, 1).reshape(P, SGU_G * P)),
        "in_b_s": np.ascontiguousarray(np.broadcast_to(a["sgu_b_s"][0].reshape(1, SGU_G * P), (P, SGU_G * P))),
        "in_pos": position_table(),
    }
    nc = bacc.Bacc("TRN2", target_bir_lowering=False, num_devices=1)
    io = {n[3:]: nc.dram_tensor(n, v.shape, F32, kind="ExternalInput").ap() for n, v in arrays.items()}
    io["out"] = nc.dram_tensor("out_x", (P, KT * T), F32, kind="ExternalOutput").ap()
    build(nc, io)
    r = run_bass_kernel_spmd(nc, [arrays], core_ids=[0])
    out = np.asarray(r.results[0]["out_x"])
    return np.ascontiguousarray(out.reshape(P, KT, T).transpose(2, 1, 0).reshape(1, T, D))
```

```python
from contextlib import ExitStack

import numpy as np

import concourse.bass as bass
from concourse import mybir

P = 128
D = 2048
T = 256
KT = D // P
EPS = 1e-6
SGU_W = 2 * D
SGU_G = 16
D_FF = 11 * D // 4
FT = D_FF // P
NH, NKV, HD = 16, 4, 128
GRP = NH // NKV
CMP_LEN, CMP_STRIDE = 32, 16
NCMP = T // CMP_STRIDE - 1
NB = NKV * NCMP
NGATE = 3 * NH
BIG = 1e30

COLS = 512
TPC = COLS // P
KPP = 4
PIECE = KPP * COLS
SUB = PIECE // 2
RAW_SLOTS = 4
SPLIT_SLOTS = 4
HILO = 2 * T

F32, F32R = mybir.dt.float32, mybir.dt.float32r
ALU, ACT, AX = mybir.AluOpType, mybir.ActivationFunctionType, mybir.AxisListType

MODS = [("mod0", 0), ("mod0", 1), ("mod0", 2), ("mod0", 3), ("mod0", 4), ("mod0", 5), ("kv", 0), ("kv", 1),
        ("mod1", 0), ("mod1", 1), ("mod1", 2), ("mod1", 3), ("mod1", 4), ("mod1", 5)]
SH1_0, SC1_0, G1_0, SH2_0, SC2_0, G2_0, SH_KV, SC_KV, SH1_1, SC1_1, G1_1, SH2_1, SC2_1, G2_1 = range(14)
GAIN_OF = {SC1_0: 0, SC2_0: 1, SC_KV: 4, SC1_1: 2, SC2_1: 3}

C_MODB = 0
C_GAIN = C_MODB + len(MODS) * KT
C_VGAIN = C_GAIN + 5 * KT
C_CONVW = C_VGAIN + SGU_W // P
C_CONVB = C_CONVW + 2 * 3 * 2 * FT
C_KG = C_CONVB + 2 * 2 * FT
C_QG = C_KG + 3
C_POS = C_QG + 1
C_W2 = C_POS + 2 * CMP_LEN
N_SMALL = C_W2 + 2 * HD

DW = 16 + T
N_POS = 2 * DW + 2

PAT = {
    "P0": "ssssEsEsEsEs",
    "P2": "ssssEsEsmEsEsm",
    "P3": "ssssEsEsmEmsEsm",
    "Q0": "ssssEEsEsE",
    "Q1": "ssssEEsEsEm",
    "M4": "mmmm",
    "G1": "sE",
}


def ready_after(k):
    return sum(2 if j in GAIN_OF else 1 for j in range(k + 1))


class Chunk:

    def __init__(self, kind, loc, pattern, source):
        self.kind, self.loc, self.pattern, self.source = kind, loc, pattern, source
        self.tokens = PAT[pattern]
        self.nsub = self.tokens.count("s")
        self.n = {}


def is_looped(name, chunks):
    return len(chunks) >= 6 and name != "kv"


def plan():
    phases = []

    def add(name, kinds, count, pattern, source):
        phases.append((name, [Chunk(kinds[i % len(kinds)], i // len(kinds), pattern, source)
                              for i in range(count)]))

    add("mod", ["mod"], 8, "M4", None)
    add("sgu_v", ["v"], 8, "P2", ("sgu_v", 0))
    for half in range(2):
        add(f"sgu_u{half}", ["u"], 4, "P3", ("sgu_u", half))
        add(f"sgu_o{half}", ["dn"], 4, "P3", ("sgu_out", half))
    for layer in range(2):
        if layer == 1:
            phases.append(("kv", [Chunk(k, j, p, ("kv", j)) for k, j, p in (
                ("kvf", 0, "P3"), ("kvf", 1, "P3"), ("kvf", 2, "P3"), ("kvt", 3, "P3"), ("kvf", 4, "P2"),
                ("kvt", 5, "P2"))]))
            phases.append(("cmp", [Chunk("cmp", 0, "P0", ("cmp", 0))]))
            add("q", ["q"], 4, "P3", ("q", 0))
            phases.append(("gate", [Chunk("gate", 0, "G1", ("gate", 0))]))
            add("wo", ["dn"], 4, "P3", ("wo", 0))
        for part, (ups, up_pat, dn_pat) in enumerate(
                ((4, "P2", "P3"), (4, "P2", "P3"), (3, "P2", "Q1")) if layer == 0 else
                ((4, "P2", "P0"), (4, "P0", "P0"), (3, "P0", "Q0"))):
            add(f"up{layer}{part}", ["ua", "uv"], 2 * ups, up_pat, ("up", layer, part))
            add(f"dn{layer}{part}", ["dn"], 4, dn_pat, ("down", layer, part))
    count = dict(c=0, G=0, S=0, M=0, zlo=0, zsum=0, tap2=0, tap1=0, conv=0, gated=0, prod=0, ahi=0, alo=0, xup=0,
                 vread=0, moved=0)
    every, mod_end = [], []
    for name, chunks in phases:
        for ch in chunks:
            ch.in_looped = is_looped(name, chunks)
            ch.n = dict(count)
            ch.piece_of, ch.kinds_of = [], []
            halves = 0
            for tok in ch.tokens:
                if tok == "m" or (tok == "s" and halves % 2 == 0):
                    ch.kinds_of.append("m" if tok == "m" else "w")
                halves += tok == "s"
                if tok != "E":
                    ch.piece_of.append(len(ch.kinds_of) - 1)
                else:
                    ch.piece_of.append(None)
            count["G"] += len(ch.kinds_of)
            pieces = [i for i, k in enumerate(ch.kinds_of) if k == "m"]
            if pieces and ch.in_looped:
                count["moved"] += 1
            for i, off in enumerate(pieces):
                if (count["M"] + i + 1) % KT == 0:
                    mod_end.append({"piece": ch.n["G"] + off, "moved": count["moved"]})
            count["M"] += len(pieces)
            count["S"] += ch.nsub
            k = ch.kind
            if k != "mod":
                count["c"] += 1
            if k in ("ua", "uv", "u", "kvf", "q", "cmp"):
                count["zlo"] += 1
                count["zsum"] += 1
            if k in ("ua", "uv"):
                count["tap2"] += 1
                count["tap1"] += 1
                count["conv"] += 1
            if k in ("ua", "u"):
                count["gated"] += 1
            if k in ("uv", "u"):
                count["prod"] += 1
                count["ahi"] += 1
                count["alo"] += 1
            if k == "dn":
                count["xup"] += 1
            if k in ("v", "kvt", "gate"):
                count["vread"] += 1
            if k != "mod":
                every.append(ch)
    assert count["M"] == len(MODS) * KT
    return phases, every, count, mod_end


def free_rule(ch):
    if ch.kind in ("v", "kvt", "gate"):
        return "vread", ch.n["vread"] + 1
    if ch.kind == "dn":
        return "xlow", ch.n["xup"] + 1
    return "zsum", ch.n["zsum"] + 1


class At:

    def __init__(self, first, second=None, it=None, back=0):
        self.first, self.second, self.it, self.back = first, second, it, back

    def val(self, f):
        a = f(self.first)
        if self.second is None:
            return a
        step = f(self.second) - a
        return a - step * self.back + self.it * step if step else a

    def static(self, f):
        assert self.second is None or f(self.first) == f(self.second)
        return f(self.first)


def walk(eng, phases, step):
    prev = None
    for name, chunks in phases:
        body = 2 if len(chunks) > 1 else 1
        looped = is_looped(name, chunks)
        straight = chunks[:body] if looped else chunks
        for i, ch in enumerate(straight):
            step(name, At(ch), At(prev) if prev else None, i == 0)
            prev = ch
        if looped:
            with eng.Fori(1, len(chunks) // body) as it:
                for b in range(body):
                    cur = At(chunks[b], chunks[b + body], it)
                    before = At(chunks[b - 1], chunks[b - 1 + body], it, 0) if b else \
                        At(chunks[body - 1], chunks[2 * body - 1], it, 1)
                    step(name, cur, before, False)
            prev = chunks[-1]


PHASES, EVERY, TOTAL, MOD_END = plan()
BY_NAME = dict(PHASES)
ORDER = {ch.n["c"]: ch for ch in EVERY}


def build(nc, io, stop=None):
    phases = PHASES
    if stop is not None:
        names = [n for n, _ in PHASES]
        phases = PHASES[:names.index(stop)]
    n_pieces = TOTAL["G"] if stop is None else BY_NAME[stop][0].n["G"]
    slopes = [2.0 ** (-8.0 * (h + 1) / NH) for h in range(NH)]
    ctx = ExitStack()
    with ctx:
        def sb(name, shape, dt=F32):
            return ctx.enter_context(nc.sbuf_tensor(name, shape, dt))

        with nc.sbuf_tensor("attn_area", [P, KT * HILO], F32) as attn_area:
            pass
        h_op = sb("h_op", [P, KT, HILO], F32R)
        with nc.sbuf_tensor("mix_area", [P, KT * HILO], F32) as mix_area:
            pass
        act_op = sb("act_op", [P, KT, HILO], F32R)
        x = sb("x_res", [P, KT, T])
        raw = sb("raw", [P, RAW_SLOTS, PIECE])
        w_hi = sb("w_hi", [P, SPLIT_SLOTS, SUB], F32R)
        w_lo = sb("w_lo", [P, SPLIT_SLOTS, SUB], F32R)
        scratch = sb("scratch", [P, 32 * T])
        c_all = sb("c_all", [P, D])
        mod_sums = sb("mod_sums", [P, len(MODS) * KT])
        mod_col = sb("mod_col", [P, 4])
        small = sb("small", [P, N_SMALL])
        zpad = sb("zpad", [P, TPC, T + 2])
        temp = sb("temp", [P, 2, TPC * T])
        rstd = sb("rstd", [P, T])
        kcmp = sb("kcmp", [P, NB])
        vcmp = sb("vcmp", [16, NKV * HD])
        gates = sb("gates", [P, 2, NGATE])
        cmp_g = sb("cmp_g", [P, 2 * NB])
        ones = sb("ones", [P, P])
        ident = sb("ident", [P, P])
        vstat = sb("vstat", [P, 24])
        pick = sb("pick", [P, 2 * NH - 1])
        eps = sb("eps", [P, 1])
        banks = ctx.enter_context(nc.psum_tensor("banks", [P, 8, 512], F32))

        modv = mod_sums[:, :].rearrange("p (m k) -> p m k", k=KT)
        y, gt = temp[:, 0, :], temp[:, 1, :]
        y4 = y.rearrange("p (j t) -> p j t", j=TPC)
        gt4 = gt.rearrange("p (j t) -> p j t", j=TPC)
        sv = scratch[:, :].rearrange("p (c t) -> p c t", t=T)
        w_sT = mix_area[:, 0:2048].rearrange("p (g t) -> p g t", g=SGU_G)
        w_sn = mix_area[:, 2048:6144].rearrange("p (n g t) -> p n g t", n=2, g=SGU_G)
        b_sb = mix_area[:, 6144:8192].rearrange("p (g t) -> p g t", g=SGU_G)
        squares = mix_area[:, 0:6144]
        kc0, vc0 = scratch[:, 0:1024], scratch[:, 1024:2048]
        q_raw = scratch[:, 0:4096]
        k_slc, k_win = scratch[:, 4096:5120], scratch[:, 5120:6144]
        v_slc, v_win = scratch[:, 6144:7168], scratch[:, 7168:8192]
        blocks = temp[:, :, :].rearrange("p a b -> p (a b)")[:, 0:CMP_LEN * NB]
        blk_op = act_op[:, :, :].rearrange("p k t -> p (k t)")

        sems = {}

        def sem(name):
            if name not in sems:
                sems[name] = ctx.enter_context(nc.semaphore(name))
            return sems[name]

        raw_loaded = [sem(f"raw_loaded{s}") for s in range(RAW_SLOTS)]
        hi_ready = sem("hi_ready")
        stream = sem("stream")
        sub_done = sem("sub_done")
        small_loaded, x_loaded, mix_loaded, pos_loaded = (
            sem("small_loaded"), sem("x_loaded"), sem("mix_loaded"), sem("pos_loaded"))
        zeroed, consts_set, c_ready = sem("zeroed"), sem("consts_set"), sem("c_ready")
        zlo, zsum, tap2, tap1, conv = sem("zlo"), sem("zsum"), sem("tap2"), sem("tap1"), sem("conv")
        gated, prod, ahi, alo, xup, xlow, vread = (
            sem("gated"), sem("prod"), sem("ahi"), sem("alo"), sem("xup"), sem("xlow"), sem("vread"))
        read_sems = {"vread": vread, "zsum": zsum, "xlow": xlow}
        mod_ready, mod_moved = sem("mod_ready"), sem("mod_moved")
        squared, summed, rms_ok, rstd_ok, xsq, xhalf, xquarter, xsum = (
            sem("squared"), sem("summed"), sem("rms_ok"), sem("rstd_ok"), sem("xsq"), sem("xhalf"),
            sem("xquarter"), sem("xsum"))
        normed, affine, h_hi, h_ready = sem("normed"), sem("affine"), sem("h_hi"), sem("h_ready")
        vsq, vred, vmean, vrec, vrstd = sem("vsq"), sem("vred"), sem("vmean"), sem("vrec"), sem("vrstd")
        masked, wsn, mixed, sv_ready = sem("masked"), sem("wsn"), sem("mixed"), sem("sv_ready")
        blk, blk_hi, blk_lo, cmp_gelu = sem("blk"), sem("blk_hi"), sem("blk_lo"), sem("cmp_gelu")
        at_sqk, at_sqq, at_olo = sem("at_sqk"), sem("at_sqq"), sem("at_olo")
        stored = sem("stored")

        def vec(slice_, kt):
            return modv[:, slice_, kt:kt + 1] if isinstance(kt, int) else modv[:, slice_, bass.ds(kt, 1)]

        def col(c0, i):
            return small[:, c0 + i:c0 + i + 1] if isinstance(i, int) else small[:, bass.ds(i + c0, 1)]

        H_OF = {"sgu_v": (SH1_0, SC1_0, True), "up00": (SH2_0, SC2_0, True), "kv": (SH_KV, SC_KV, True),
                "q": (SH1_1, SC1_1, False), "up10": (SH2_1, SC2_1, True)}
        H_ORDER = [n for n, _ in PHASES if n in H_OF]
        STAT_ORDER = [n for n in H_ORDER if H_OF[n][2]]
        FINISHED = {"sgu_v": [SH1_0, SC1_0], "sgu_o0": [G1_0], "sgu_o1": [SH2_0], "up00": [SC2_0, G2_0],
                    "up01": [SH_KV], "up02": [SC_KV], "kv": [SH1_1, SC1_1], "wo": [G1_1, SH2_1], "up10": [SC2_1],
                    "dn10": [G2_1]}
        GATE_OF = {"sgu_o0": G1_0, "sgu_o1": G1_0, "dn00": G2_0, "dn01": G2_0, "dn02": G2_0, "wo": G1_1,
                   "dn10": G2_1, "dn11": G2_1, "dn12": G2_1}
        PHASE_OF = {}
        for pname, chunks in PHASES:
            for ch in chunks:
                PHASE_OF[id(ch)] = pname

        X_FROM = {"up00": "sgu_o1", "kv": "dn02", "up10": "wo"}

        def h_index(name):
            return H_ORDER.index(name)

        def free_wait(eng, cur):
            if cur.first.n["c"] < 2 and cur.second is None:
                return
            if cur.second is None:
                which, value = free_rule(ORDER[cur.first.n["c"] - 2])
            else:
                which, value = free_rule(cur.first)
                step = free_rule(cur.second)[1] - value
                value = value - step + cur.it * step
            eng.wait_ge(read_sems[which], value)

        def stages_at(name, cur, first, e):
            if first and (name in H_OF or name in ("wo", "sgu_u0")):
                return range(4) if e == 0 else ()
            return range(4) if cur.first.kind == "gate" else (e,)

        def done_wait(eng, prev):
            eng.wait_ge(sub_done, prev.val(lambda c: c.n["S"] + c.nsub))

        def group(prev):
            return 4 * (prev.static(lambda c: c.n["c"] % 2))

        UNITS = [(h, qb) for h in range(NH) for qb in range(2)]
        area = attn_area
        pos = area[:, 7168:7168 + N_POS]
        r_k = area[0:16, 3584:3584 + T]
        r_q = area[0:16, 3840:3840 + T]
        r_c = area[:, 4096:4096 + NB]
        sq_c = area[:, 4160:4160 + NB]
        q_scale = area[:, 4224:4256]
        neg_max = area[:, 6400:6400 + 96]
        denom = area[:, 6500:6500 + 96]
        coef = area[:, 6600:6600 + 96]
        k_gains = vstat[:, 0:3]

        def scores(i):
            return area[:, 528 * (i % 4):528 * (i % 4) + 528]

        def both(ap, n):
            return ap.rearrange("p (b k) -> p b k", b=2)[:, :, 0:n]

        def probs_t(i):
            o = 2112 + 640 * (i % 2)
            return area[:, o:o + 640]

        def attention_act(act):
            act.dma_start(pos, io["pos"]).then_inc(pos_loaded, 16)
            act.wait_ge(sem("at_stat"), 1)
            act.activation(r_k, banks[0:16, 0, 0:T], ACT.Sqrt, scale=1.0 / HD, bias=eps[0:16, :]) \
                .then_inc(sem("at_rt"), 1)
            act.wait_ge(sem("at_kc"), 1)
            act.activation(sq_c, kcmp[:, :], ACT.Square).then_inc(sem("at_sqc"), 1)
            act.wait_ge(sem("at_stat"), 2)
            act.activation(r_c, banks[:, 3, 0:NB], ACT.Sqrt, scale=1.0 / HD, bias=eps[:, :]) \
                .then_inc(sem("at_rt"), 1)
            act.wait_ge(sem("at_stat"), 3)
            act.activation(r_q, banks[0:16, 1, 0:T], ACT.Sqrt, scale=1.0 / HD, bias=eps[0:16, :]) \
                .then_inc(sem("at_rt"), 1)
            for i in range(len(UNITS) + 3):
                if i < len(UNITS):
                    h, qb = UNITS[i]
                    keys = P * (qb + 1)
                    act.wait_ge(sem("at_qk"), i + 1)
                    act.wait_ge(sem("at_kn"), 3)
                    if i >= 4:
                        act.wait_ge(sem("at_tr"), i - 3)
                    r = q_scale[:, 16 * qb + h:16 * qb + h + 1]
                    act.activation(both(scores(i)[:, 16:528], keys), both(banks[:, i % 2, :], keys), ACT.Copy,
                                   scale=r)
                    act.activation(scores(i)[:, 0:NCMP], banks[:, 2 + i % 2, 0:NCMP], ACT.Copy, scale=r) \
                        .then_inc(sem("at_sc"), 1)
                if 1 <= i <= len(UNITS):
                    j = i - 1
                    keys = P * (UNITS[j][1] + 1)
                    act.wait_ge(sem("at_mx"), j + 1)
                    for b, (o, n) in enumerate(((0, NCMP), (16, keys), (16 + T, keys))):
                        part = scores(j)[:, o:o + n]
                        last = act.activation(part, part, ACT.Exp, bias=neg_max[:, 3 * j + b:3 * j + b + 1],
                                              accum_out=denom[:, 3 * j + b:3 * j + b + 1])
                    last.then_inc(sem("at_ex"), 1)
                if i >= 3:
                    j = i - 3
                    h, qb = UNITS[j]
                    act.wait_ge(sem("at_pv"), j + 1)
                    act.activation(act_op[:, h, P * qb:P * (qb + 1)], banks[:, 6 + j % 2, 0:P], ACT.Copy) \
                        .then_inc(sem("at_ohi"), 1)

        def attention_dve(dve):
            dve.wait_ge(vread, BY_NAME["gate"][0].n["vread"] + 1)
            dve.wait_ge(pos_loaded, 16)
            for qb in range(2):
                dve.tensor_scalar(gates[:, qb, 0:NH], gates[:, qb, 0:NH],
                                  pos[:, 2 * DW + qb:2 * DW + qb + 1], None, ALU.mult)
            dve.tensor_scalar(k_gains, small[:, C_KG:C_KG + 3], small[:, C_QG:C_QG + 1], None, ALU.mult) \
                .then_inc(sem("at_gains"), 1)
            dve.wait_ge(sem("at_cmp"), 1)
            dve.tensor_copy(kcmp[:, :], banks[:, 5, 0:NB])
            dve.tensor_copy(vcmp[0:NCMP, :], banks[0:NCMP, 6, :]).then_inc(sem("at_kc"), 1)
            dve.wait_ge(sem("at_rt"), 1)
            dve.reciprocal(r_k, r_k).then_inc(sem("at_rec"), 1)
            dve.wait_ge(sem("at_gains"), 1)
            dve.wait_ge(sem("at_rt"), 2)
            dve.reciprocal(r_c, r_c).then_inc(sem("at_rec"), 1)
            dve.wait_ge(sem("at_rec"), 2)
            dve.scalar_tensor_tensor(out=kcmp[:, :], in0=kcmp[:, :], scalar=k_gains[:, 0:1], in1=r_c,
                                     op0=ALU.mult, op1=ALU.mult).then_inc(sem("at_kn"), 1)
            dve.wait_ge(sem("at_rt"), 3)
            dve.reciprocal(r_q, r_q).then_inc(sem("at_inv_q"), 1)
            dve.wait_ge(sem("at_inv_q"), 1)
            dve.tensor_scalar(r_q, r_q, float(HD) ** -0.5, None, ALU.mult).then_inc(sem("at_rec"), 1)
            dve.wait_ge(sem("at_kb"), 1)
            for b, k in ((1, k_slc), (2, k_win)):
                last = dve.scalar_tensor_tensor(
                    out=k, in0=k, scalar=k_gains[:, b:b + 1],
                    in1=banks[:, 2 + 2 * b:4 + 2 * b, :].rearrange("p a t -> p (a t)"), op0=ALU.mult,
                    op1=ALU.mult)
            last.then_inc(sem("at_kn"), 1)
            dve.wait_ge(sem("at_qt"), 1)
            dve.tensor_copy(q_scale, banks[:, 2, 0:32]).then_inc(sem("at_kn"), 1)
            for i in range(len(UNITS) + 3):
                if i < len(UNITS):
                    h, qb = UNITS[i]
                    keys = P * (qb + 1)
                    dist = pos[:, DW * qb:DW * (qb + 1)]
                    main, short = both(scores(i)[:, 16:528], keys), scores(i)[:, 0:NCMP]
                    dve.wait_ge(sem("at_sc"), i + 1)
                    dve.scalar_tensor_tensor(
                        out=main, in0=dist[:, 16:16 + keys].rearrange("p (o k) -> p o k", o=1)
                        .to_broadcast([P, 2, keys]), scalar=-slopes[h], in1=main, op0=ALU.mult, op1=ALU.add)
                    dve.scalar_tensor_tensor(out=short, in0=dist[:, 0:NCMP], scalar=-slopes[h], in1=short,
                                             op0=ALU.mult, op1=ALU.add).then_inc(sem("at_bias"), 1)
                    dve.wait_ge(sem("at_bias"), i + 1)
                    dve.tensor_reduce(neg_max[:, 3 * i + 1:3 * i + 3], main, AX.X, ALU.max, negate=True)
                    dve.tensor_reduce(neg_max[:, 3 * i:3 * i + 1], short, AX.X, ALU.max, negate=True) \
                        .then_inc(sem("at_mx"), 1)
                if 1 <= i <= len(UNITS):
                    j = i - 1
                    h, qb = UNITS[j]
                    d, f = denom[:, 3 * j:3 * j + 3], coef[:, 3 * j:3 * j + 3]
                    dve.wait_ge(sem("at_ex"), j + 1)
                    dve.tensor_scalar(d, d, 1e-30, None, ALU.max).then_inc(sem("at_den"), 1)
                    dve.wait_ge(sem("at_den"), j + 1)
                    dve.reciprocal(f, d).then_inc(sem("at_inv"), 1)
                    dve.wait_ge(sem("at_inv"), j + 1)
                    dve.tensor_tensor(f, f, gates[:, qb, :].rearrange("p (b h) -> p h b", h=NH)[:, h, :],
                                      ALU.mult).then_inc(sem("at_coef"), 1)
                if 2 <= i <= len(UNITS) + 1:
                    j = i - 2
                    keys = P * (UNITS[j][1] + 1)
                    dve.wait_ge(sem("at_tr"), j + 1)
                    if j >= 2:
                        dve.wait_ge(sem("at_pv"), j - 1)
                    dve.tensor_copy(both(probs_t(j)[:, 0:512], keys), both(banks[:, 4 + j % 2, :], keys))
                    dve.tensor_copy(probs_t(j)[0:NCMP, 512:640], banks[0:NCMP, 6 + j % 2, P:2 * P]) \
                        .then_inc(sem("at_pt"), 1)
                if i >= 3:
                    j = i - 3
                    h, qb = UNITS[j]
                    dve.wait_ge(sem("at_ohi"), j + 1)
                    dve.tensor_tensor(act_op[:, h, T + P * qb:T + P * (qb + 1)], banks[:, 6 + j % 2, 0:P],
                                      act_op[:, h, P * qb:P * (qb + 1)].bitcast(F32), ALU.subtract) \
                        .then_inc(sem("at_olo"), 1)

        def attention_pool(pool):
            for j in range(len(UNITS)):
                keys = P * (UNITS[j][1] + 1)
                pool.wait_ge(sem("at_coef"), j + 1)
                for b, (o, n) in enumerate(((0, NCMP), (16, keys), (16 + T, keys))):
                    part = scores(j)[:, o:o + n]
                    last = pool.tensor_scalar(part, part, coef[:, 3 * j + b:3 * j + b + 1], None, ALU.mult)
                last.then_inc(sem("at_scaled"), 1)

        def attention_pe(pe):
            gate = BY_NAME["gate"][0]
            pe.wait_ge(vread, gate.n["vread"] + 1)
            pe.wait_ge(sem("ident_set"), 1)
            pe.wait_ge(cmp_gelu, 1)
            pe.matmul(banks[:, 5, 0:NB], small[:, C_W2:C_W2 + HD], cmp_g[:, 0:NB], start=True, stop=True,
                      skip_group_check=True)
            for g in range(NKV):
                last = pe.matmul(banks[0:NCMP, 6, HD * g:HD * (g + 1)],
                                 cmp_g[:, NB + NCMP * g:NB + NCMP * (g + 1)], small[:, C_W2 + HD:C_W2 + 2 * HD],
                                 start=True, stop=True, skip_group_check=True)
            last.then_inc(sem("at_cmp"), 1)
            pe.wait_ge(at_sqk, 1)
            for r in range(2 * NKV):
                last = pe.matmul(banks[0:16, 0, 0:T], pick[:, NH - 1 - r:2 * NH - 1 - r],
                                 squares[:, 4096 + T * r:4096 + T * (r + 1)], start=(r == 0),
                                 stop=(r == 2 * NKV - 1))
            last.then_inc(sem("at_stat"), 1)
            pe.wait_ge(sem("at_sqc"), 1)
            pe.matmul(banks[:, 3, 0:NB], ones[:, :], sq_c, start=True, stop=True).then_inc(sem("at_stat"), 1)
            for h in range(NH):
                if h % TPC == 0:
                    pe.wait_ge(at_sqq, h // TPC + 1)
                last = pe.matmul(banks[0:16, 1, 0:T], pick[:, NH - 1 - h:2 * NH - 1 - h],
                                 squares[:, T * h:T * (h + 1)], start=(h == 0), stop=(h == NH - 1))
            last.then_inc(sem("at_stat"), 1)
            pe.wait_ge(sem("at_rec"), 1)
            for r in range(2 * NKV):
                last = pe.matmul(banks[:, 4 + r // 2, T * (r % 2):T * (r % 2 + 1)],
                                 ident[0:16, r:r + 1].to_broadcast([16, P]), r_k, start=True, stop=True,
                                 skip_group_check=True)
            last.then_inc(sem("at_kb"), 1)
            pe.wait_ge(sem("at_rec"), 3)
            for qb in range(2):
                last = pe.transpose(banks[:, 2, 16 * qb:16 * (qb + 1)], r_q[:, P * qb:P * (qb + 1)],
                                    ident[0:16, 0:16])
            last.then_inc(sem("at_qt"), 1)
            pe.wait_ge(sem("at_kn"), 3)

            def score(i):
                h, qb = UNITS[i]
                g, keys = h // GRP, P * (qb + 1)
                if i >= 2:
                    pe.wait_ge(sem("at_sc"), i - 1)
                query = q_raw[:, T * h + P * qb:T * h + P * (qb + 1)]
                pe.matmul(banks[:, i % 2, 0:keys], query, k_slc[:, T * g:T * g + keys], start=True, stop=True,
                          skip_group_check=True)
                pe.matmul(banks[:, i % 2, T:T + keys], query, k_win[:, T * g:T * g + keys], start=True,
                          stop=True, skip_group_check=True)
                pe.matmul(banks[:, 2 + i % 2, 0:NCMP], query, kcmp[:, NCMP * g:NCMP * (g + 1)], start=True,
                          stop=True, skip_group_check=True).then_inc(sem("at_qk"), 1)

            score(0)
            for i in range(len(UNITS) + 3):
                if i + 1 < len(UNITS):
                    score(i + 1)
                if 2 <= i <= len(UNITS) + 1:
                    j = i - 2
                    qb = UNITS[j][1]
                    pe.wait_ge(sem("at_scaled"), j + 1)
                    if j >= 2:
                        pe.wait_ge(sem("at_pt"), j - 1)
                        pe.wait_ge(sem("at_olo"), j - 1)
                    for b in range(2):
                        for n in range(qb + 1):
                            o = T * b + P * n
                            pe.transpose(banks[:, 4 + j % 2, o:o + P], scores(j)[:, 16 + o:16 + o + P],
                                         ident[:, :])
                    pe.transpose(banks[0:NCMP, 6 + j % 2, P:2 * P], scores(j)[:, 0:NCMP], ident[:, :]) \
                        .then_inc(sem("at_tr"), 1)
                if i >= 3:
                    j = i - 3
                    h, qb = UNITS[j]
                    g = h // GRP
                    pe.wait_ge(sem("at_pt"), j + 1)
                    out = banks[:, 6 + j % 2, 0:P]
                    pt = probs_t(j)
                    for b, v in ((0, v_slc), (1, v_win)):
                        for n in range(qb + 1):
                            pe.matmul(out, v[:, 512 * n + HD * g:512 * n + HD * (g + 1)],
                                      pt[:, T * b + P * n:T * b + P * (n + 1)], start=(b == 0 and n == 0),
                                      stop=False, skip_group_check=True)
                    pe.matmul(out, vcmp[0:NCMP, HD * g:HD * (g + 1)], pt[0:NCMP, 512:640], start=False, stop=True,
                              skip_group_check=True).then_inc(sem("at_pv"), 1)

        def z_view(prev):
            kind = prev.first.kind
            if kind in ("ua", "uv"):
                return zpad[:, :, 2:T + 2]
            if kind == "u":
                return y4
            if kind == "q":
                o = TPC * T * BY_NAME["q"].index(prev.first)
                return q_raw[:, o:o + TPC * T].rearrange("p (j t) -> p j t", j=TPC)
            dst = {0: kc0, 1: vc0, 2: k_slc, 4: k_win}[prev.first.loc]
            return dst.rearrange("p (j t) -> p j t", j=4)

        def local(prev):
            phase = BY_NAME[PHASE_OF[id(prev.first)]]
            c0 = phase[0].n["c"]
            per = 2 if prev.first.kind in ("ua", "uv") else 1
            return prev.val(lambda c: (c.n["c"] - c0) // per)

        def act_tiles(prev):
            k = local(prev)
            return act_op[:, TPC * k:TPC * k + TPC, :] if isinstance(k, int) else \
                act_op[:, bass.ds(k * TPC, TPC), :]

        def v_tiles(prev, n):
            k = local(prev)
            rows = sv[:, 4 * k:4 * k + 4, :] if isinstance(k, int) else sv[:, bass.ds(k * 4, 4), :]
            return rows[:, :, P * n:P * (n + 1)]

        def x_tile(prev, j):
            k = local(prev)
            return x[:, TPC * k + j, :]

        def conv_col(prev, tap, j):
            name = PHASE_OF[id(prev.first)]
            layer, part = int(name[2]), int(name[3])
            k = local(prev)
            base = (C_CONVB + layer * 2 * FT) if tap is None else C_CONVW + (layer * 3 + tap) * 2 * FT
            base += (FT if prev.first.kind == "uv" else 0) + 16 * part + j
            return small[:, base + 4 * k:base + 4 * k + 1] if isinstance(k, int) else \
                small[:, bass.ds(k * 4 + base, 1)]

        def blk_view(i):
            return blk_op[:, i * CMP_LEN * 2 * NB:(i + 1) * CMP_LEN * 2 * NB].rearrange(
                "p (l n) -> p l n", l=CMP_LEN)

        def mix_dve(dve):
            dve.wait_ge(vsq, 16)
            dve.tensor_reduce(vstat[:, 16:18], vstat[:, 0:16].rearrange("p (n c) -> p n c", n=2), AX.X, ALU.add) \
                .then_inc(vred, 1)
            dve.wait_ge(vred, 1)
            dve.tensor_scalar(vstat[:, 20:22], vstat[:, 16:18], 1.0 / SGU_W, EPS, ALU.mult, ALU.add) \
                .then_inc(vmean, 1)
            dve.wait_ge(vmean, 1)
            dve.wait_ge(vrstd, 1)
            dve.reciprocal(vstat[:, 22:24], vstat[:, 18:20]).then_inc(vrec, 1)
            dve.wait_ge(vrec, 1)
            dve.wait_ge(masked, 1)
            for n in range(2):
                dve.tensor_scalar(w_sn[:, n, :, :], w_sT, vstat[:, 22 + n:23 + n], None, ALU.mult).then_inc(wsn, 1)
            dve.wait_ge(mix_loaded, 32)
            for ct in range(SGU_W // P):
                dve.wait_ge(mixed, ct + 1)
                dve.scalar_tensor_tensor(
                    out=sv[:, ct, :].rearrange("p (n t) -> p n t", n=2),
                    in0=banks[:, ct % 4, 0:T].rearrange("p (n t) -> p n t", n=2), scalar=col(C_VGAIN, ct),
                    in1=b_sb[:, ct // 2, :].rearrange("p (o t) -> p o t", o=1).to_broadcast([P, 2, P]),
                    op0=ALU.mult, op1=ALU.add).then_inc(sv_ready, 1)

        block = ctx.enter_context(nc.Block())

        @block.sync
        def _(sp):
            sp.dma_start(small[:, :], io["small"]).then_inc(small_loaded, 16)
            sp.dma_start(c_all[:, :], io["c"]).then_inc(sem("c_loaded"), 16)
            sp.dma_start(x[:, :, :], io["x"].rearrange("p (k t) -> p k t", t=T)).then_inc(x_loaded, 16)
            for s in range(RAW_SLOTS):
                sp.dma_start(raw[:, s, :], io["stream"][s * P:(s + 1) * P, :]).then_inc(raw_loaded[s], 16)
            sp.dma_start(w_sT, io["w_s"].rearrange("p (g t) -> p g t", g=SGU_G)).then_inc(mix_loaded, 16)
            sp.dma_start(b_sb, io["b_s"].rearrange("p (g t) -> p g t", g=SGU_G)).then_inc(mix_loaded, 16)
            full = n_pieces // RAW_SLOTS
            with sp.Fori(1, full) as i:
                for s in range(RAW_SLOTS):
                    sp.wait_ge(stream, i * (2 * RAW_SLOTS) + (2 * (s + 1) - 2 * RAW_SLOTS))
                    sp.dma_start(raw[:, s, :], io["stream"][bass.ds(i * (RAW_SLOTS * P) + s * P, P), :]) \
                        .then_inc(raw_loaded[s], 16)
            for g in range(full * RAW_SLOTS, n_pieces):
                sp.wait_ge(stream, 2 * (g - RAW_SLOTS + 1))
                sp.dma_start(raw[:, g % RAW_SLOTS, :], io["stream"][g * P:(g + 1) * P, :]) \
                    .then_inc(raw_loaded[g % RAW_SLOTS], 16)
            last = phases[-1][1]
            if last[0].kind == "dn" and len(last) == 4:
                for i, ch in enumerate(last):
                    sp.wait_ge(xlow, ch.n["xup"] + 1)
                    sp.dma_start(io["out"].rearrange("p (k t) -> p k t", t=T)[:, TPC * i:TPC * (i + 1), :],
                                 x[:, TPC * i:TPC * (i + 1), :]).then_inc(stored, 16)
                sp.wait_ge(stored, 64)

        @block.scalar
        def _(act):
            act.wait_ge(sem("c_loaded"), 16)
            act.activation(c_all[:, :], c_all[:, :], ACT.Silu).then_inc(c_ready, 1)

            def split_hi(cur, u, tok):
                off, chunk = cur.first.piece_of[tok], cur.first
                slot = cur.static(lambda c: (c.n["G"] + off) % RAW_SLOTS)
                out = cur.static(lambda c: (c.n["S"] + u) % SPLIT_SLOTS)
                act.wait_ge(raw_loaded[slot], cur.val(lambda c: 16 * ((c.n["G"] + off) // RAW_SLOTS + 1)))
                if cur.second is not None or chunk.n["S"] + u >= SPLIT_SLOTS:
                    act.wait_ge(sub_done, cur.val(lambda c: c.n["S"] + u - SPLIT_SLOTS + 1))
                n = KT * NGATE if chunk.kind == "gate" else SUB
                half = (u % 2) * SUB
                act.activation(w_hi[:, out, 0:n], raw[:, slot, half:half + n], ACT.Copy).then_inc(hi_ready, 1)

            def make_h(name):
                i = h_index(name)
                if H_OF[name][2]:
                    k = STAT_ORDER.index(name)
                    if k == 0:
                        act.wait_ge(x_loaded, 16)
                    else:
                        act.wait_ge(xlow, BY_NAME[X_FROM[name]][3].n["xup"] + 1)
                    act.wait_ge(xhalf, 3 * (k + 1))
                    act.activation(y, x[:, 3 * TPC:KT, :].rearrange("p k t -> p (k t)"), ACT.Square) \
                        .then_inc(squared, 1)
                    act.wait_ge(summed, k + 1)
                    act.wait_ge(consts_set, 1)
                    act.activation(rstd[:, :], banks[:, 0, 0:T], ACT.Sqrt, scale=1.0 / D, bias=eps[:, :]) \
                        .then_inc(rms_ok, 1)
                for q in range(4):
                    act.wait_ge(affine, 4 * i + q + 1)
                    act.activation(h_op[:, TPC * q:TPC * (q + 1), 0:T],
                                   temp[:, q % 2, :].rearrange("p (k t) -> p k t", t=T), ACT.Copy).then_inc(h_hi, 1)

            def evacuate(e, name, cur, prev, first):
                kind = prev.first.kind if prev else "mod"
                g = group(prev) if kind != "mod" else None
                if e == 0 and kind in ("ua", "uv", "u", "kvf", "q", "cmp"):
                    done_wait(act, prev)
                    if kind == "cmp":
                        out, src = cmp_g[:, :].rearrange("p (i n) -> p i n", i=2), banks[:, g:g + 2, NB:2 * NB]
                    else:
                        out, src = z_view(prev), banks[:, g:g + 4, T:HILO]
                    if kind in ("ua", "uv"):
                        act.wait_ge(zeroed, 1)
                        act.wait_ge(conv, prev.val(lambda c: c.n["conv"]))
                    if kind == "u":
                        act.wait_ge(alo, prev.val(lambda c: c.n["alo"]))
                    if kind == "q":
                        act.wait_ge(blk, 2)
                    act.activation(out, src, ACT.Copy).then_inc(zlo, 1)
                if e == 1 and kind in ("ua", "uv"):
                    act.wait_ge(zsum, prev.val(lambda c: c.n["zsum"] + 1))
                    act.wait_ge(alo, prev.val(lambda c: c.n["alo"]))
                    act.wait_ge(gated, prev.val(lambda c: c.n["gated"]))
                    for j in range(TPC):
                        act.activation(y4[:, j, :], zpad[:, j, 2:T + 2], ACT.Identity, bias=conv_col(prev, None, j),
                                       scale=conv_col(prev, 2, j)).then_inc(tap2, 1)
                if e == 2 and kind == "ua":
                    act.wait_ge(conv, prev.val(lambda c: c.n["conv"] + 1))
                    act.wait_ge(prod, prev.val(lambda c: c.n["prod"]))
                    act.activation(gt, y, ACT.Silu).then_inc(gated, 1)
                if e == 1 and kind == "u":
                    act.wait_ge(zsum, prev.val(lambda c: c.n["zsum"] + 1))
                    act.activation(gt, y, ACT.Gelu_apprx_tanh).then_inc(gated, 1)
                if e == 3 and kind in ("uv", "u"):
                    act.wait_ge(prod, prev.val(lambda c: c.n["prod"] + 1))
                    act.activation(act_tiles(prev)[:, :, 0:T], y4, ACT.Copy).then_inc(ahi, 1)
                if e == 1 and kind == "cmp":
                    act.wait_ge(zsum, prev.val(lambda c: c.n["zsum"] + 1))
                    act.activation(cmp_g[:, :], cmp_g[:, :], ACT.Gelu_apprx_tanh).then_inc(cmp_gelu, 1)
                if e == 2 and kind == "cmp":
                    act.activation(squares[:, 4096:6144], scratch[:, 4096:6144], ACT.Square).then_inc(at_sqk, 1)
                if e == 2 and kind == "q":
                    act.wait_ge(zsum, prev.val(lambda c: c.n["zsum"] + 1))
                    o = TPC * T * BY_NAME["q"].index(prev.first)
                    act.activation(squares[:, o:o + TPC * T], q_raw[:, o:o + TPC * T], ACT.Square) \
                        .then_inc(at_sqq, 1)
                if e == 0 and kind == "v":
                    done_wait(act, prev)
                    for n in range(2):
                        last = act.activation(v_tiles(prev, n), banks[:, g + n, :].rearrange("p (c t) -> p c t", t=P),
                                              ACT.Gelu_apprx_tanh)
                    last.then_inc(vread, 1)
                if e == 2 and kind == "v":
                    act.wait_ge(vread, prev.val(lambda c: c.n["vread"] + 1))
                    if prev.first.n["vread"] > 0 or prev.second is not None:
                        act.wait_ge(vsq, prev.val(lambda c: 2 * c.n["vread"]))
                    for n in range(2):
                        loc = prev.val(lambda c: c.n["c"] + 8 * n)
                        out = vstat[:, loc:loc + 1] if isinstance(loc, int) else vstat[:, bass.ds(loc, 1)]
                        act.activation(temp[:, n, 0:COLS].rearrange("p (c t) -> p c t", t=P), v_tiles(prev, n),
                                       ACT.Square, accum_out=out).then_inc(vsq, 1)
                if e == 0 and kind == "kvt":
                    done_wait(act, prev)
                    dst = v_slc if prev.first.loc == 3 else v_win
                    act.activation(dst.rearrange("p (n c) -> p n c", n=2), banks[:, g:g + 2, :], ACT.Copy) \
                        .then_inc(vread, 1)
                if e == 0 and kind == "gate":
                    done_wait(act, prev)
                    act.activation(gates[:, :, :], banks[:, g:g + 2, 0:NGATE], ACT.Sigmoid).then_inc(vread, 1)
                if e == 3 and name == "kv" and not first and cur.first.loc in (3, 4):
                    i = cur.first.loc - 3
                    act.wait_ge(blk, i + 1)
                    act.activation(blk_view(i)[:, :, 0:NB], blocks.rearrange("p (l n) -> p l n", l=CMP_LEN),
                                   ACT.Copy).then_inc(blk_hi, 1)
                if e == 3 and first and name == "sgu_u0":
                    act.wait_ge(vmean, 1)
                    act.activation(vstat[:, 18:20], vstat[:, 20:22], ACT.Sqrt).then_inc(vrstd, 1)
                if e == 3 and first and name == "wo":
                    attention_act(act)
                if e == 3 and first and name in H_OF:
                    make_h(name)

            def step(name, cur, prev, first):
                if cur.first.kind == "mod":
                    return
                u, e = 0, 0
                for tok, t in enumerate(cur.first.tokens):
                    if t == "s":
                        split_hi(cur, u, tok)
                        u += 1
                    elif t == "E":
                        for stage in stages_at(name, cur, first, e):
                            evacuate(stage, name, cur, prev, first)
                        e += 1

            walk(act, phases, step)

        @block.vector
        def _(dve):
            dve.memset(zpad[:, :, :], 0.0).then_inc(zeroed, 1)
            dve.memset(pick[:, :], 0.0).then_inc(sem("pick_zero"), 1)
            dve.wait_ge(sem("pick_zero"), 1)
            dve.memset(pick[:, NH - 1:NH], 1.0)
            dve.memset(eps[:, :], EPS)
            dve.memset(ones[:, :], 1.0).then_inc(consts_set, 1)

            def split_lo(cur, u, tok):
                off, chunk = cur.first.piece_of[tok], cur.first
                slot = cur.static(lambda c: (c.n["G"] + off) % RAW_SLOTS)
                out = cur.static(lambda c: (c.n["S"] + u) % SPLIT_SLOTS)
                dve.wait_ge(hi_ready, cur.val(lambda c: c.n["S"] + u + 1))
                n = KT * NGATE if chunk.kind == "gate" else SUB
                half = (u % 2) * SUB
                dve.tensor_tensor(w_lo[:, out, 0:n], raw[:, slot, half:half + n], w_hi[:, out, 0:n].bitcast(F32),
                                  ALU.subtract).then_inc(stream, 2 if chunk.kind == "gate" else 1)

            def mod_piece(cur, m, tok):
                off = cur.first.piece_of[tok]
                slot = cur.static(lambda c: (c.n["G"] + off) % RAW_SLOTS)
                dve.wait_ge(raw_loaded[slot], cur.val(lambda c: 16 * ((c.n["G"] + off) // RAW_SLOTS + 1)))
                looped = cur.first.in_looped
                column = cur.first.n["M"] + m
                out = mod_col[:, m:m + 1] if looped else mod_sums[:, column:column + 1]
                if looped and m == 0:
                    dve.wait_ge(mod_moved, cur.val(lambda c: c.n["moved"]))
                dve.wait_ge(c_ready, 1)
                dve.tensor_tensor_reduce(raw[:, slot, :], raw[:, slot, :], c_all[:, :], 1.0, 0.0, ALU.mult, ALU.add,
                                         out).then_inc(stream, 2)
                of_chunk = cur.first.kinds_of.count("m")
                if m == of_chunk - 1:
                    if looped:
                        dve.wait_ge(stream, cur.val(lambda c: 2 * (c.n["G"] + off + 1)))
                        first_column = cur.val(lambda c: c.n["M"])
                        dst = mod_sums[:, first_column:first_column + of_chunk] if isinstance(first_column, int) \
                            else mod_sums[:, bass.ds(first_column, of_chunk)]
                        dve.tensor_copy(dst, mod_col[:, 0:of_chunk]).then_inc(mod_moved, 1)

            def mod_vector(k):
                end = MOD_END[k]
                dve.wait_ge(stream, 2 * (end["piece"] + 1))
                dve.wait_ge(mod_moved, end["moved"])
                dve.tensor_tensor(modv[:, k, :], mod_sums[:, KT * k:KT * (k + 1)],
                                  small[:, C_MODB + KT * k:C_MODB + KT * (k + 1)], ALU.add).then_inc(mod_ready, 1)
                if k in GAIN_OF:
                    g = C_GAIN + KT * GAIN_OF[k]
                    dve.wait_ge(mod_ready, ready_after(k) - 1)
                    dve.scalar_tensor_tensor(out=modv[:, k, :], in0=modv[:, k, :], scalar=1.0,
                                             in1=small[:, g:g + KT], op0=ALU.add, op1=ALU.mult) \
                        .then_inc(mod_ready, 1)

            def make_h(name):
                i = h_index(name)
                shift, scale, fresh = H_OF[name]
                if fresh:
                    k = STAT_ORDER.index(name)
                    dve.wait_ge(rms_ok, k + 1)
                    dve.reciprocal(rstd[:, :], rstd[:, :]).then_inc(rstd_ok, 1)
                    dve.wait_ge(rstd_ok, k + 1)
                dve.wait_ge(mod_ready, ready_after(scale))
                if name == "q":
                    dve.wait_ge(blk_lo, 2)

                def norm(q):
                    if q >= 2:
                        dve.wait_ge(h_ready, 4 * i + q - 1)
                    elif not fresh:
                        dve.wait_ge(h_ready, 4 * i)
                    dve.tensor_tensor(temp[:, q % 2, :].rearrange("p (k t) -> p k t", t=T),
                                      x[:, TPC * q:TPC * (q + 1), :],
                                      rstd[:, :].rearrange("p (o t) -> p o t", o=1).to_broadcast([P, TPC, T]),
                                      ALU.mult).then_inc(normed, 1)

                def scale_shift(q):
                    dve.wait_ge(normed, 4 * i + q + 1)
                    for j in range(TPC):
                        part = temp[:, q % 2, T * j:T * (j + 1)]
                        kt = TPC * q + j
                        last = dve.tensor_scalar(part, part, vec(scale, kt), vec(shift, kt), ALU.mult, ALU.add)
                    last.then_inc(affine, 1)

                def low(q):
                    dve.wait_ge(h_hi, 4 * i + q + 1)
                    rows = h_op[:, TPC * q:TPC * (q + 1), :]
                    dve.tensor_tensor(rows[:, :, T:HILO], temp[:, q % 2, :].rearrange("p (k t) -> p k t", t=T),
                                      rows[:, :, 0:T].bitcast(F32), ALU.subtract).then_inc(h_ready, 1)

                norm(0)
                scale_shift(0)
                norm(1)
                scale_shift(1)
                for q in range(4):
                    low(q)
                    if q + 2 < 4:
                        norm(q + 2)
                        scale_shift(q + 2)

            def evacuate(e, name, cur, prev, first):
                kind = prev.first.kind if prev else "mod"
                g = group(prev) if kind != "mod" else None
                if e == 0 and kind in ("ua", "uv", "u", "kvf", "q", "cmp"):
                    dve.wait_ge(zlo, prev.val(lambda c: c.n["zlo"] + 1))
                    if kind == "cmp":
                        out, src = cmp_g[:, :].rearrange("p (i n) -> p i n", i=2), banks[:, g:g + 2, 0:NB]
                    else:
                        out, src = z_view(prev), banks[:, g:g + 4, 0:T]
                    dve.tensor_tensor(out, src, out, ALU.add).then_inc(zsum, 1)
                if e == 1 and kind in ("ua", "uv"):
                    dve.wait_ge(zeroed, 1)
                    for j in range(TPC):
                        dve.wait_ge(tap2, prev.val(lambda c: TPC * c.n["tap2"]) + j + 1)
                        dve.scalar_tensor_tensor(
                            out=y4[:, j, :], in0=zpad[:, j, 1:1 + T], scalar=conv_col(prev, 1, j),
                            in1=y4[:, j, :], op0=ALU.mult, op1=ALU.add).then_inc(tap1, 1)
                    for j in range(TPC):
                        dve.wait_ge(tap1, prev.val(lambda c: TPC * c.n["tap1"]) + j + 1)
                        last = dve.scalar_tensor_tensor(
                            out=y4[:, j, :], in0=zpad[:, j, 0:T], scalar=conv_col(prev, 0, j),
                            in1=y4[:, j, :], op0=ALU.mult, op1=ALU.add)
                    last.then_inc(conv, 1)
                if kind == "dn" and e < 2:
                    gate = GATE_OF[PHASE_OF[id(prev.first)]]
                    if e == 0:
                        done_wait(dve, prev)
                        dve.wait_ge(mod_ready, ready_after(gate))
                        if prev.first.n["xup"] > 0:
                            dve.wait_ge(xlow, prev.first.n["xup"])
                    else:
                        dve.wait_ge(xup, prev.first.n["xup"] + 1)
                    for j in range(TPC):
                        kt = TPC * prev.first.loc + j
                        last = dve.scalar_tensor_tensor(
                            out=x[:, kt, :], in0=banks[:, g + j, T * e:T * (e + 1)], scalar=vec(gate, kt),
                            in1=x[:, kt, :], op0=ALU.mult, op1=ALU.add)
                    last.then_inc(xlow if e else xup, 1)
                if e == 3 and first and name == "sgu_u0":
                    mix_dve(dve)
                if e == 3 and first and name == "wo":
                    attention_dve(dve)
                if e == 3 and first and name in H_OF:
                    make_h(name)

            def step(name, cur, prev, first):
                u = m = e = 0
                for tok, t in enumerate(cur.first.tokens):
                    if t == "s":
                        split_lo(cur, u, tok)
                        u += 1
                    elif t == "m":
                        mod_piece(cur, m, tok)
                        m += 1
                    else:
                        if first and e == 0:
                            for k in FINISHED.get(name, []):
                                mod_vector(k)
                        for stage in stages_at(name, cur, first, e):
                            evacuate(stage, name, cur, prev, first)
                        e += 1

            walk(dve, phases, step)
            if phases[-1][1][-1].kind == "dn":
                last_chunk = At(phases[-1][1][-1])
                for stage in range(2):
                    evacuate(stage, "end", last_chunk, last_chunk, False)

        @block.gpsimd
        def _(pool):
            pool.memset(ident[:, :], 0.0).then_inc(sem("ident_zero"), 1)
            pool.wait_ge(sem("ident_zero"), 1)
            pool.affine_select(out=ident[:, :], in_=ident[:, :], compare_op=ALU.not_equal, fill=1.0, base=0,
                               pattern=[[-1, P]], channel_multiplier=1).then_inc(sem("ident_set"), 1)

            def sum_squares(k, q):
                if q == 3:
                    return
                n = 3 * k + q
                if k == 0:
                    pool.wait_ge(x_loaded, 16)
                else:
                    name = STAT_ORDER[k]
                    pool.wait_ge(xlow, BY_NAME[X_FROM[name]][q].n["xup"] + 1)
                tiles = x[:, TPC * q:TPC * (q + 1), :].rearrange("p k t -> p (k t)")
                if n:
                    pool.wait_ge(xhalf, n)
                pool.tensor_tensor(y, tiles, tiles, ALU.mult).then_inc(xsq, 1)
                pool.wait_ge(xsq, n + 1)
                if n:
                    pool.wait_ge(xsum, n)
                pool.tensor_tensor(gt[:, 512:1024], y[:, 0:512], y[:, 512:1024], ALU.add).then_inc(xhalf, 1)
                pool.wait_ge(xhalf, n + 1)
                pool.tensor_tensor(gt[:, 256:512], gt[:, 512:768], gt[:, 768:1024], ALU.add).then_inc(xquarter, 1)
                pool.wait_ge(xquarter, n + 1)
                if q == 0:
                    pool.tensor_copy(gt[:, 0:256], gt[:, 256:512]).then_inc(xsum, 1)
                else:
                    pool.tensor_tensor(gt[:, 0:256], gt[:, 0:256], gt[:, 256:512], ALU.add).then_inc(xsum, 1)

            for q in range(3):
                sum_squares(0, q)
            pool.wait_ge(mix_loaded, 32)
            pool.affine_select(out=w_sT, in_=w_sT, compare_op=ALU.is_ge, fill=0.0, base=0,
                               pattern=[[0, SGU_G], [1, P]], channel_multiplier=-1).then_inc(masked, 1)

            def step(name, cur, prev, first):
                kind = prev.first.kind if prev else "mod"
                if kind in ("uv", "u"):
                    if kind == "uv":
                        pool.wait_ge(conv, prev.val(lambda c: c.n["conv"] + 1))
                        pool.wait_ge(gated, prev.val(lambda c: c.n["gated"]))
                        pool.tensor_tensor(y, y, gt, ALU.mult).then_inc(prod, 1)
                    else:
                        half = int(PHASE_OF[id(prev.first)][-1])
                        ct = 16 * half + TPC * prev.first.loc
                        pool.wait_ge(gated, prev.val(lambda c: c.n["gated"] + 1))
                        pool.wait_ge(sv_ready, ct + 4)
                        pool.tensor_tensor(y4, gt4, sv[:, ct:ct + 4, :], ALU.mult).then_inc(prod, 1)
                    pool.wait_ge(ahi, prev.val(lambda c: c.n["ahi"] + 1))
                    rows = act_tiles(prev)
                    pool.tensor_tensor(rows[:, :, T:HILO], y4, rows[:, :, 0:T].bitcast(F32), ALU.subtract) \
                        .then_inc(alo, 1)
                if kind == "dn":
                    for k in range(1, len(STAT_ORDER)):
                        if PHASE_OF[id(prev.first)] == X_FROM[STAT_ORDER[k]]:
                            sum_squares(k, prev.first.loc)
                if name == "kv" and not first and cur.first.loc in (3, 4):
                    i = cur.first.loc - 3
                    src = (kc0, vc0)[i]
                    pool.wait_ge(zsum, BY_NAME["kv"][i].n["zsum"] + 1)
                    if i:
                        pool.wait_ge(blk_lo, 1)
                    else:
                        pool.wait_ge(h_ready, 4 * (h_index("kv") + 1))
                    for g in range(NKV):
                        token = src[:, g * T:(g + 1) * T].rearrange("p (n l) -> p l n", l=CMP_STRIDE)
                        for part in range(2):
                            c0 = C_POS + CMP_LEN * i + CMP_STRIDE * part
                            last = pool.tensor_tensor(
                                blocks.rearrange("p (l g n) -> p l g n", l=CMP_LEN, g=NKV)
                                [:, CMP_STRIDE * part:CMP_STRIDE * (part + 1), g, :],
                                token[:, :, part:part + NCMP],
                                small[:, c0:c0 + CMP_STRIDE].rearrange("p (l o) -> p l o", o=1)
                                .to_broadcast([P, CMP_STRIDE, NCMP]), ALU.add)
                    last.then_inc(blk, 1)
                    pool.wait_ge(blk_hi, i + 1)
                    pool.tensor_tensor(blk_view(i)[:, :, NB:2 * NB], blocks.rearrange("p (l n) -> p l n", l=CMP_LEN),
                                       blk_view(i)[:, :, 0:NB].bitcast(F32), ALU.subtract).then_inc(blk_lo, 1)
                if first and name == "wo":
                    attention_pool(pool)

            walk(pool, phases, step)

        @block.tensor
        def _(pe):
            def operand_wait(name, u):
                if name == "wo":
                    pe.wait_ge(at_olo, 4 * (u + 1))
                if name == "cmp" and u == 0:
                    pe.wait_ge(blk_lo, 2)
                if u % 2:
                    return
                need = u // 2 + 1
                if name in H_OF:
                    pe.wait_ge(h_ready, 4 * h_index(name) + need)
                elif name.startswith("dn"):
                    v = [c for c in BY_NAME["up" + name[2:]] if c.kind == "uv"]
                    pe.wait_ge(alo, v[need - 1].n["alo"] + 1)
                elif name.startswith("sgu_o"):
                    pe.wait_ge(alo, BY_NAME["sgu_u" + name[-1]][need - 1].n["alo"] + 1)

            def step(name, cur, prev, first):
                kind = cur.first.kind
                if kind == "mod":
                    return
                g = group(cur)
                free_wait(pe, cur)
                if first and name == "sgu_u0":
                    mix_pe()
                if first and name == "wo":
                    attention_pe(pe)
                if first and name in H_OF and H_OF[name][2]:
                    k = STAT_ORDER.index(name)
                    pe.wait_ge(consts_set, 1)
                    pe.wait_ge(xsum, 3 * (k + 1))
                    pe.matmul(banks[:, 0, 0:T], ones[:, :], gt[:, 0:T], start=True, stop=False)
                    pe.wait_ge(squared, k + 1)
                    for j in range(TPC):
                        last = pe.matmul(banks[:, 0, 0:T], ones[:, :], y[:, T * j:T * (j + 1)], start=False,
                                         stop=(j == TPC - 1))
                    last.then_inc(summed, 1)
                operand = h_op if name in ("sgu_v", "sgu_u0", "sgu_u1", "kv", "q", "gate") or \
                    name.startswith("up") else act_op
                u = 0
                for tok, t in enumerate(cur.first.tokens):
                    if t != "s":
                        continue
                    off = cur.first.piece_of[tok]
                    slot = cur.static(lambda c: (c.n["S"] + u) % SPLIT_SLOTS)
                    pe.wait_ge(stream, cur.val(lambda c: 2 * (c.n["G"] + off) + u % 2 + 1))
                    if first:
                        operand_wait(name, u)
                    if kind in ("v", "kvt"):
                        hi = w_hi[:, slot, :].rearrange("p (k c) -> p k c", k=2)
                        lo = w_lo[:, slot, :].rearrange("p (k c) -> p k c", k=2)
                        for n in range(2):
                            for k in range(2):
                                kt = 2 * u + k
                                a_hi, a_lo = (operand[:, kt, o + P * n:o + P * (n + 1)] for o in (0, T))
                                out = banks[:, g + n, :]
                                pe.matmul(out, a_hi, hi[:, k, :], start=(kt == 0), stop=False,
                                          skip_group_check=True)
                                pe.matmul(out, a_hi, lo[:, k, :], start=False, stop=False, skip_group_check=True)
                                last = pe.matmul(out, a_lo, hi[:, k, :], start=False, stop=(kt == KT - 1),
                                                 skip_group_check=True)
                    elif kind == "gate":
                        hi = w_hi[:, slot, 0:KT * NGATE].rearrange("p (k c) -> p k c", k=KT)
                        lo = w_lo[:, slot, 0:KT * NGATE].rearrange("p (k c) -> p k c", k=KT)
                        for n in range(2):
                            for kt in range(KT):
                                a_hi, a_lo = (operand[:, kt, o + P * n:o + P * (n + 1)] for o in (0, T))
                                out = banks[:, g + n, 0:NGATE]
                                pe.matmul(out, a_hi, hi[:, kt, :], start=(kt == 0), stop=False,
                                          skip_group_check=True)
                                pe.matmul(out, a_hi, lo[:, kt, :], start=False, stop=False, skip_group_check=True)
                                last = pe.matmul(out, a_lo, hi[:, kt, :], start=False, stop=(kt == KT - 1),
                                                 skip_group_check=True)
                    elif kind == "cmp":
                        hi = w_hi[:, slot, :].rearrange("p (l c) -> p l c", l=8)
                        lo = w_lo[:, slot, :].rearrange("p (l c) -> p l c", l=8)
                        i = u // 4
                        for k in range(8):
                            row = 8 * (u % 4) + k
                            rows = blk_view(i)[:, row, :]
                            pe.matmul(banks[:, g + i, 0:2 * NB], hi[:, k, :], rows, start=(row == 0), stop=False,
                                      skip_group_check=True)
                            last = pe.matmul(banks[:, g + i, 0:NB], lo[:, k, :], rows[:, 0:NB], start=False,
                                             stop=(row == CMP_LEN - 1), skip_group_check=True)
                    else:
                        hi = w_hi[:, slot, :].rearrange("p (k c) -> p k c", k=2)
                        lo = w_lo[:, slot, :].rearrange("p (k c) -> p k c", k=2)
                        last_kt = 2 * cur.first.nsub - 1
                        for j in range(TPC):
                            for k in range(2):
                                kt = 2 * u + k
                                pe.matmul(banks[:, g + j, :], hi[:, k, P * j:P * (j + 1)], operand[:, kt, :],
                                          start=(kt == 0), stop=False, skip_group_check=True)
                                last = pe.matmul(banks[:, g + j, 0:T], lo[:, k, P * j:P * (j + 1)],
                                                 operand[:, kt, 0:T], start=False, stop=(kt == last_kt),
                                                 skip_group_check=True)
                    last.then_inc(sub_done, 1)
                    u += 1

            def mix_pe():
                pe.wait_ge(vread, 8)
                for ct in range(SGU_W // P):
                    if ct >= 4:
                        pe.wait_ge(sv_ready, ct - 3)
                    for n in range(2):
                        if ct == 0:
                            pe.wait_ge(wsn, n + 1)
                        last = pe.matmul(banks[:, ct % 4, P * n:P * (n + 1)], sv[:, ct, P * n:P * (n + 1)],
                                         w_sn[:, n, ct // 2, :], start=True, stop=True, skip_group_check=True)
                    last.then_inc(mixed, 1)
                pe.wait_ge(sv_ready, SGU_W // P)

            walk(pe, phases, step)


def stream_pieces(a):
    def cut(w):
        n = w.shape[1] // COLS
        k = w.shape[0] // (KPP * P)
        return w.reshape(k, KPP, P, n, COLS).transpose(3, 0, 2, 1, 4).reshape(n, k, P, PIECE)

    mod = {"mod0": a["mod_w"][0], "mod1": a["mod_w"][1], "kv": a["kv_mod_w"]}
    out = np.zeros((TOTAL["G"], P, PIECE), np.float32)
    cache = {}

    def weights(ch):
        s, i = ch.source, ch.loc
        if s not in cache:
            cache.clear()
            if s[0] == "sgu_v":
                cache[s] = cut(a["sgu_w_in"][0][:, SGU_W:])
            elif s[0] == "sgu_u":
                cache[s] = cut(a["sgu_w_in"][0][:, D * s[1]:D * (s[1] + 1)])
            elif s[0] == "sgu_out":
                cache[s] = cut(a["sgu_w_out"][0][D * s[1]:D * (s[1] + 1)])
            elif s[0] == "up":
                w = a["ffn_w_up"][s[1]]
                c0 = D * s[2]
                c1 = min(c0 + D, D_FF)
                both = [cut(w[:, c0:c1]), cut(w[:, D_FF + c0:D_FF + c1])]
                cache[s] = np.stack(both, 1)
            elif s[0] == "down":
                cache[s] = cut(a["ffn_w_down"][s[1]][D * s[2]:min(D * (s[2] + 1), D_FF)])
            elif s[0] == "kv":
                cache[s] = cut(a["w_kv"])
            elif s[0] == "q":
                cache[s] = cut(a["nsa_w_in"][0][:, :D])
            elif s[0] == "wo":
                cache[s] = cut(a["nsa_w_o"][0])
            elif s[0] == "cmp":
                cache[s] = a["cmp_w1"].reshape(2, 2, 16, P, HD).transpose(0, 1, 3, 2, 4).reshape(1, 4, P, PIECE)
            elif s[0] == "gate":
                g = a["nsa_w_in"][0][:, D:].reshape(KT, P, NGATE).transpose(1, 0, 2).reshape(P, KT * NGATE)
                cache[s] = np.zeros((1, 1, P, PIECE), np.float32)
                cache[s][0, 0, :, :KT * NGATE] = g
        w = cache[s]
        if ch.kind in ("ua", "uv"):
            return w[i, 0 if ch.kind == "ua" else 1]
        if ch.kind in ("kvf", "kvt"):
            return w[ch.loc]
        return w[i]

    for _, chunks in PHASES:
        for ch in chunks:
            g, m, q = ch.n["G"], ch.n["M"], 0
            w = weights(ch) if ch.source else None
            for kind in ch.kinds_of:
                if kind == "m":
                    name, block = MODS[m // KT]
                    o = D * block + P * (m % KT)
                    out[g] = mod[name][:, o:o + P].T
                    m += 1
                else:
                    out[g] = w[q]
                    q += 1
                g += 1
    return out.reshape(TOTAL["G"] * P, PIECE)


def small_table(a):
    def tall(v):
        return np.ascontiguousarray(v.reshape(-1, P).T)

    modb = {"mod0": a["mod_b"][0], "mod1": a["mod_b"][1], "kv": a["kv_mod_b"]}
    parts = [tall(modb[n][D * b:D * (b + 1)]) for n, b in MODS]
    parts += [tall(a["norm_gain"].reshape(4 * D)), tall(a["kv_gain"]), tall(a["sgu_v_gain"][0])]
    parts += [tall(a["ffn_conv_w"].reshape(-1)), tall(a["ffn_conv_b"].reshape(-1))]
    parts += [a["k_gain"].T, a["nsa_q_gain"].T]
    parts += [a["cmp_pos"].reshape(2 * CMP_LEN, HD).T]
    parts += [a["cmp_w2"][0], a["cmp_w2"][1]]
    out = np.ascontiguousarray(np.concatenate(parts, 1))
    assert out.shape == (P, N_SMALL), out.shape
    return out


def position_table():
    out = np.zeros((P, N_POS), np.float32)
    for qb in range(2):
        t = qb * P + np.arange(P)[:, None]
        d = t - (np.arange(NCMP) * CMP_STRIDE + CMP_LEN - 1)[None, :]
        out[:, DW * qb:DW * qb + NCMP] = np.where(d >= 0, d, BIG)
        d = t - np.arange(T)[None, :]
        out[:, DW * qb + 16:DW * (qb + 1)] = np.where(d >= 0, d, BIG)
        out[:, 2 * DW + qb] = t[:, 0] >= CMP_LEN - 1
    return out


def kernel(**inputs):
    import concourse.bacc as bacc
    from concourse.bass_utils import run_bass_kernel_spmd

    a = {k: np.asarray(v) for k, v in inputs.items()}
    arrays = {
        "in_stream": stream_pieces(a),
        "in_small": small_table(a),
        "in_c": np.ascontiguousarray(np.broadcast_to(a["c"], (P, D))),
        "in_x": np.ascontiguousarray(a["x"][0].T.reshape(KT, P, T).transpose(1, 0, 2).reshape(P, KT * T)),
        "in_w_s": np.ascontiguousarray(a["sgu_w_s"][0].transpose(2, 0, 1).reshape(P, SGU_G * P)),
        "in_b_s": np.ascontiguousarray(np.broadcast_to(a["sgu_b_s"][0].reshape(1, SGU_G * P), (P, SGU_G * P))),
        "in_pos": position_table(),
    }
    nc = bacc.Bacc("TRN2", target_bir_lowering=False, num_devices=1)
    io = {n[3:]: nc.dram_tensor(n, v.shape, F32, kind="ExternalInput").ap() for n, v in arrays.items()}
    io["out"] = nc.dram_tensor("out_x", (P, KT * T), F32, kind="ExternalOutput").ap()
    build(nc, io)
    r = run_bass_kernel_spmd(nc, [arrays], core_ids=[0])
    out = np.asarray(r.results[0]["out_x"])
    return np.ascontiguousarray(out.reshape(P, KT, T).transpose(2, 1, 0).reshape(1, T, D))
```

```python
from contextlib import ExitStack

import numpy as np

import concourse.bass as bass
from concourse import mybir

P = 128
D = 2048
T = 256
KT = D // P
EPS = 1e-6
SGU_W = 2 * D
SGU_G = 16
D_FF = 11 * D // 4
FT = D_FF // P
NH, NKV, HD = 16, 4, 128
GRP = NH // NKV
CMP_LEN, CMP_STRIDE = 32, 16
NCMP = T // CMP_STRIDE - 1
NB = NKV * NCMP
NGATE = 3 * NH
BIG = 1e30

COLS = 512
TPC = COLS // P
KPP = 4
PIECE = KPP * COLS
SUB = PIECE // 2
RAW_SLOTS = 4
SPLIT_SLOTS = 4
HILO = 2 * T

F32, F32R = mybir.dt.float32, mybir.dt.float32r
ALU, ACT, AX = mybir.AluOpType, mybir.ActivationFunctionType, mybir.AxisListType

MODS = [("mod0", 0), ("mod0", 1), ("mod0", 2), ("mod0", 3), ("mod0", 4), ("mod0", 5), ("kv", 0), ("kv", 1),
        ("mod1", 0), ("mod1", 1), ("mod1", 2), ("mod1", 3), ("mod1", 4), ("mod1", 5)]
SH1_0, SC1_0, G1_0, SH2_0, SC2_0, G2_0, SH_KV, SC_KV, SH1_1, SC1_1, G1_1, SH2_1, SC2_1, G2_1 = range(14)
GAIN_OF = {SC1_0: 0, SC2_0: 1, SC_KV: 4, SC1_1: 2, SC2_1: 3}

C_MODB = 0
C_GAIN = C_MODB + len(MODS) * KT
C_VGAIN = C_GAIN + 5 * KT
C_CONVW = C_VGAIN + SGU_W // P
C_CONVB = C_CONVW + 2 * 3 * 2 * FT
C_KG = C_CONVB + 2 * 2 * FT
C_QG = C_KG + 3
C_POS = C_QG + 1
C_W2 = C_POS + 2 * CMP_LEN
N_SMALL = C_W2 + 2 * HD

DW = 16 + T
N_POS = 2 * DW + 2

PAT = {
    "P0": "sssEsEsEsEss",
    "P2": "sssEsEsEsmEssm",
    "P3": "sssEsEsEsmmEssm",
    "F2": "sssEsEsEsEssmm",
    "F3": "sssEsEsEsEssmmm",
    "Q0": "sssEEsEsEs",
    "Q1": "sssEEsEsEsm",
    "H0": "mmmmmmmmE" + 4 * "ssmm",
    "H": "E" + 4 * "ssmm",
    "H3": "Essssssss",
    "G1": "smmE",
}


QUARTERS = 4
READY_QUARTER = 3


def ready_after(k):
    return QUARTERS * READY_QUARTER + sum(2 if j in GAIN_OF else 1 for j in range(2, k + 1))


def mod_place(m):
    if m < 2 * KT:
        quarter, r = divmod(m, 2 * KT // QUARTERS)
        return r // TPC, TPC * quarter + r % TPC
    return divmod(m, KT)


class Chunk:

    def __init__(self, kind, loc, pattern, source):
        self.kind, self.loc, self.pattern, self.source = kind, loc, pattern, source
        self.tokens = PAT[pattern]
        self.nsub = self.tokens.count("s")
        self.n = {}


def is_looped(name, chunks):
    return len(chunks) >= 6 and name != "kv"


def plan():
    phases = []

    def add(name, kinds, count, pattern, source):
        phases.append((name, [Chunk(kinds[i % len(kinds)], i // len(kinds), pattern, source)
                              for i in range(count)]))

    phases.append(("head", [Chunk("vh", i, p, ("sgu_v", 0)) for i, p in enumerate(("H0", "H", "H", "H3"))]))
    phases.append(("sgu_v", [Chunk("v", 4 + i, "P3", ("sgu_v", 0)) for i in range(4)]))
    for half in range(2):
        add(f"sgu_u{half}", ["u"], 4, "P3", ("sgu_u", half))
        add(f"sgu_o{half}", ["dn"], 4, "P3", ("sgu_out", half))
    for layer in range(2):
        if layer == 1:
            phases.append(("kv", [Chunk(k, j, p, ("kv", j)) for k, j, p in (
                ("kvf", 0, "F3"), ("kvf", 1, "P3"), ("kvf", 2, "P3"), ("kvt", 3, "P3"), ("kvf", 4, "P3"),
                ("kvt", 5, "P3"))]))
            phases.append(("q", [Chunk("q", 0, "F3", ("q", 0))]))
            phases.append(("cmp", [Chunk("cmp", 0, "P0", ("cmp", 0))]))
            phases.append(("q1", [Chunk("q", 1 + i, "P3", ("q", 0)) for i in range(3)]))
            phases.append(("gate", [Chunk("gate", 0, "G1", ("gate", 0))]))
            add("wo", ["dn"], 4, "P3", ("wo", 0))
        for part, (ups, up_pat, dn_pat) in enumerate(
                ((4, "P2", "P3"), (4, "P2", "P3"), (3, "P2", "Q1")) if layer == 0 else
                ((4, "P2", "P0"), (4, "P0", "P0"), (3, "P0", "Q0"))):
            add(f"up{layer}{part}", ["ua", "uv"], 2 * ups, up_pat, ("up", layer, part))
            if part == 0:
                phases[-1][1][0] = Chunk("ua", 0, "F2", ("up", layer, part))
            add(f"dn{layer}{part}", ["dn"], 4, dn_pat, ("down", layer, part))
    count = dict(c=0, G=0, S=0, M=0, zlo=0, zsum=0, tap2=0, tap1=0, conv=0, gated=0, prod=0, ahi=0, alo=0, xup=0,
                 vread=0, moved=0)
    every, mod_end = [], []
    for name, chunks in phases:
        for ch in chunks:
            ch.in_looped = is_looped(name, chunks)
            ch.n = dict(count)
            ch.piece_of, ch.kinds_of = [], []
            halves = 0
            for tok in ch.tokens:
                if tok == "m" or (tok == "s" and halves % 2 == 0):
                    ch.kinds_of.append("m" if tok == "m" else "w")
                halves += tok == "s"
                if tok != "E":
                    ch.piece_of.append(len(ch.kinds_of) - 1)
                else:
                    ch.piece_of.append(None)
            count["G"] += len(ch.kinds_of)
            pieces = [i for i, k in enumerate(ch.kinds_of) if k == "m"]
            if pieces and ch.in_looped:
                count["moved"] += 1
            for i, off in enumerate(pieces):
                if (count["M"] + i + 1) % KT == 0:
                    mod_end.append({"piece": ch.n["G"] + off, "moved": count["moved"]})
            count["M"] += len(pieces)
            count["S"] += ch.nsub
            k = ch.kind
            count["c"] += 1
            if k in ("ua", "uv", "u", "kvf", "q", "cmp", "gate"):
                count["zlo"] += 1
                count["zsum"] += 1
            if k in ("ua", "uv"):
                count["tap2"] += 1
                count["tap1"] += 1
                count["conv"] += 1
            if k in ("ua", "u"):
                count["gated"] += 1
            if k in ("uv", "u"):
                count["prod"] += 1
                count["ahi"] += 1
                count["alo"] += 1
            if k == "dn":
                count["xup"] += 1
            if k in ("v", "kvt"):
                count["vread"] += 1
            if k == "vh" and ch.loc == QUARTERS - 1:
                count["vread"] += 4
            every.append(ch)
    assert count["M"] == len(MODS) * KT
    return phases, every, count, mod_end


def free_rule(ch):
    if ch.kind == "vh":
        return "vread", {2: 1, 3: 3}[ch.loc]
    if ch.kind in ("v", "kvt"):
        return "vread", ch.n["vread"] + 1
    if ch.kind == "dn":
        return "xlow", TPC * (ch.n["xup"] + 1)
    return "zsum", ch.n["zsum"] + 1


class At:

    def __init__(self, first, second=None, it=None, back=0):
        self.first, self.second, self.it, self.back = first, second, it, back

    def val(self, f):
        a = f(self.first)
        if self.second is None:
            return a
        step = f(self.second) - a
        return a - step * self.back + self.it * step if step else a

    def static(self, f):
        assert self.second is None or f(self.first) == f(self.second)
        return f(self.first)


def walk(eng, phases, step):
    prev = None
    for name, chunks in phases:
        body = 2 if len(chunks) > 1 else 1
        looped = is_looped(name, chunks)
        straight = chunks[:body] if looped else chunks
        for i, ch in enumerate(straight):
            step(name, At(ch), At(prev) if prev else None, i == 0)
            prev = ch
        if looped:
            with eng.Fori(1, len(chunks) // body) as it:
                for b in range(body):
                    cur = At(chunks[body + b], chunks[2 * body + b], it, 1)
                    before = At(chunks[body + b - 1], chunks[2 * body + b - 1], it, 1)
                    step(name, cur, before, False)
            prev = chunks[-1]


PHASES, EVERY, TOTAL, MOD_END = plan()
BY_NAME = dict(PHASES)
ORDER = {ch.n["c"]: ch for ch in EVERY}


def build(nc, io, stop=None):
    phases = PHASES
    if stop is not None:
        names = [n for n, _ in PHASES]
        phases = PHASES[:names.index(stop)]
    n_pieces = TOTAL["G"] if stop is None else BY_NAME[stop][0].n["G"]
    slopes = [2.0 ** (-8.0 * (h + 1) / NH) for h in range(NH)]
    ctx = ExitStack()
    with ctx:
        def sb(name, shape, dt=F32):
            return ctx.enter_context(nc.sbuf_tensor(name, shape, dt))

        with nc.sbuf_tensor("attn_area", [P, KT * HILO], F32) as attn_area:
            pass
        h_op = sb("h_op", [P, KT, HILO], F32R)
        with nc.sbuf_tensor("mix_area", [P, KT * HILO], F32) as mix_area:
            pass
        act_op = sb("act_op", [P, KT, HILO], F32R)
        x = sb("x_res", [P, KT, T])
        raw = sb("raw", [P, RAW_SLOTS, PIECE])
        w_hi = sb("w_hi", [P, SPLIT_SLOTS, SUB], F32R)
        w_lo = sb("w_lo", [P, SPLIT_SLOTS, SUB], F32R)
        scratch = sb("scratch", [P, 32 * T])
        c_all = sb("c_all", [P, D])
        mod_sums = sb("mod_sums", [P, len(MODS) * KT])
        mod_col = sb("mod_col", [P, 4])
        small = sb("small", [P, N_SMALL])
        zpad = sb("zpad", [P, TPC, T + 2])
        temp = sb("temp", [P, 2, TPC * T])
        rstd = sb("rstd", [P, T])
        kcmp = sb("kcmp", [P, NB])
        vcmp = sb("vcmp", [16, NKV * HD])
        gates = sb("gates", [P, 2, NGATE])
        cmp_g = sb("cmp_g", [P, 2 * NB])
        ones = sb("ones", [P, P])
        ident = sb("ident", [P, P])
        vstat = sb("vstat", [P, 24])
        pick = sb("pick", [P, 2 * NH - 1])
        eps = sb("eps", [P, 1])
        banks = ctx.enter_context(nc.psum_tensor("banks", [P, 8, 512], F32))

        modv = mod_sums[:, :].rearrange("p (m k) -> p m k", k=KT)
        y, gt = temp[:, 0, :], temp[:, 1, :]
        temp8 = temp[:, :, :].rearrange("p a (j t) -> p (a j) t", t=T)
        y4 = y.rearrange("p (j t) -> p j t", j=TPC)
        gt4 = gt.rearrange("p (j t) -> p j t", j=TPC)
        sv = scratch[:, :].rearrange("p (c t) -> p c t", t=T)
        w_sT = mix_area[:, 0:2048].rearrange("p (g t) -> p g t", g=SGU_G)
        w_sn = mix_area[:, 2048:6144].rearrange("p (n g t) -> p n g t", n=2, g=SGU_G)
        b_sb = mix_area[:, 6144:8192].rearrange("p (g t) -> p g t", g=SGU_G)
        squares = mix_area[:, 0:6144]
        kc0, vc0 = scratch[:, 0:1024], scratch[:, 1024:2048]
        q_raw = scratch[:, 0:4096]
        k_slc, k_win = scratch[:, 4096:5120], scratch[:, 5120:6144]
        v_slc, v_win = scratch[:, 6144:7168], scratch[:, 7168:8192]
        blocks = temp[:, :, :].rearrange("p a b -> p (a b)")[:, 0:CMP_LEN * NB]
        blk_op = act_op[:, :, :].rearrange("p k t -> p (k t)")

        def sem(name):
            return ctx.enter_context(nc.semaphore(name))

        raw_loaded = [sem(f"raw_loaded{s}") for s in range(RAW_SLOTS)]
        hi_ready = sem("hi_ready")
        stream = sem("stream")
        sub_done = sem("sub_done")
        tile_done = sem("tile_done")
        small_loaded = sem("small_loaded")
        x_loaded = sem("x_loaded")
        mix_loaded = sem("mix_loaded")
        pos_loaded = sem("pos_loaded")
        c_loaded = sem("c_loaded")
        c_spread = sem("c_spread")
        c_ready = sem("c_ready")
        zeroed = sem("zeroed")
        pick_zero = sem("pick_zero")
        consts_set = sem("consts_set")
        ident_zero = sem("ident_zero")
        ident_set = sem("ident_set")
        mod_moved = sem("mod_moved")
        mod_ready = sem("mod_ready")
        xsq = sem("xsq")
        xhalf = sem("xhalf")
        xquarter = sem("xquarter")
        xsum = sem("xsum")
        squared = sem("squared")
        summed = sem("summed")
        rms_ok = sem("rms_ok")
        rstd_ok = sem("rstd_ok")
        normed = sem("normed")
        h_hi = sem("h_hi")
        h_ready = sem("h_ready")
        zlo = sem("zlo")
        zsum = sem("zsum")
        tap2 = sem("tap2")
        tap1 = sem("tap1")
        conv = sem("conv")
        gated = sem("gated")
        prod = sem("prod")
        ahi = sem("ahi")
        alo = sem("alo")
        xup = sem("xup")
        xlow = sem("xlow")
        vread = sem("vread")
        vsq = sem("vsq")
        vred = sem("vred")
        vmean = sem("vmean")
        vrstd = sem("vrstd")
        vrec = sem("vrec")
        masked = sem("masked")
        wsn = sem("wsn")
        mixed = sem("mixed")
        sv_ready = sem("sv_ready")
        blk = sem("blk")
        blk_hi = sem("blk_hi")
        blk_lo = sem("blk_lo")
        cmp_gelu = sem("cmp_gelu")
        cmp_done = sem("cmp_done")
        cmp_read = sem("cmp_read")
        keys_squared = sem("keys_squared")
        cmp_keys_squared = sem("cmp_keys_squared")
        queries_squared = sem("queries_squared")
        square_sums = sem("square_sums")
        rms_taken = sem("rms_taken")
        rms_inverted = sem("rms_inverted")
        query_rms_inverted = sem("query_rms_inverted")
        gains_multiplied = sem("gains_multiplied")
        key_rms_spread = sem("key_rms_spread")
        query_rms_turned = sem("query_rms_turned")
        keys_normed = sem("keys_normed")
        gates_ready = sem("gates_ready")
        gates_turned = sem("gates_turned")
        qk_done = sem("qk_done")
        scores_scaled = sem("scores_scaled")
        scores_biased = sem("scores_biased")
        max_ready = sem("max_ready")
        exp_ready = sem("exp_ready")
        sums_guarded = sem("sums_guarded")
        sums_inverted = sem("sums_inverted")
        coef_ready = sem("coef_ready")
        weights_scaled = sem("weights_scaled")
        weights_turned = sem("weights_turned")
        turned_read = sem("turned_read")
        turned_cmp_read = sem("turned_cmp_read")
        pv_done = sem("pv_done")
        out_hi = sem("out_hi")
        out_lo = sem("out_lo")
        stored = sem("stored")
        read_sems = {"vread": vread, "zsum": zsum, "xlow": xlow}

        def vec(slice_, kt):
            return modv[:, slice_, kt:kt + 1] if isinstance(kt, int) else modv[:, slice_, bass.ds(kt, 1)]

        def col(c0, i):
            return small[:, c0 + i:c0 + i + 1] if isinstance(i, int) else small[:, bass.ds(i + c0, 1)]

        H_OF = {"head": (SH1_0, SC1_0, True), "up00": (SH2_0, SC2_0, True), "kv": (SH_KV, SC_KV, True),
                "q": (SH1_1, SC1_1, False), "up10": (SH2_1, SC2_1, True)}
        H_ORDER = [n for n, _ in PHASES if n in H_OF]
        STAT_ORDER = [n for n in H_ORDER if H_OF[n][2]]
        FINISHED = {"sgu_o0": [G1_0], "sgu_o1": [SH2_0], "up00": [SC2_0], "dn00": [G2_0],
                    "up01": [SH_KV], "up02": [SC_KV], "kv": [SH1_1, SC1_1], "wo": [G1_1, SH2_1], "up10": [SC2_1],
                    "dn10": [G2_1]}
        GATE_OF = {"sgu_o0": G1_0, "sgu_o1": G1_0, "dn00": G2_0, "dn01": G2_0, "dn02": G2_0, "wo": G1_1,
                   "dn10": G2_1, "dn11": G2_1, "dn12": G2_1}
        PHASE_OF = {}
        for pname, chunks in PHASES:
            for ch in chunks:
                PHASE_OF[id(ch)] = pname

        X_FROM = {"up00": "sgu_o1", "kv": "dn02", "up10": "wo"}

        def h_index(name):
            return H_ORDER.index(name)

        def free_wait(eng, cur):
            if cur.first.kind == "vh":
                return
            if cur.second is None:
                which, value = free_rule(ORDER[cur.first.n["c"] - 2])
            else:
                which, value = free_rule(cur.first)
                step = free_rule(cur.second)[1] - value
                value = value - step * (1 + cur.back) + cur.it * step
            eng.wait_ge(read_sems[which], value)

        def stages_at(name, cur, first, e):
            if cur.first.kind == "vh":
                return ()
            if first and (name in H_OF or name == "wo"):
                return range(4) if e == 0 else ()
            return range(4) if cur.first.kind == "gate" else (e,)

        def done_wait(eng, prev):
            eng.wait_ge(sub_done, prev.val(lambda c: c.n["S"] + c.nsub))

        UPDATES = {0: [(0, j) for j in range(TPC)], 1: [(1, j) for j in range(TPC)],
                   "all": [(0, 0), (0, 1), (1, 0), (0, 2), (1, 1), (0, 3), (1, 2), (1, 3)]}

        def h_tiles(e):
            return {0: range(0, 8), 1: range(8, 12), 2: range(12, 16), 3: range(0)}[e]

        def group(prev):
            return 4 * (prev.static(lambda c: c.n["c"] % 2))

        UNITS = [(h, qb) for h in range(NH) for qb in range(2)]
        area = attn_area
        pos = area[:, 7168:7168 + N_POS]
        r_k = area[0:16, 3584:3584 + T]
        r_q = area[0:16, 3840:3840 + T]
        r_c = area[:, 4096:4096 + NB]
        sq_c = area[:, 4160:4160 + NB]
        q_scale = area[:, 4224:4256]
        gates_t = area[0:NGATE, 4352:4352 + T]
        neg_max = area[:, 6400:6400 + 96]
        denom = area[:, 6500:6500 + 96]
        coef = area[:, 6600:6600 + 96]
        k_gains = vstat[:, 0:3]

        def scores(i):
            return area[:, 528 * (i % 4):528 * (i % 4) + 528]

        def both(ap, n):
            return ap.rearrange("p (b k) -> p b k", b=2)[:, :, 0:n]

        def probs_t(i):
            o = 2112 + 640 * (i % 2)
            return area[:, o:o + 640]

        def attention_act(act):
            act.dma_start(pos, io["pos"]).then_inc(pos_loaded, 16)
            act.wait_ge(square_sums, 1)
            act.activation(r_k, banks[0:16, 7, 0:T], ACT.Sqrt, scale=1.0 / HD, bias=eps[0:16, :]) \
                .then_inc(rms_taken, 1)
            act.wait_ge(cmp_read, 1)
            act.activation(sq_c, kcmp[:, :], ACT.Square).then_inc(cmp_keys_squared, 1)
            act.wait_ge(square_sums, 2)
            act.activation(r_c, banks[:, 5, 0:NB], ACT.Sqrt, scale=1.0 / HD, bias=eps[:, :]) \
                .then_inc(rms_taken, 1)
            act.wait_ge(square_sums, 3)
            act.activation(r_q, banks[0:16, 1, 0:T], ACT.Sqrt, scale=1.0 / HD, bias=eps[0:16, :]) \
                .then_inc(rms_taken, 1)
            act.wait_ge(zsum, BY_NAME["gate"][0].n["zsum"] + 1)
            act.activation(gates_t, gates_t, ACT.Sigmoid).then_inc(gates_ready, 1)
            for i in range(len(UNITS) + 4):
                if i < len(UNITS):
                    h, qb = UNITS[i]
                    keys = P * (qb + 1)
                    act.wait_ge(qk_done, i + 1)
                    act.wait_ge(keys_normed, 3)
                    if i >= 4:
                        act.wait_ge(weights_turned, i - 3)
                    r = q_scale[:, 16 * qb + h:16 * qb + h + 1]
                    act.activation(both(scores(i)[:, 16:528], keys), both(banks[:, i % 2, :], keys), ACT.Copy,
                                   scale=r)
                    act.activation(scores(i)[:, 0:NCMP], banks[:, 2 + i % 2, 0:NCMP], ACT.Copy, scale=r) \
                        .then_inc(scores_scaled, 1)
                if 1 <= i <= len(UNITS):
                    j = i - 1
                    keys = P * (UNITS[j][1] + 1)
                    act.wait_ge(max_ready, j + 1)
                    for b, (o, n) in enumerate(((0, NCMP), (16, keys), (16 + T, keys))):
                        part = scores(j)[:, o:o + n]
                        last = act.activation(part, part, ACT.Exp, bias=neg_max[:, 3 * j + b:3 * j + b + 1],
                                              accum_out=denom[:, 3 * j + b:3 * j + b + 1])
                    last.then_inc(exp_ready, 1)
                if 3 <= i <= len(UNITS) + 2:
                    j = i - 3
                    act.wait_ge(weights_turned, j + 1)
                    if j >= 2:
                        act.wait_ge(pv_done, j - 1)
                    act.activation(probs_t(j)[0:NCMP, 512:640], banks[0:NCMP, 6 + j % 2, P:2 * P], ACT.Copy) \
                        .then_inc(turned_cmp_read, 1)
                if i >= 4:
                    j = i - 4
                    h, qb = UNITS[j]
                    act.wait_ge(pv_done, j + 1)
                    act.activation(act_op[:, h, P * qb:P * (qb + 1)], banks[:, 6 + j % 2, 0:P], ACT.Copy) \
                        .then_inc(out_hi, 1)

        def attention_dve(dve):
            dve.tensor_scalar(k_gains, small[:, C_KG:C_KG + 3], small[:, C_QG:C_QG + 1], None, ALU.mult) \
                .then_inc(gains_multiplied, 1)
            dve.wait_ge(cmp_done, 1)
            dve.tensor_copy(kcmp[:, :], banks[:, 5, 0:NB])
            dve.tensor_copy(vcmp[0:NCMP, :], banks[0:NCMP, 6, :]).then_inc(cmp_read, 1)
            dve.wait_ge(rms_taken, 1)
            dve.reciprocal(r_k, r_k).then_inc(rms_inverted, 1)
            dve.wait_ge(gains_multiplied, 1)
            dve.wait_ge(rms_taken, 2)
            dve.reciprocal(r_c, r_c).then_inc(rms_inverted, 1)
            dve.wait_ge(rms_inverted, 2)
            dve.scalar_tensor_tensor(out=kcmp[:, :], in0=kcmp[:, :], scalar=k_gains[:, 0:1], in1=r_c,
                                     op0=ALU.mult, op1=ALU.mult).then_inc(keys_normed, 1)
            dve.wait_ge(rms_taken, 3)
            dve.reciprocal(r_q, r_q).then_inc(query_rms_inverted, 1)
            dve.wait_ge(query_rms_inverted, 1)
            dve.tensor_scalar(r_q, r_q, float(HD) ** -0.5, None, ALU.mult).then_inc(rms_inverted, 1)
            dve.wait_ge(key_rms_spread, 1)
            for b, k in ((1, k_slc), (2, k_win)):
                last = dve.scalar_tensor_tensor(
                    out=k, in0=k, scalar=k_gains[:, b:b + 1],
                    in1=banks[:, 2 + 2 * b:4 + 2 * b, :].rearrange("p a t -> p (a t)"), op0=ALU.mult,
                    op1=ALU.mult)
            last.then_inc(keys_normed, 1)
            dve.wait_ge(query_rms_turned, 1)
            dve.tensor_copy(q_scale, banks[:, 2, 0:32]).then_inc(keys_normed, 1)
            dve.wait_ge(gates_turned, 1)
            dve.wait_ge(pos_loaded, 16)
            gates_psum = banks[:, 7, 0:2 * NGATE].rearrange("p (q c) -> p q c", q=2)
            dve.tensor_copy(gates[:, :, NH:NGATE], gates_psum[:, :, NH:NGATE])
            for qb in range(2):
                dve.tensor_scalar(gates[:, qb, 0:NH], gates_psum[:, qb, 0:NH],
                                  pos[:, 2 * DW + qb:2 * DW + qb + 1], None, ALU.mult)
            for i in range(len(UNITS) + 4):
                if i < len(UNITS):
                    h, qb = UNITS[i]
                    keys = P * (qb + 1)
                    dist = pos[:, DW * qb:DW * (qb + 1)]
                    main, short = both(scores(i)[:, 16:528], keys), scores(i)[:, 0:NCMP]
                    dve.wait_ge(scores_scaled, i + 1)
                    dve.scalar_tensor_tensor(
                        out=main, in0=dist[:, 16:16 + keys].rearrange("p (o k) -> p o k", o=1)
                        .to_broadcast([P, 2, keys]), scalar=-slopes[h], in1=main, op0=ALU.mult, op1=ALU.add)
                    dve.scalar_tensor_tensor(out=short, in0=dist[:, 0:NCMP], scalar=-slopes[h], in1=short,
                                             op0=ALU.mult, op1=ALU.add).then_inc(scores_biased, 1)
                if 3 <= i <= len(UNITS) + 2:
                    j = i - 3
                    keys = P * (UNITS[j][1] + 1)
                    dve.wait_ge(weights_turned, j + 1)
                    if j >= 2:
                        dve.wait_ge(pv_done, j - 1)
                    dve.tensor_copy(both(probs_t(j)[:, 0:512], keys), both(banks[:, 4 + j % 2, :], keys)) \
                        .then_inc(turned_read, 1)
                if i < len(UNITS):
                    dve.wait_ge(scores_biased, i + 1)
                    dve.tensor_reduce(neg_max[:, 3 * i + 1:3 * i + 3], main, AX.X, ALU.max, negate=True)
                    dve.tensor_reduce(neg_max[:, 3 * i:3 * i + 1], short, AX.X, ALU.max, negate=True) \
                        .then_inc(max_ready, 1)
                j = i - 1
                if 0 <= j < len(UNITS):
                    d, f = denom[:, 3 * j:3 * j + 3], coef[:, 3 * j:3 * j + 3]
                    dve.wait_ge(exp_ready, j + 1)
                    dve.tensor_scalar(d, d, 1e-30, None, ALU.max).then_inc(sums_guarded, 1)
                if i >= 4:
                    n = i - 4
                    h, qb = UNITS[n]
                    dve.wait_ge(out_hi, n + 1)
                    dve.tensor_tensor(act_op[:, h, T + P * qb:T + P * (qb + 1)], banks[:, 6 + n % 2, 0:P],
                                      act_op[:, h, P * qb:P * (qb + 1)].bitcast(F32), ALU.subtract) \
                        .then_inc(out_lo, 1)
                if 0 <= j < len(UNITS):
                    h, qb = UNITS[j]
                    dve.wait_ge(sums_guarded, j + 1)
                    dve.reciprocal(f, d).then_inc(sums_inverted, 1)
                    dve.wait_ge(sums_inverted, j + 1)
                    dve.tensor_tensor(f, f, gates[:, qb, :].rearrange("p (b h) -> p h b", h=NH)[:, h, :],
                                      ALU.mult).then_inc(coef_ready, 1)

        def attention_pool(pool):
            for j in range(len(UNITS)):
                keys = P * (UNITS[j][1] + 1)
                pool.wait_ge(coef_ready, j + 1)
                for b, (o, n) in enumerate(((0, NCMP), (16, keys), (16 + T, keys))):
                    part = scores(j)[:, o:o + n]
                    last = pool.tensor_scalar(part, part, coef[:, 3 * j + b:3 * j + b + 1], None, ALU.mult)
                last.then_inc(weights_scaled, 1)

        def attention_pe(pe):
            pe.wait_ge(ident_set, 1)
            pe.wait_ge(cmp_gelu, 1)
            pe.matmul(banks[:, 5, 0:NB], small[:, C_W2:C_W2 + HD], cmp_g[:, 0:NB], start=True, stop=True,
                      skip_group_check=True)
            for g in range(NKV):
                last = pe.matmul(banks[0:NCMP, 6, HD * g:HD * (g + 1)],
                                 cmp_g[:, NB + NCMP * g:NB + NCMP * (g + 1)], small[:, C_W2 + HD:C_W2 + 2 * HD],
                                 start=True, stop=True, skip_group_check=True)
            last.then_inc(cmp_done, 1)
            pe.wait_ge(keys_squared, 1)
            for r in range(2 * NKV):
                last = pe.matmul(banks[0:16, 7, 0:T], pick[:, NH - 1 - r:2 * NH - 1 - r],
                                 squares[:, 4096 + T * r:4096 + T * (r + 1)], start=(r == 0),
                                 stop=(r == 2 * NKV - 1))
            last.then_inc(square_sums, 1)
            pe.wait_ge(cmp_keys_squared, 1)
            pe.matmul(banks[:, 5, 0:NB], ones[:, :], sq_c, start=True, stop=True).then_inc(square_sums, 1)
            pe.wait_ge(zsum, BY_NAME["q1"][-1].n["zsum"] + 1)
            for h in range(NH):
                if h % TPC == 0:
                    pe.wait_ge(queries_squared, h // TPC + 1)
                last = pe.matmul(banks[0:16, 1, 0:T], pick[:, NH - 1 - h:2 * NH - 1 - h],
                                 squares[:, T * h:T * (h + 1)], start=(h == 0), stop=(h == NH - 1))
            last.then_inc(square_sums, 1)
            pe.wait_ge(rms_inverted, 2)
            pe.wait_ge(zsum, BY_NAME["gate"][0].n["zsum"] + 1)
            for r in range(2 * NKV):
                last = pe.matmul(banks[:, 4 + r // 2, T * (r % 2):T * (r % 2 + 1)],
                                 ident[0:16, r:r + 1].to_broadcast([16, P]), r_k, start=True, stop=True,
                                 skip_group_check=True)
            last.then_inc(key_rms_spread, 1)
            pe.wait_ge(rms_inverted, 3)
            for qb in range(2):
                last = pe.transpose(banks[:, 2, 16 * qb:16 * (qb + 1)], r_q[:, P * qb:P * (qb + 1)],
                                    ident[0:16, 0:16])
            last.then_inc(query_rms_turned, 1)
            pe.wait_ge(gates_ready, 1)
            pe.wait_ge(keys_normed, 2)
            for qb in range(2):
                last = pe.transpose(banks[:, 7, NGATE * qb:NGATE * (qb + 1)], gates_t[:, P * qb:P * (qb + 1)],
                                    ident[0:NGATE, 0:NGATE])
            last.then_inc(gates_turned, 1)
            pe.wait_ge(keys_normed, 3)

            def score(i):
                h, qb = UNITS[i]
                g, keys = h // GRP, P * (qb + 1)
                if i >= 2:
                    pe.wait_ge(scores_scaled, i - 1)
                query = q_raw[:, T * h + P * qb:T * h + P * (qb + 1)]
                pe.matmul(banks[:, i % 2, 0:keys], query, k_slc[:, T * g:T * g + keys], start=True, stop=True,
                          skip_group_check=True)
                pe.matmul(banks[:, i % 2, T:T + keys], query, k_win[:, T * g:T * g + keys], start=True,
                          stop=True, skip_group_check=True)
                pe.matmul(banks[:, 2 + i % 2, 0:NCMP], query, kcmp[:, NCMP * g:NCMP * (g + 1)], start=True,
                          stop=True, skip_group_check=True).then_inc(qk_done, 1)

            score(0)
            for i in range(len(UNITS) + 4):
                if i + 1 < len(UNITS):
                    score(i + 1)
                if 3 <= i <= len(UNITS) + 2:
                    j = i - 3
                    qb = UNITS[j][1]
                    pe.wait_ge(weights_scaled, j + 1)
                    if j >= 2:
                        pe.wait_ge(turned_read, j - 1)
                        pe.wait_ge(turned_cmp_read, j - 1)
                        pe.wait_ge(out_lo, j - 1)
                    for b in range(2):
                        for n in range(qb + 1):
                            o = T * b + P * n
                            pe.transpose(banks[:, 4 + j % 2, o:o + P], scores(j)[:, 16 + o:16 + o + P],
                                         ident[:, :])
                    pe.transpose(banks[0:NCMP, 6 + j % 2, P:2 * P], scores(j)[:, 0:NCMP], ident[:, :]) \
                        .then_inc(weights_turned, 1)
                if i >= 4:
                    j = i - 4
                    h, qb = UNITS[j]
                    g = h // GRP
                    pe.wait_ge(turned_read, j + 1)
                    pe.wait_ge(turned_cmp_read, j + 1)
                    out = banks[:, 6 + j % 2, 0:P]
                    pt = probs_t(j)
                    for b, v in ((0, v_slc), (1, v_win)):
                        for n in range(qb + 1):
                            pe.matmul(out, v[:, 512 * n + HD * g:512 * n + HD * (g + 1)],
                                      pt[:, T * b + P * n:T * b + P * (n + 1)], start=(b == 0 and n == 0),
                                      stop=False, skip_group_check=True)
                    pe.matmul(out, vcmp[0:NCMP, HD * g:HD * (g + 1)], pt[0:NCMP, 512:640], start=False, stop=True,
                              skip_group_check=True).then_inc(pv_done, 1)

        def z_view(prev):
            kind = prev.first.kind
            if kind in ("ua", "uv"):
                return zpad[:, :, 2:T + 2]
            if kind == "u":
                return y4
            if kind == "q":
                o = TPC * T * prev.first.loc
                return q_raw[:, o:o + TPC * T].rearrange("p (j t) -> p j t", j=TPC)
            dst = {0: kc0, 1: vc0, 2: k_slc, 4: k_win}[prev.first.loc]
            return dst.rearrange("p (j t) -> p j t", j=4)

        def local(prev):
            phase = BY_NAME[PHASE_OF[id(prev.first)]]
            c0 = 0 if prev.first.kind == "v" else phase[0].n["c"]
            per = 2 if prev.first.kind in ("ua", "uv") else 1
            return prev.val(lambda c: (c.n["c"] - c0) // per)

        def act_tiles(prev):
            k = local(prev)
            return act_op[:, TPC * k:TPC * k + TPC, :] if isinstance(k, int) else \
                act_op[:, bass.ds(k * TPC, TPC), :]

        def v_tiles(k, n):
            return sv[:, 4 * k:4 * k + 4, P * n:P * (n + 1)]

        def conv_col(prev, tap, j):
            name = PHASE_OF[id(prev.first)]
            layer, part = int(name[2]), int(name[3])
            k = local(prev)
            base = (C_CONVB + layer * 2 * FT) if tap is None else C_CONVW + (layer * 3 + tap) * 2 * FT
            base += (FT if prev.first.kind == "uv" else 0) + 16 * part + j
            return small[:, base + 4 * k:base + 4 * k + 1] if isinstance(k, int) else \
                small[:, bass.ds(k * 4 + base, 1)]

        def blk_view(i):
            return blk_op[:, i * CMP_LEN * 2 * NB:(i + 1) * CMP_LEN * 2 * NB].rearrange(
                "p (l n) -> p l n", l=CMP_LEN)

        def mix_weights(dve):
            dve.wait_ge(vsq, 16)
            dve.tensor_reduce(vstat[:, 16:18], vstat[:, 0:16].rearrange("p (n c) -> p n c", n=2), AX.X, ALU.add) \
                .then_inc(vred, 1)
            dve.wait_ge(vred, 1)
            dve.tensor_scalar(vstat[:, 20:22], vstat[:, 16:18], 1.0 / SGU_W, EPS, ALU.mult, ALU.add) \
                .then_inc(vmean, 1)
            dve.wait_ge(vmean, 1)
            dve.wait_ge(vrstd, 1)
            dve.reciprocal(vstat[:, 22:24], vstat[:, 18:20]).then_inc(vrec, 1)
            dve.wait_ge(vrec, 1)
            dve.wait_ge(masked, 1)
            for n in range(2):
                dve.tensor_scalar(w_sn[:, n, :, :], w_sT, vstat[:, 22 + n:23 + n], None, ALU.mult).then_inc(wsn, 1)

        def mix_tiles(dve, g):
            dve.wait_ge(mix_loaded, 32)
            for ct in range(SGU_W // P):
                dve.wait_ge(mixed, ct + 1)
                dve.scalar_tensor_tensor(
                    out=sv[:, ct, :].rearrange("p (n t) -> p n t", n=2),
                    in0=banks[:, g + ct % 4, 0:T].rearrange("p (n t) -> p n t", n=2), scalar=col(C_VGAIN, ct),
                    in1=b_sb[:, ct // 2, :].rearrange("p (o t) -> p o t", o=1).to_broadcast([P, 2, P]),
                    op0=ALU.mult, op1=ALU.add).then_inc(sv_ready, 1)

        block = ctx.enter_context(nc.Block())

        @block.sync
        def _(sp):
            def first_pieces(slots):
                for s in slots:
                    sp.dma_start(raw[:, s, :], io["stream"][s * P:(s + 1) * P, :]).then_inc(raw_loaded[s], 16)

            sp.dma_start(c_all[0:1, :], io["c"]).then_inc(c_loaded, 16)
            first_pieces((0, 1))
            sp.dma_start(x[:, :, :], io["x"].rearrange("p (k t) -> p k t", t=T)).then_inc(x_loaded, 16)
            first_pieces((2, 3))
            sp.dma_start(small[:, :], io["small"]).then_inc(small_loaded, 16)
            full = n_pieces // RAW_SLOTS
            with sp.Fori(1, full) as i:
                for s in range(RAW_SLOTS):
                    sp.wait_ge(stream, i * (2 * RAW_SLOTS) + (2 * (s + 1) - 2 * RAW_SLOTS))
                    sp.dma_start(raw[:, s, :], io["stream"][bass.ds(i * (RAW_SLOTS * P) + s * P, P), :]) \
                        .then_inc(raw_loaded[s], 16)
            for g in range(full * RAW_SLOTS, n_pieces):
                sp.wait_ge(stream, 2 * (g - RAW_SLOTS + 1))
                sp.dma_start(raw[:, g % RAW_SLOTS, :], io["stream"][g * P:(g + 1) * P, :]) \
                    .then_inc(raw_loaded[g % RAW_SLOTS], 16)
            last = phases[-1][1]
            if last[0].kind == "dn" and len(last) == 4:
                for i, ch in enumerate(last):
                    sp.wait_ge(xlow, TPC * (ch.n["xup"] + 1))
                    sp.dma_start(io["out"].rearrange("p (k t) -> p k t", t=T)[:, TPC * i:TPC * (i + 1), :],
                                 x[:, TPC * i:TPC * (i + 1), :]).then_inc(stored, 16)
                sp.wait_ge(stored, 64)

        @block.scalar
        def _(act):
            act.wait_ge(c_spread, 1)
            act.activation(c_all[:, :].rearrange("p (b n) -> p b n", b=4), banks[:, 4:8, :], ACT.Silu) \
                .then_inc(c_ready, 1)

            def split_hi(cur, u, tok):
                off, chunk = cur.first.piece_of[tok], cur.first
                slot = cur.static(lambda c: (c.n["G"] + off) % RAW_SLOTS)
                out = cur.static(lambda c: (c.n["S"] + u) % SPLIT_SLOTS)
                act.wait_ge(raw_loaded[slot], cur.val(lambda c: 16 * ((c.n["G"] + off) // RAW_SLOTS + 1)))
                if cur.second is not None or chunk.n["S"] + u >= SPLIT_SLOTS:
                    act.wait_ge(sub_done, cur.val(lambda c: c.n["S"] + u - SPLIT_SLOTS + 1))
                n = KT * NGATE if chunk.kind == "gate" else SUB
                half = (u % 2) * SUB
                act.activation(w_hi[:, out, 0:n], raw[:, slot, half:half + n], ACT.Copy).then_inc(hi_ready, 1)

            def make_h(name, tiles, fresh, ready):
                i = h_index(name)
                if fresh:
                    k = STAT_ORDER.index(name)
                    if k == 0:
                        act.wait_ge(x_loaded, 16)
                    act.wait_ge(xhalf, 3 * (k + 1))
                    for j in range(TPC):
                        if k:
                            act.wait_ge(xlow, TPC * BY_NAME[X_FROM[name]][3].n["xup"] + j + 1)
                        act.activation(y4[:, j, :], x[:, 3 * TPC + j, :], ACT.Square).then_inc(squared, 1)
                    act.wait_ge(summed, k + 1)
                    act.wait_ge(consts_set, 1)
                    act.activation(rstd[:, :], banks[:, 0, 0:T], ACT.Sqrt, scale=1.0 / D, bias=eps[:, :]) \
                        .then_inc(rms_ok, 1)
                shift = H_OF[name][0]
                act.wait_ge(mod_ready, ready)
                for kt in tiles:
                    act.wait_ge(normed, KT * i + kt + 1)
                    act.activation(h_op[:, kt, 0:T], temp8[:, kt % 8, :], ACT.Identity, bias=vec(shift, kt)) \
                        .then_inc(h_hi, 1)

            def evacuate(e, name, cur, prev, first):
                kind = prev.first.kind
                g = group(prev)
                if e == 0 and kind in ("ua", "uv", "u", "kvf", "q", "cmp", "gate"):
                    done_wait(act, prev)
                    if kind == "cmp":
                        out, src = cmp_g[:, :].rearrange("p (i n) -> p i n", i=2), banks[:, g:g + 2, NB:2 * NB]
                    elif kind == "gate":
                        out, src = gates_t, banks[0:NGATE, g, T:HILO]
                    else:
                        out, src = z_view(prev), banks[:, g:g + 4, T:HILO]
                    if kind in ("ua", "uv"):
                        act.wait_ge(zeroed, 1)
                        act.wait_ge(conv, prev.val(lambda c: c.n["conv"]))
                    if kind == "u":
                        act.wait_ge(alo, prev.val(lambda c: c.n["alo"]))
                    if kind == "q":
                        act.wait_ge(blk, 2)
                    act.activation(out, src, ACT.Copy).then_inc(zlo, 1)
                if e == 1 and kind in ("ua", "uv"):
                    act.wait_ge(zsum, prev.val(lambda c: c.n["zsum"] + 1))
                    act.wait_ge(alo, prev.val(lambda c: c.n["alo"]))
                    act.wait_ge(gated, prev.val(lambda c: c.n["gated"]))
                    for j in range(TPC):
                        act.activation(y4[:, j, :], zpad[:, j, 2:T + 2], ACT.Identity, bias=conv_col(prev, None, j),
                                       scale=conv_col(prev, 2, j)).then_inc(tap2, 1)
                if e == 2 and kind == "ua":
                    act.wait_ge(conv, prev.val(lambda c: c.n["conv"] + 1))
                    act.wait_ge(prod, prev.val(lambda c: c.n["prod"]))
                    act.activation(gt, y, ACT.Silu).then_inc(gated, 1)
                if e == 1 and kind == "u":
                    act.wait_ge(zsum, prev.val(lambda c: c.n["zsum"] + 1))
                    act.activation(gt, y, ACT.Gelu_apprx_tanh).then_inc(gated, 1)
                if e == 3 and kind in ("uv", "u"):
                    act.wait_ge(prod, prev.val(lambda c: c.n["prod"] + 1))
                    act.activation(act_tiles(prev)[:, :, 0:T], y4, ACT.Copy).then_inc(ahi, 1)
                if e == 1 and kind == "cmp":
                    act.wait_ge(zsum, prev.val(lambda c: c.n["zsum"] + 1))
                    act.activation(cmp_g[:, :], cmp_g[:, :], ACT.Gelu_apprx_tanh).then_inc(cmp_gelu, 1)
                if e == 2 and kind == "cmp":
                    act.activation(squares[:, 4096:6144], scratch[:, 4096:6144], ACT.Square).then_inc(keys_squared, 1)
                done_q = 0 if kind == "cmp" else prev.first.loc if kind == "q" and prev.first.loc else None
                if e == 2 and done_q is not None:
                    act.wait_ge(zsum, prev.first.n["zsum"] + 1)
                    o = TPC * T * done_q
                    act.activation(squares[:, o:o + TPC * T], q_raw[:, o:o + TPC * T], ACT.Square) \
                        .then_inc(queries_squared, 1)
                v_chunks = [(prev.first.n["c"], g)] if kind == "v" else \
                    [(k, 2 * k) for k in range(4)] if kind == "vh" and prev.first.loc == QUARTERS - 1 else []
                if e == 0 and v_chunks:
                    done_wait(act, prev)
                    for k, bank in v_chunks:
                        for n in range(2):
                            last = act.activation(v_tiles(k, n),
                                                  banks[:, bank + n, :].rearrange("p (c t) -> p c t", t=P),
                                                  ACT.Gelu_apprx_tanh)
                        last.then_inc(vread, 1)
                if e == 2:
                    for k, _ in v_chunks:
                        act.wait_ge(vread, k + 1)
                        for n in range(2):
                            if k:
                                act.wait_ge(vsq, 2 * k + n - 1)
                            act.activation(temp[:, n, 0:COLS].rearrange("p (c t) -> p c t", t=P), v_tiles(k, n),
                                           ACT.Square, accum_out=vstat[:, k + 8 * n:k + 8 * n + 1]).then_inc(vsq, 1)
                if e == 0 and kind == "kvt":
                    done_wait(act, prev)
                    dst = v_slc if prev.first.loc == 3 else v_win
                    act.activation(dst.rearrange("p (n c) -> p n c", n=2), banks[:, g:g + 2, :], ACT.Copy) \
                        .then_inc(vread, 1)
                if e == 3 and name == "kv" and not first and cur.first.loc in (3, 4):
                    i = cur.first.loc - 3
                    act.wait_ge(blk, i + 1)
                    act.activation(blk_view(i)[:, :, 0:NB], blocks.rearrange("p (l n) -> p l n", l=CMP_LEN),
                                   ACT.Copy).then_inc(blk_hi, 1)
                if e == 3 and first and name == "sgu_u0":
                    act.wait_ge(vmean, 1)
                    act.activation(vstat[:, 18:20], vstat[:, 20:22], ACT.Sqrt).then_inc(vrstd, 1)
                if e == 3 and first and name == "wo":
                    attention_act(act)

            def step(name, cur, prev, first):
                u, e = 0, 0
                if first and name == "sgu_v":
                    act.dma_start(w_sT, io["w_s"].rearrange("p (g t) -> p g t", g=SGU_G)).then_inc(mix_loaded, 16)
                    act.dma_start(b_sb, io["b_s"].rearrange("p (g t) -> p g t", g=SGU_G)).then_inc(mix_loaded, 16)
                for tok, t in enumerate(cur.first.tokens):
                    if t == "s":
                        split_hi(cur, u, tok)
                        u += 1
                    elif t == "E":
                        if name == "head":
                            quarter = cur.first.loc
                            make_h(name, range(TPC * quarter, TPC * (quarter + 1)), first,
                                   READY_QUARTER * (quarter + 1))
                        for stage in stages_at(name, cur, first, e):
                            evacuate(stage, name, cur, prev, first)
                        if first and name in H_OF and name != "head":
                            make_h(name, h_tiles(e), H_OF[name][2] and e == 0, ready_after(H_OF[name][1]))
                        e += 1

            walk(act, phases, step)

        @block.vector
        def _(dve):
            dve.memset(zpad[:, :, :], 0.0).then_inc(zeroed, 1)
            dve.memset(pick[:, :], 0.0).then_inc(pick_zero, 1)
            dve.wait_ge(pick_zero, 1)
            dve.memset(pick[:, NH - 1:NH], 1.0)
            dve.memset(eps[:, :], EPS)
            dve.memset(ones[:, :], 1.0).then_inc(consts_set, 1)

            def split_lo(cur, u, tok):
                off, chunk = cur.first.piece_of[tok], cur.first
                slot = cur.static(lambda c: (c.n["G"] + off) % RAW_SLOTS)
                out = cur.static(lambda c: (c.n["S"] + u) % SPLIT_SLOTS)
                dve.wait_ge(hi_ready, cur.val(lambda c: c.n["S"] + u + 1))
                n = KT * NGATE if chunk.kind == "gate" else SUB
                half = (u % 2) * SUB
                dve.tensor_tensor(w_lo[:, out, 0:n], raw[:, slot, half:half + n], w_hi[:, out, 0:n].bitcast(F32),
                                  ALU.subtract).then_inc(stream, 2 if chunk.kind == "gate" else 1)

            def mod_piece(cur, m, tok):
                off = cur.first.piece_of[tok]
                slot = cur.static(lambda c: (c.n["G"] + off) % RAW_SLOTS)
                dve.wait_ge(raw_loaded[slot], cur.val(lambda c: 16 * ((c.n["G"] + off) // RAW_SLOTS + 1)))
                looped = cur.first.in_looped
                slice_, kt = mod_place(cur.first.n["M"] + m)
                column = KT * slice_ + kt
                out = mod_col[:, m:m + 1] if looped else mod_sums[:, column:column + 1]
                if looped and m == 0:
                    dve.wait_ge(mod_moved, cur.val(lambda c: c.n["moved"]))
                dve.wait_ge(c_ready, 1)
                dve.tensor_tensor_reduce(raw[:, slot, :], raw[:, slot, :], c_all[:, :], 1.0, 0.0, ALU.mult, ALU.add,
                                         out).then_inc(stream, 2)
                of_chunk = cur.first.kinds_of.count("m")
                if m == of_chunk - 1:
                    if looped:
                        dve.wait_ge(stream, cur.val(lambda c: 2 * (c.n["G"] + off + 1)))
                        first_column = cur.val(lambda c: c.n["M"])
                        dst = mod_sums[:, first_column:first_column + of_chunk] if isinstance(first_column, int) \
                            else mod_sums[:, bass.ds(first_column, of_chunk)]
                        dve.tensor_copy(dst, mod_col[:, 0:of_chunk]).then_inc(mod_moved, 1)

            def mod_vector(k, quarter=None):
                if quarter is None:
                    dve.wait_ge(stream, 2 * (MOD_END[k]["piece"] + 1))
                    if MOD_END[k]["moved"]:
                        dve.wait_ge(mod_moved, MOD_END[k]["moved"])
                    lo, n, ready = 0, KT, ready_after(k)
                else:
                    dve.wait_ge(stream, 2 * (BY_NAME["head"][quarter].n["G"] + (0 if quarter else 2 * TPC)))
                    lo, n, ready = TPC * quarter, TPC, READY_QUARTER * (quarter + 1)
                out = modv[:, k, lo:lo + n]
                dve.tensor_tensor(out, out, small[:, C_MODB + KT * k + lo:C_MODB + KT * k + lo + n], ALU.add) \
                    .then_inc(mod_ready, 1)
                if k in GAIN_OF:
                    g = C_GAIN + KT * GAIN_OF[k] + lo
                    dve.wait_ge(mod_ready, ready - 1)
                    dve.scalar_tensor_tensor(out=out, in0=out, scalar=1.0, in1=small[:, g:g + n], op0=ALU.add,
                                             op1=ALU.mult).then_inc(mod_ready, 1)

            def make_h(name, tiles, fresh, ready):
                i = h_index(name)
                shift, scale, _ = H_OF[name]
                if fresh:
                    k = STAT_ORDER.index(name)
                    dve.wait_ge(rms_ok, k + 1)
                    dve.reciprocal(rstd[:, :], rstd[:, :]).then_inc(rstd_ok, 1)
                    dve.wait_ge(rstd_ok, k + 1)
                dve.wait_ge(mod_ready, ready)
                if name == "q":
                    dve.wait_ge(blk_lo, 2)
                def norm(kt):
                    if kt >= 8:
                        dve.wait_ge(h_ready, KT * i + kt - 7)
                    elif i:
                        dve.wait_ge(h_ready, KT * i)
                    dve.scalar_tensor_tensor(out=temp8[:, kt % 8, :], in0=x[:, kt, :], scalar=vec(scale, kt),
                                             in1=rstd[:, :], op0=ALU.mult, op1=ALU.mult).then_inc(normed, 1)

                def low(kt):
                    dve.wait_ge(h_hi, KT * i + kt + 1)
                    dve.scalar_tensor_tensor(out=h_op[:, kt, T:HILO], in0=temp8[:, kt % 8, :],
                                             scalar=vec(shift, kt), in1=h_op[:, kt, 0:T].bitcast(F32),
                                             op0=ALU.add, op1=ALU.subtract).then_inc(h_ready, 1)

                for kt in list(tiles)[:2]:
                    norm(kt)
                for kt in tiles:
                    if kt + 2 <= tiles[-1]:
                        norm(kt + 2)
                    low(kt)

            def evacuate(e, name, cur, prev, first):
                kind = prev.first.kind
                g = group(prev)
                if e == 0 and name == "sgu_u0" and cur.first.loc == 1:
                    mix_tiles(dve, group(cur))
                if e == 0 and kind in ("ua", "uv", "u", "kvf", "q", "cmp", "gate"):
                    dve.wait_ge(zlo, prev.val(lambda c: c.n["zlo"] + 1))
                    if kind == "cmp":
                        out, src = cmp_g[:, :].rearrange("p (i n) -> p i n", i=2), banks[:, g:g + 2, 0:NB]
                    elif kind == "gate":
                        out, src = gates_t, banks[0:NGATE, g, 0:T]
                    else:
                        out, src = z_view(prev), banks[:, g:g + 4, 0:T]
                    dve.tensor_tensor(out, src, out, ALU.add).then_inc(zsum, 1)
                if e == 1 and kind in ("ua", "uv"):
                    dve.wait_ge(zeroed, 1)
                    for j in range(TPC):
                        dve.wait_ge(tap2, prev.val(lambda c: TPC * c.n["tap2"]) + j + 1)
                        dve.scalar_tensor_tensor(
                            out=y4[:, j, :], in0=zpad[:, j, 1:1 + T], scalar=conv_col(prev, 1, j),
                            in1=y4[:, j, :], op0=ALU.mult, op1=ALU.add).then_inc(tap1, 1)
                    for j in range(TPC):
                        dve.wait_ge(tap1, prev.val(lambda c: TPC * c.n["tap1"]) + j + 1)
                        last = dve.scalar_tensor_tensor(
                            out=y4[:, j, :], in0=zpad[:, j, 0:T], scalar=conv_col(prev, 0, j),
                            in1=y4[:, j, :], op0=ALU.mult, op1=ALU.add)
                    last.then_inc(conv, 1)
                whole = first and name in H_OF
                if kind == "dn" and (e == 0 or e == 1 and not whole):
                    gate, n = GATE_OF[PHASE_OF[id(prev.first)]], prev.first.n["xup"]
                    if e == 0:
                        dve.wait_ge(mod_ready, ready_after(gate))
                        if n:
                            dve.wait_ge(xlow, TPC * n)
                    for part, j in UPDATES["all" if whole else e]:
                        if part:
                            dve.wait_ge(xup, TPC * n + j + 1)
                        elif j < TPC - 1:
                            dve.wait_ge(tile_done, (TPC - 1) * n + j + 1)
                        else:
                            done_wait(dve, prev)
                        kt = TPC * prev.first.loc + j
                        dve.scalar_tensor_tensor(
                            out=x[:, kt, :], in0=banks[:, g + j, T * part:T * (part + 1)], scalar=vec(gate, kt),
                            in1=x[:, kt, :], op0=ALU.mult, op1=ALU.add).then_inc(xlow if part else xup, 1)
                if e == 3 and first and name == "sgu_u0":
                    mix_weights(dve)
                if e == 3 and first and name == "wo":
                    attention_dve(dve)

            def step(name, cur, prev, first):
                u = m = e = 0
                for tok, t in enumerate(cur.first.tokens):
                    if t == "s":
                        split_lo(cur, u, tok)
                        u += 1
                    elif t == "m":
                        mod_piece(cur, m, tok)
                        m += 1
                    else:
                        if first and e == 0:
                            for k in FINISHED.get(name, []):
                                mod_vector(k)
                        if name == "head":
                            if first:
                                dve.wait_ge(small_loaded, 16)
                            for k in (SH1_0, SC1_0):
                                mod_vector(k, cur.first.loc)
                            quarter = cur.first.loc
                            make_h(name, range(TPC * quarter, TPC * (quarter + 1)), first,
                                   READY_QUARTER * (quarter + 1))
                        for stage in stages_at(name, cur, first, e):
                            evacuate(stage, name, cur, prev, first)
                        if first and name in H_OF and name != "head":
                            make_h(name, h_tiles(e), H_OF[name][2] and e == 0, ready_after(H_OF[name][1]))
                        e += 1

            walk(dve, phases, step)
            if phases[-1][1][-1].kind == "dn":
                last_chunk = At(phases[-1][1][-1])
                for stage in range(2):
                    evacuate(stage, "end", last_chunk, last_chunk, False)

        @block.gpsimd
        def _(pool):
            pool.memset(ident[:, :], 0.0).then_inc(ident_zero, 1)
            pool.wait_ge(ident_zero, 1)
            pool.affine_select(out=ident[:, :], in_=ident[:, :], compare_op=ALU.not_equal, fill=1.0, base=0,
                               pattern=[[-1, P]], channel_multiplier=1).then_inc(ident_set, 1)

            def sum_squares(k, q):
                if q == 3:
                    return
                n = 3 * k + q
                if k == 0:
                    pool.wait_ge(x_loaded, 16)
                else:
                    name = STAT_ORDER[k]
                    pool.wait_ge(xlow, TPC * (BY_NAME[X_FROM[name]][q].n["xup"] + 1))
                tiles = x[:, TPC * q:TPC * (q + 1), :].rearrange("p k t -> p (k t)")
                if n:
                    pool.wait_ge(xhalf, n)
                pool.tensor_tensor(y, tiles, tiles, ALU.mult).then_inc(xsq, 1)
                pool.wait_ge(xsq, n + 1)
                if n:
                    pool.wait_ge(xsum, n)
                pool.tensor_tensor(gt[:, 512:1024], y[:, 0:512], y[:, 512:1024], ALU.add).then_inc(xhalf, 1)
                pool.wait_ge(xhalf, n + 1)
                pool.tensor_tensor(gt[:, 256:512], gt[:, 512:768], gt[:, 768:1024], ALU.add).then_inc(xquarter, 1)
                pool.wait_ge(xquarter, n + 1)
                if q == 0:
                    pool.tensor_copy(gt[:, 0:256], gt[:, 256:512]).then_inc(xsum, 1)
                else:
                    pool.tensor_tensor(gt[:, 0:256], gt[:, 0:256], gt[:, 256:512], ALU.add).then_inc(xsum, 1)

            for q in range(3):
                sum_squares(0, q)
            pool.wait_ge(mix_loaded, 32)
            pool.affine_select(out=w_sT, in_=w_sT, compare_op=ALU.is_ge, fill=0.0, base=0,
                               pattern=[[0, SGU_G], [1, P]], channel_multiplier=-1).then_inc(masked, 1)

            def step(name, cur, prev, first):
                kind = prev.first.kind if prev else None
                if kind in ("uv", "u"):
                    if kind == "uv":
                        pool.wait_ge(conv, prev.val(lambda c: c.n["conv"] + 1))
                        pool.wait_ge(gated, prev.val(lambda c: c.n["gated"]))
                        pool.tensor_tensor(y, y, gt, ALU.mult).then_inc(prod, 1)
                    else:
                        half = int(PHASE_OF[id(prev.first)][-1])
                        ct = 16 * half + TPC * prev.first.loc
                        pool.wait_ge(gated, prev.val(lambda c: c.n["gated"] + 1))
                        pool.wait_ge(sv_ready, ct + 4)
                        pool.tensor_tensor(y4, gt4, sv[:, ct:ct + 4, :], ALU.mult).then_inc(prod, 1)
                    pool.wait_ge(ahi, prev.val(lambda c: c.n["ahi"] + 1))
                    rows = act_tiles(prev)
                    pool.tensor_tensor(rows[:, :, T:HILO], y4, rows[:, :, 0:T].bitcast(F32), ALU.subtract) \
                        .then_inc(alo, 1)
                if kind == "dn":
                    for k in range(1, len(STAT_ORDER)):
                        if PHASE_OF[id(prev.first)] == X_FROM[STAT_ORDER[k]]:
                            sum_squares(k, prev.first.loc)
                if name == "kv" and not first and cur.first.loc in (3, 4):
                    i = cur.first.loc - 3
                    src = (kc0, vc0)[i]
                    pool.wait_ge(zsum, BY_NAME["kv"][i].n["zsum"] + 1)
                    if i:
                        pool.wait_ge(blk_lo, 1)
                    else:
                        pool.wait_ge(h_ready, KT * (h_index("kv") + 1))
                    for g in range(NKV):
                        token = src[:, g * T:(g + 1) * T].rearrange("p (n l) -> p l n", l=CMP_STRIDE)
                        for part in range(2):
                            c0 = C_POS + CMP_LEN * i + CMP_STRIDE * part
                            last = pool.tensor_tensor(
                                blocks.rearrange("p (l g n) -> p l g n", l=CMP_LEN, g=NKV)
                                [:, CMP_STRIDE * part:CMP_STRIDE * (part + 1), g, :],
                                token[:, :, part:part + NCMP],
                                small[:, c0:c0 + CMP_STRIDE].rearrange("p (l o) -> p l o", o=1)
                                .to_broadcast([P, CMP_STRIDE, NCMP]), ALU.add)
                    last.then_inc(blk, 1)
                    pool.wait_ge(blk_hi, i + 1)
                    pool.tensor_tensor(blk_view(i)[:, :, NB:2 * NB], blocks.rearrange("p (l n) -> p l n", l=CMP_LEN),
                                       blk_view(i)[:, :, 0:NB].bitcast(F32), ALU.subtract).then_inc(blk_lo, 1)
                if first and name == "wo":
                    attention_pool(pool)

            walk(pool, phases, step)

        @block.tensor
        def _(pe):
            def operand_wait(name, u):
                if name == "wo":
                    pe.wait_ge(out_lo, 4 * (u + 1))
                if name == "cmp" and u == 0:
                    pe.wait_ge(blk_lo, 2)
                if name in H_OF and name != "head":
                    pe.wait_ge(h_ready, KT * h_index(name) + 2 * (u + 1))
                if u % 2:
                    return
                need = u // 2 + 1
                if name.startswith("dn"):
                    v = [c for c in BY_NAME["up" + name[2:]] if c.kind == "uv"]
                    pe.wait_ge(alo, v[need - 1].n["alo"] + 1)
                elif name.startswith("sgu_o"):
                    pe.wait_ge(alo, BY_NAME["sgu_u" + name[-1]][need - 1].n["alo"] + 1)

            pe.wait_ge(consts_set, 1)
            pe.wait_ge(c_loaded, 16)
            for b in range(4):
                spread = pe.matmul(banks[:, 4 + b, :], ones[0:1, :], c_all[0:1, 512 * b:512 * (b + 1)], start=True,
                                   stop=True)
            spread.then_inc(c_spread, 1)

            def step(name, cur, prev, first):
                kind = cur.first.kind
                g = group(cur)
                if first and name == "wo":
                    attention_pe(pe)
                free_wait(pe, cur)
                if name == "sgu_u0" and cur.first.loc == 1:
                    mix_pe(g)
                if first and name in H_OF and H_OF[name][2]:
                    k = STAT_ORDER.index(name)
                    pe.wait_ge(consts_set, 1)
                    pe.wait_ge(xsum, 3 * (k + 1))
                    pe.matmul(banks[:, 0, 0:T], ones[:, :], gt[:, 0:T], start=True, stop=False)
                    for j in range(TPC):
                        pe.wait_ge(squared, TPC * k + j + 1)
                        last = pe.matmul(banks[:, 0, 0:T], ones[:, :], y[:, T * j:T * (j + 1)], start=False,
                                         stop=(j == TPC - 1))
                    last.then_inc(summed, 1)
                operand = h_op if name in ("head", "sgu_v", "sgu_u0", "sgu_u1", "kv", "q", "q1", "gate") or \
                    name.startswith("up") else act_op
                u = 0
                for tok, t in enumerate(cur.first.tokens):
                    if t != "s":
                        continue
                    off = cur.first.piece_of[tok]
                    slot = cur.static(lambda c: (c.n["S"] + u) % SPLIT_SLOTS)
                    pe.wait_ge(stream, cur.val(lambda c: 2 * (c.n["G"] + off) + u % 2 + 1))
                    if first:
                        operand_wait(name, u)
                    if kind in ("v", "kvt", "vh"):
                        pair, g = (u, g) if kind != "vh" else (2 * cur.first.loc + u % 2, 2 * (u // 2))
                        if kind == "vh" and u < 2:
                            pe.wait_ge(h_ready, 2 * (pair + 1))
                        hi = w_hi[:, slot, :].rearrange("p (k c) -> p k c", k=2)
                        lo = w_lo[:, slot, :].rearrange("p (k c) -> p k c", k=2)
                        for n in range(2):
                            for k in range(2):
                                kt = 2 * pair + k
                                a_hi, a_lo = (operand[:, kt, o + P * n:o + P * (n + 1)] for o in (0, T))
                                out = banks[:, g + n, :]
                                pe.matmul(out, a_hi, hi[:, k, :], start=(kt == 0), stop=False,
                                          skip_group_check=True)
                                pe.matmul(out, a_hi, lo[:, k, :], start=False, stop=False, skip_group_check=True)
                                last = pe.matmul(out, a_lo, hi[:, k, :], start=False, stop=(kt == KT - 1),
                                                 skip_group_check=True)
                    elif kind == "gate":
                        hi = w_hi[:, slot, 0:KT * NGATE].rearrange("p (k c) -> p k c", k=KT)
                        lo = w_lo[:, slot, 0:KT * NGATE].rearrange("p (k c) -> p k c", k=KT)
                        for kt in range(KT):
                            pe.matmul(banks[0:NGATE, g, :], hi[:, kt, :], operand[:, kt, :], start=(kt == 0),
                                      stop=False, skip_group_check=True)
                            last = pe.matmul(banks[0:NGATE, g, 0:T], lo[:, kt, :], operand[:, kt, 0:T],
                                             start=False, stop=(kt == KT - 1), skip_group_check=True)
                    elif kind == "cmp":
                        hi = w_hi[:, slot, :].rearrange("p (l c) -> p l c", l=8)
                        lo = w_lo[:, slot, :].rearrange("p (l c) -> p l c", l=8)
                        i = u // 4
                        for k in range(8):
                            row = 8 * (u % 4) + k
                            rows = blk_view(i)[:, row, :]
                            pe.matmul(banks[:, g + i, 0:2 * NB], hi[:, k, :], rows, start=(row == 0), stop=False,
                                      skip_group_check=True)
                            last = pe.matmul(banks[:, g + i, 0:NB], lo[:, k, :], rows[:, 0:NB], start=False,
                                             stop=(row == CMP_LEN - 1), skip_group_check=True)
                    else:
                        hi = w_hi[:, slot, :].rearrange("p (k c) -> p k c", k=2)
                        lo = w_lo[:, slot, :].rearrange("p (k c) -> p k c", k=2)
                        last_kt = 2 * cur.first.nsub - 1
                        for j in range(TPC):
                            for k in range(2):
                                kt = 2 * u + k
                                pe.matmul(banks[:, g + j, :], hi[:, k, P * j:P * (j + 1)], operand[:, kt, :],
                                          start=(kt == 0), stop=False, skip_group_check=True)
                                last = pe.matmul(banks[:, g + j, 0:T], lo[:, k, P * j:P * (j + 1)],
                                                 operand[:, kt, 0:T], start=False, stop=(kt == last_kt),
                                                 skip_group_check=True)
                            if kind == "dn" and u == cur.first.nsub - 1 and j < TPC - 1:
                                last.then_inc(tile_done, 1)
                    last.then_inc(sub_done, 1)
                    u += 1

            def mix_pe(g):
                pe.wait_ge(vread, 8)
                for ct in range(SGU_W // P):
                    if ct >= 4:
                        pe.wait_ge(sv_ready, ct - 3)
                    for n in range(2):
                        if ct == 0:
                            pe.wait_ge(wsn, n + 1)
                        last = pe.matmul(banks[:, g + ct % 4, P * n:P * (n + 1)], sv[:, ct, P * n:P * (n + 1)],
                                         w_sn[:, n, ct // 2, :], start=True, stop=True, skip_group_check=True)
                    last.then_inc(mixed, 1)
                pe.wait_ge(sv_ready, SGU_W // P)

            walk(pe, phases, step)


def stream_pieces(a):
    def cut(w):
        n = w.shape[1] // COLS
        k = w.shape[0] // (KPP * P)
        return w.reshape(k, KPP, P, n, COLS).transpose(3, 0, 2, 1, 4).reshape(n, k, P, PIECE)

    mod = {"mod0": a["mod_w"][0], "mod1": a["mod_w"][1], "kv": a["kv_mod_w"]}
    out = np.zeros((TOTAL["G"], P, PIECE), np.float32)
    cache = {}

    def weights(ch):
        s, i = ch.source, ch.loc
        if s not in cache:
            cache.clear()
            if s[0] == "sgu_v":
                cache[s] = cut(a["sgu_w_in"][0][:, SGU_W:])
            elif s[0] == "sgu_u":
                cache[s] = cut(a["sgu_w_in"][0][:, D * s[1]:D * (s[1] + 1)])
            elif s[0] == "sgu_out":
                cache[s] = cut(a["sgu_w_out"][0][D * s[1]:D * (s[1] + 1)])
            elif s[0] == "up":
                w = a["ffn_w_up"][s[1]]
                c0 = D * s[2]
                c1 = min(c0 + D, D_FF)
                both = [cut(w[:, c0:c1]), cut(w[:, D_FF + c0:D_FF + c1])]
                cache[s] = np.stack(both, 1)
            elif s[0] == "down":
                cache[s] = cut(a["ffn_w_down"][s[1]][D * s[2]:min(D * (s[2] + 1), D_FF)])
            elif s[0] == "kv":
                cache[s] = cut(a["w_kv"])
            elif s[0] == "q":
                cache[s] = cut(a["nsa_w_in"][0][:, :D])
            elif s[0] == "wo":
                cache[s] = cut(a["nsa_w_o"][0])
            elif s[0] == "cmp":
                cache[s] = a["cmp_w1"].reshape(2, 2, 16, P, HD).transpose(0, 1, 3, 2, 4).reshape(1, 4, P, PIECE)
            elif s[0] == "gate":
                g = a["nsa_w_in"][0][:, D:].reshape(KT, P, NGATE).transpose(1, 0, 2).reshape(P, KT * NGATE)
                cache[s] = np.zeros((1, 1, P, PIECE), np.float32)
                cache[s][0, 0, :, :KT * NGATE] = g
        w = cache[s]
        if ch.kind == "vh":
            return w[0:4, i]
        if ch.kind in ("ua", "uv"):
            return w[i, 0 if ch.kind == "ua" else 1]
        if ch.kind in ("kvf", "kvt"):
            return w[ch.loc]
        return w[i]

    for _, chunks in PHASES:
        for ch in chunks:
            g, m, q = ch.n["G"], ch.n["M"], 0
            w = weights(ch) if ch.source else None
            for kind in ch.kinds_of:
                if kind == "m":
                    slice_, kt = mod_place(m)
                    name, block = MODS[slice_]
                    o = D * block + P * kt
                    out[g] = mod[name][:, o:o + P].T
                    m += 1
                else:
                    out[g] = w[q]
                    q += 1
                g += 1
    return out.reshape(TOTAL["G"] * P, PIECE)


def small_table(a):
    def tall(v):
        return np.ascontiguousarray(v.reshape(-1, P).T)

    modb = {"mod0": a["mod_b"][0], "mod1": a["mod_b"][1], "kv": a["kv_mod_b"]}
    parts = [tall(modb[n][D * b:D * (b + 1)]) for n, b in MODS]
    parts += [tall(a["norm_gain"].reshape(4 * D)), tall(a["kv_gain"]), tall(a["sgu_v_gain"][0])]
    parts += [tall(a["ffn_conv_w"].reshape(-1)), tall(a["ffn_conv_b"].reshape(-1))]
    parts += [a["k_gain"].T, a["nsa_q_gain"].T]
    parts += [a["cmp_pos"].reshape(2 * CMP_LEN, HD).T]
    parts += [a["cmp_w2"][0], a["cmp_w2"][1]]
    out = np.ascontiguousarray(np.concatenate(parts, 1))
    assert out.shape == (P, N_SMALL), out.shape
    return out


def position_table():
    out = np.zeros((P, N_POS), np.float32)
    for qb in range(2):
        t = qb * P + np.arange(P)[:, None]
        d = t - (np.arange(NCMP) * CMP_STRIDE + CMP_LEN - 1)[None, :]
        out[:, DW * qb:DW * qb + NCMP] = np.where(d >= 0, d, BIG)
        d = t - np.arange(T)[None, :]
        out[:, DW * qb + 16:DW * (qb + 1)] = np.where(d >= 0, d, BIG)
        out[:, 2 * DW + qb] = t[:, 0] >= CMP_LEN - 1
    return out


def kernel(**inputs):
    import concourse.bacc as bacc
    from concourse.bass_utils import run_bass_kernel_spmd

    a = {k: np.asarray(v) for k, v in inputs.items()}
    arrays = {
        "in_stream": stream_pieces(a),
        "in_small": small_table(a),
        "in_c": np.ascontiguousarray(a["c"].reshape(1, D)),
        "in_x": np.ascontiguousarray(a["x"][0].T.reshape(KT, P, T).transpose(1, 0, 2).reshape(P, KT * T)),
        "in_w_s": np.ascontiguousarray(a["sgu_w_s"][0].transpose(2, 0, 1).reshape(P, SGU_G * P)),
        "in_b_s": np.ascontiguousarray(np.broadcast_to(a["sgu_b_s"][0].reshape(1, SGU_G * P), (P, SGU_G * P))),
        "in_pos": position_table(),
    }
    nc = bacc.Bacc("TRN2", target_bir_lowering=False, num_devices=1)
    io = {n[3:]: nc.dram_tensor(n, v.shape, F32, kind="ExternalInput").ap() for n, v in arrays.items()}
    io["out"] = nc.dram_tensor("out_x", (P, KT * T), F32, kind="ExternalOutput").ap()
    build(nc, io)
    r = run_bass_kernel_spmd(nc, [arrays], core_ids=[0])
    out = np.asarray(r.results[0]["out_x"])
    return np.ascontiguousarray(out.reshape(P, KT, T).transpose(2, 1, 0).reshape(1, T, D))
```
